# Optimizing a Trainium2 kernel written in Bass

```python
import math
import jax, jax.numpy as jnp
from jax import lax
import numpy as np

D_MODEL = 1024
BATCH = 1
SEQ = 1024
DEPTH = 1

MEM_LEN = 256

SB_HEADS = 8
SB_HEAD_DIM = D_MODEL // 16
SB_WIDTH = SB_HEADS * SB_HEAD_DIM
SB_BLOCK = 128

RET_HEADS = 4
RET_QK_DIM = D_MODEL // 8
RET_V_DIM = 2 * RET_QK_DIM
RET_QK_WIDTH = RET_HEADS * RET_QK_DIM
RET_V_WIDTH = RET_HEADS * RET_V_DIM
RET_CHUNK = 128
ROPE_BASE = 10000.0

N_BRANCHES = 2

OFF_SB_Q = 0
OFF_SB_K = OFF_SB_Q + SB_WIDTH
OFF_SB_V = OFF_SB_K + SB_WIDTH
OFF_RET_Q = OFF_SB_V + SB_WIDTH
OFF_RET_K = OFF_RET_Q + RET_QK_WIDTH
OFF_RET_V = OFF_RET_K + RET_QK_WIDTH
OFF_RET_G = OFF_RET_V + RET_V_WIDTH
OFF_GATE = OFF_RET_G + RET_V_WIDTH
IN_WIDTH = OFF_GATE + N_BRANCHES * D_MODEL

MEM_HEADS = 4
MEM_HEAD_DIM = D_MODEL // MEM_HEADS

FFN_HIDDEN = -(-8 * D_MODEL // (3 * 256)) * 256

DN_ALPHA = (2.0 * DEPTH) ** 0.25
DN_BETA = (8.0 * DEPTH) ** -0.25
LN_EPS = 1e-5

kernel_name = "hybrid_stickbreak_retention_deepnorm"

def layer_norm(x, g, b):
    xf = x.astype(jnp.float32)
    mu = jnp.mean(xf, -1, keepdims=True)
    var = jnp.mean(jnp.square(xf - mu), -1, keepdims=True)
    return ((xf - mu) * lax.rsqrt(var + LN_EPS)).astype(x.dtype) * g + b

def head_norm(x):
    xf = x.astype(jnp.float32)
    mu = jnp.mean(xf, -1, keepdims=True)
    var = jnp.mean(jnp.square(xf - mu), -1, keepdims=True)
    return (xf - mu) * lax.rsqrt(var + LN_EPS)

def rotary(x):
    S, d = x.shape[1], x.shape[-1]
    half = d // 2
    inv = 1.0 / (ROPE_BASE ** (jnp.arange(half, dtype=jnp.float32) / half))
    ang = jnp.arange(S, dtype=jnp.float32)[:, None] * inv[None, :]
    cos = jnp.cos(ang)[None, :, None, :]
    sin = jnp.sin(ang)[None, :, None, :]
    xf = x.astype(jnp.float32)
    x1, x2 = xf[..., :half], xf[..., half:]
    return jnp.concatenate([x1 * cos - x2 * sin, x1 * sin + x2 * cos], -1).astype(x.dtype)

def stick_breaking_attention(q, k, v):
    B, S, H, d = q.shape
    nb = S // SB_BLOCK
    qb = (q.astype(jnp.float32) * (d ** -0.5)).reshape(B, nb, SB_BLOCK, H, d).transpose(1, 0, 3, 2, 4)
    kf = k.astype(jnp.float32).transpose(0, 2, 1, 3)
    vf = v.astype(jnp.float32).transpose(0, 2, 1, 3)
    key_pos = jnp.arange(S)

    def one_block(args):
        q_blk, blk = args
        q_pos = blk * SB_BLOCK + jnp.arange(SB_BLOCK)
        mask = key_pos[None, :] < q_pos[:, None]
        z = jnp.einsum('bhqd,bhkd->bhqk', q_blk, kf)
        log_beta = jax.nn.log_sigmoid(z)
        log_rem = jnp.where(mask, jax.nn.log_sigmoid(-z), 0.0)
        later = lax.cumsum(log_rem, axis=3, reverse=True) - log_rem
        w = jnp.where(mask, jnp.exp(log_beta + later), 0.0)
        return jnp.einsum('bhqk,bhkd->bhqd', w, vf)

    out = lax.map(one_block, (qb, jnp.arange(nb)))
    return out.transpose(1, 0, 3, 2, 4).reshape(B, S, H * d)

def retention(q, k, v):
    B, S, H, dk = q.shape
    dv = v.shape[-1]
    nc = S // RET_CHUNK
    log_gamma = jnp.log1p(-jnp.exp2(-5.0 - jnp.arange(H, dtype=jnp.float32)))
    qc = (q.astype(jnp.float32) * (dk ** -0.5)).reshape(B, nc, RET_CHUNK, H, dk)
    kc = k.astype(jnp.float32).reshape(B, nc, RET_CHUNK, H, dk)
    vc = v.astype(jnp.float32).reshape(B, nc, RET_CHUNK, H, dv)
    idx = jnp.arange(RET_CHUNK, dtype=jnp.float32)
    rel = idx[:, None] - idx[None, :]
    decay = jnp.where(rel[None] >= 0,
                      jnp.exp(log_gamma[:, None, None] * jnp.maximum(rel, 0.0)[None]), 0.0)
    scores = jnp.einsum('bnihd,bnjhd->bnhij', qc, kc) * decay
    inner = jnp.einsum('bnhij,bnjhe->bnihe', scores, vc)
    k_decay = jnp.exp(log_gamma[None, :] * (RET_CHUNK - 1.0 - idx)[:, None])
    chunk_kv = jnp.einsum('bnjhd,jh,bnjhe->nbhde', kc, k_decay, vc)
    chunk_decay = jnp.exp(log_gamma * RET_CHUNK)[None, :, None, None]

    def step(state, kv):
        return state * chunk_decay + kv, state

    _, states = lax.scan(step, jnp.zeros((B, H, dk, dv), jnp.float32), chunk_kv)
    q_decay = jnp.exp(log_gamma[None, :] * (idx + 1.0)[:, None])
    cross = jnp.einsum('bnihd,ih,nbhde->bnihe', qc, q_decay, states)
    return (inner + cross).reshape(B, S, H, dv)

def memory_cross_attention(x, mem, w_q, w_kv, w_o):
    B, S, _ = x.shape
    q = (x @ w_q).reshape(B, S, MEM_HEADS, MEM_HEAD_DIM)
    kv = (mem @ w_kv).reshape(B, MEM_LEN, 2, MEM_HEADS, MEM_HEAD_DIM)
    k, v = kv[:, :, 0], kv[:, :, 1]
    s = jnp.einsum('bshd,bmhd->bhsm', q.astype(jnp.float32), k.astype(jnp.float32)) * (MEM_HEAD_DIM ** -0.5)
    p = jax.nn.softmax(s, axis=-1)
    o = jnp.einsum('bhsm,bmhd->bshd', p, v.astype(jnp.float32)).reshape(B, S, D_MODEL)
    return o.astype(x.dtype) @ w_o

def setup_inputs(seed: int = 0) -> dict:
    key = jax.random.key(seed)
    ks = jax.random.split(key, 24)
    nrm = lambda k, shape: jax.random.normal(k, shape, jnp.float32)

    def dense(k, fan_in, fan_out, scale=1.0):
        return nrm(k, (DEPTH, fan_in, fan_out)) * (fan_in ** -0.5) * scale

    gain = lambda k: 1.0 + 0.02 * nrm(k, (DEPTH, D_MODEL))
    bias = lambda k, n: 0.02 * nrm(k, (DEPTH, n))

    col_scale = jnp.concatenate([
        jnp.ones((OFF_SB_V,), jnp.float32),
        jnp.full((SB_WIDTH,), DN_BETA, jnp.float32),
        jnp.ones((2 * RET_QK_WIDTH,), jnp.float32),
        jnp.full((RET_V_WIDTH,), DN_BETA, jnp.float32),
        jnp.ones((RET_V_WIDTH + N_BRANCHES * D_MODEL,), jnp.float32)])
    mem_kv_scale = jnp.concatenate([jnp.ones((D_MODEL,), jnp.float32),
                                    jnp.full((D_MODEL,), DN_BETA, jnp.float32)])
    return {
        "x": nrm(ks[0], (BATCH, SEQ, D_MODEL)),
        "mem": nrm(ks[1], (BATCH, MEM_LEN, D_MODEL)),
        "w_in": dense(ks[2], D_MODEL, IN_WIDTH) * col_scale,
        "b_gate": bias(ks[3], N_BRANCHES * D_MODEL),
        "w_sb_o": dense(ks[4], SB_WIDTH, D_MODEL),
        "w_ret_o": dense(ks[5], RET_V_WIDTH, D_MODEL),
        "w_mix_o": dense(ks[6], D_MODEL, D_MODEL, DN_BETA),
        "ln1_g": gain(ks[7]),
        "ln1_b": bias(ks[8], D_MODEL),
        "w_mem_q": dense(ks[9], D_MODEL, D_MODEL),
        "w_mem_kv": dense(ks[10], D_MODEL, 2 * D_MODEL) * mem_kv_scale,
        "w_mem_o": dense(ks[11], D_MODEL, D_MODEL, DN_BETA),
        "ln2_g": gain(ks[12]),
        "ln2_b": bias(ks[13], D_MODEL),
        "w_ffn_in": dense(ks[14], D_MODEL, 2 * FFN_HIDDEN, DN_BETA),
        "w_ffn_out": dense(ks[15], FFN_HIDDEN, D_MODEL, DN_BETA),
        "ln3_g": gain(ks[16]),
        "ln3_b": bias(ks[17], D_MODEL),
    }

def reference(x, mem, w_in, b_gate, w_sb_o, w_ret_o, w_mix_o, ln1_g, ln1_b,
              w_mem_q, w_mem_kv, w_mem_o, ln2_g, ln2_b, w_ffn_in, w_ffn_out, ln3_g, ln3_b):
    B, S, _ = x.shape
    for l in range(DEPTH):
        h = x @ w_in[l]
        sb_q = h[..., OFF_SB_Q:OFF_SB_K].reshape(B, S, SB_HEADS, SB_HEAD_DIM)
        sb_k = h[..., OFF_SB_K:OFF_SB_V].reshape(B, S, SB_HEADS, SB_HEAD_DIM)
        sb_v = h[..., OFF_SB_V:OFF_RET_Q].reshape(B, S, SB_HEADS, SB_HEAD_DIM)
        r_q = rotary(h[..., OFF_RET_Q:OFF_RET_K].reshape(B, S, RET_HEADS, RET_QK_DIM))
        r_k = rotary(h[..., OFF_RET_K:OFF_RET_V].reshape(B, S, RET_HEADS, RET_QK_DIM))
        r_v = h[..., OFF_RET_V:OFF_RET_G].reshape(B, S, RET_HEADS, RET_V_DIM)
        r_g = h[..., OFF_RET_G:OFF_GATE]
        gates = jax.nn.sigmoid(h[..., OFF_GATE:] + b_gate[l]).reshape(B, S, N_BRANCHES, D_MODEL)

        y_sb = stick_breaking_attention(sb_q, sb_k, sb_v).astype(x.dtype) @ w_sb_o[l]
        ret = head_norm(retention(r_q, r_k, r_v)).reshape(B, S, RET_V_WIDTH)
        y_ret = (jax.nn.silu(r_g) * ret.astype(x.dtype)) @ w_ret_o[l]
        mix = (gates[:, :, 0] * y_sb + gates[:, :, 1] * y_ret) @ w_mix_o[l]
        x = layer_norm(DN_ALPHA * x + mix, ln1_g[l], ln1_b[l])

        xa = memory_cross_attention(x, mem, w_mem_q[l], w_mem_kv[l], w_mem_o[l])
        x = layer_norm(DN_ALPHA * x + xa, ln2_g[l], ln2_b[l])

        f = x @ w_ffn_in[l]
        ff = (jax.nn.silu(f[..., :FFN_HIDDEN]) * f[..., FFN_HIDDEN:]) @ w_ffn_out[l]
        x = layer_norm(DN_ALPHA * x + ff, ln3_g[l], ln3_b[l])
    return x


_drawn_inputs = setup_inputs


def setup_inputs(seed=0):
    import zlib

    import numpy as np

    out = dict(_drawn_inputs(seed))
    spreads = {}
    factors = {'b_gate': 38.346,
     'ln1_g': 7.769,
     'ln1_b': 8.092,
     'ln2_g': 7.929,
     'ln2_b': 7.542,
     'ln3_g': 8.162,
     'ln3_b': 8.212}
    for name, (base, spread) in spreads.items():
        noise = np.random.default_rng([zlib.crc32(name.encode()), seed]).standard_normal(out[name].shape)
        drawn = base * np.exp(spread * noise) if base else spread * noise
        out[name] = __import__('jax').numpy.asarray(drawn.astype(out[name].dtype))
    for name, factor in factors.items():
        out[name] = (out[name] * factor).astype(out[name].dtype)
    return out
```

```python
from contextlib import ExitStack

import numpy as np

import concourse.bass as bass
from concourse import mybir

ALU = mybir.AluOpType
ACT = mybir.ActivationFunctionType
F32 = mybir.dt.float32
F32R = mybir.dt.float32r
AX_X = mybir.AxisListType.X

P = 128
D = 1024
SEQ = 1024
HALF = 512
KT = D // P
MEM = 256
SB_HEADS, SB_DIM = 8, 64
SB_PAIRS = SB_HEADS // 2
SB_WIDTH = SB_HEADS * SB_DIM
RET_HEADS, RET_QK, RET_V = 4, 128, 256
RET_WIDTH = RET_HEADS * RET_V
MEM_HEADS, MEM_DIM = 4, 256
FFN = 2816
FFN_TILES = FFN // P
FFN_PARTS = (8, 7, 7)
ALPHA = 2.0 ** 0.25
EPS = 1e-5
QT = SEQ // P
MASKED = -1e30

BLK_SB_Q, BLK_SB_K, BLK_SB_V = 0, 4, 8
BLK_RET_Q, BLK_RET_K, BLK_RET_V, BLK_RET_G = 12, 16, 20, 28
BLK_GATE_SB, BLK_GATE_RET = 36, 44

CH_RET, CH_GRET, CH_SB, CH_GSB, CH_MIX, CH_MEM, CH_MO, CH_FFN = 0, 24, 40, 52, 64, 72, 96, 104
U_RET, U_GRET, U_SB, U_GSB, U_MIX, U_MEM, U_MO, U_FFN = 0, 40, 56, 136, 152, 160, 184, 192
RU, SU, GU, XU = 10, 20, 8, 6


def f32(ap):
    return ap.bitcast(F32)


def layer_program(nc, xT, memT, stream8, stream7, params, rope, consts, outT):
    ctx = ExitStack()
    with ctx:
        def sem(name):
            return ctx.enter_context(nc.semaphore(name))

        def sb(stack, name, shape, dt=F32):
            return stack.enter_context(nc.sbuf_tensor(name, shape, dt))

        x_hi = sb(ctx, "x_hi", [P, KT, SEQ], F32R)
        x_lo = sb(ctx, "x_lo", [P, KT, SEQ], F32R)
        acc = sb(ctx, "acc", [P, KT, SEQ])
        w_raw = sb(ctx, "w_raw", [P, 2, D])
        w_hi = [sb(ctx, f"w_hi{s}", [P, D], F32R) for s in range(2)]
        w_lo = [sb(ctx, f"w_lo{s}", [P, D], F32R) for s in range(2)]
        par = sb(ctx, "par", [P, 64])
        one = sb(ctx, "one", [P, 1])
        ident = sb(ctx, "ident", [P, P])
        causal = sb(ctx, "causal", [P, P])
        ln_ones = sb(ctx, "ln_ones", [P, P], F32R)

        with ExitStack() as st:
            rq_hi, rq_lo = sb(st, "rq_hi", [P, SEQ], F32R), sb(st, "rq_lo", [P, SEQ], F32R)
            rk_hi, rk_lo = sb(st, "rk_hi", [P, SEQ], F32R), sb(st, "rk_lo", [P, SEQ], F32R)
            rv_hi, rv_lo = sb(st, "rv_hi", [P, QT, RET_V], F32R), sb(st, "rv_lo", [P, QT, RET_V], F32R)
            tmp_a, tmp_b = sb(st, "tmp_a", [P, SEQ]), sb(st, "tmp_b", [P, SEQ])
            rope_sb = sb(st, "rope_sb", [P, 2, SEQ])
            rp_hi, rp_lo = sb(st, "rp_hi", [P, 2, HALF], F32R), sb(st, "rp_lo", [P, 2, HALF], F32R)
            ro_hi, ro_lo = sb(st, "ro_hi", [P, 2, HALF], F32R), sb(st, "ro_lo", [P, 2, HALF], F32R)
            rs_hi, rs_lo = sb(st, "rs_hi", [P, 2, HALF], F32R), sb(st, "rs_lo", [P, 2, HALF], F32R)
            r_mean2, r_rstd = sb(st, "r_mean2", [P, HALF]), sb(st, "r_rstd", [P, HALF])
            silu_g = sb(st, "silu_g", [P, 2, SEQ])
            diag = sb(st, "diag", [P, P])
            ret_ones = sb(st, "ret_ones", [P, P], F32R)
        with ExitStack() as st:
            ret_hi, ret_lo = sb(st, "ret_hi", [P, KT, SEQ], F32R), sb(st, "ret_lo", [P, KT, SEQ], F32R)
            gate_ret = sb(st, "gate_ret", [P, SEQ])
        with ExitStack() as st:
            sb_out = sb(st, "sb_out", [P, 4, SEQ])
            with ExitStack() as s2:
                sq_hi, sq_lo = sb(s2, "sq_hi", [P, SEQ], F32R), sb(s2, "sq_lo", [P, SEQ], F32R)
                sk_hi, sk_lo = sb(s2, "sk_hi", [P, SEQ], F32R), sb(s2, "sk_lo", [P, SEQ], F32R)
                sv_hi, sv_lo = sb(s2, "sv_hi", [P, QT, P], F32R), sb(s2, "sv_lo", [P, QT, P], F32R)
                sv_T = sb(s2, "sv_T", [P, SEQ])
                beta = sb(s2, "beta", [P, 2, SEQ])
                remain = sb(s2, "remain", [P, SEQ])
                stick = sb(s2, "stick", [P, SEQ + 1])
                wT_hi, wT_lo = sb(s2, "wT_hi", [P, 2, SEQ], F32R), sb(s2, "wT_lo", [P, 2, SEQ], F32R)
                ident_r = sb(s2, "ident_r", [P, P], F32R)
                neg_r = sb(s2, "neg_r", [P, P], F32R)
                neg = sb(s2, "neg", [P, P])
            with ExitStack() as s2:
                sbo_hi, sbo_lo = sb(s2, "sbo_hi", [P, 4, SEQ], F32R), sb(s2, "sbo_lo", [P, 4, SEQ], F32R)
                gate_sb = sb(s2, "gate_sb", [P, 2, SEQ])
        with ExitStack() as st:
            a_hi, a_lo = sb(st, "a_hi", [P, KT, SEQ], F32R), sb(st, "a_lo", [P, KT, SEQ], F32R)
            with ExitStack() as s2:
                st_hi, st_lo = sb(s2, "st_hi", [P, HALF], F32R), sb(s2, "st_lo", [P, HALF], F32R)
                sqr = sb(s2, "sqr", [P, HALF])
                sqr_hi, sqr_lo = sb(s2, "sqr_hi", [P, HALF], F32R), sb(s2, "sqr_lo", [P, HALF], F32R)
                silu_h = sb(s2, "silu_h", [P, SEQ])
                hidden = sb(s2, "hidden", [P, SEQ])
        with ExitStack() as st:
            mem_raw = sb(st, "mem_raw", [P, KT, MEM])
            mem_hi, mem_lo = sb(st, "mem_hi", [P, KT, MEM], F32R), sb(st, "mem_lo", [P, KT, MEM], F32R)
            y_out = None
            with ExitStack() as s2:
                ln_mean2, ln_rstd = sb(s2, "ln_mean2", [P, SEQ]), sb(s2, "ln_rstd", [P, SEQ])
                ln_t = sb(s2, "ln_t", [P, 2, SEQ])
                ln_x = sb(s2, "ln_x", [P, 2, SEQ])
                y_out = sb(s2, "y_out", [P, KT, SEQ])
            with ExitStack() as s2:
                mk_hi, mk_lo = sb(s2, "mk_hi", [P, 2, MEM], F32R), sb(s2, "mk_lo", [P, 2, MEM], F32R)
                mv_T = sb(s2, "mv_T", [P, 2, MEM])
                mv_hi, mv_lo = sb(s2, "mv_hi", [P, 2, MEM_DIM], F32R), sb(s2, "mv_lo", [P, 2, MEM_DIM], F32R)
                mq_hi, mq_lo = sb(s2, "mq_hi", [P, 2, SEQ], F32R), sb(s2, "mq_lo", [P, 2, SEQ], F32R)
                prob = sb(s2, "prob", [P, 4, MEM])
                pT_hi, pT_lo = sb(s2, "pT_hi", [P, 2, HALF], F32R), sb(s2, "pT_lo", [P, 2, HALF], F32R)
                neg_max, row_sum, inv_sum = (sb(s2, n, [P, 4]) for n in ("neg_max", "row_sum", "inv_sum"))

        unit = ctx.enter_context(nc.psum_tensor("unit", [P, 2, SEQ], F32))
        aux = ctx.enter_context(nc.psum_tensor("aux", [P, 4, HALF], F32))

        w_loaded = [sem(f"w_loaded{s}") for s in range(2)]
        w_hi_done, w_split, chunk_started = sem("w_hi_done"), sem("w_split"), sem("chunk_started")
        one_ready = sem("one_ready")
        consts_loaded, consts_ready = sem("consts_loaded"), sem("consts_ready")
        x_loaded = [sem(f"x_loaded{j}") for j in range(4)]
        x_hi_done, x_split = sem("x_hi_done"), sem("x_split")
        unit_ready = sem("unit_ready")
        unit_drained = [sem(f"unit_drained{s}") for s in range(2)]

        rope_loaded, rope_products, rotated, rot_hi, rot_split = (
            sem(n) for n in ("rope_loaded", "rope_products", "rotated", "rot_hi", "rot_split"))
        rv_hi_done = sem("rv_hi_done")
        rz_ready, rp_hi_done, diag_masked, diag_hi, diag_lo, rp_split = (
            sem(n) for n in ("rz_ready", "rp_hi_done", "diag_masked", "diag_hi", "diag_lo", "rp_split"))
        ro_copied, rs_hi_done, rs_split, norm_ready = (
            sem(n) for n in ("ro_copied", "rs_hi_done", "rs_split", "norm_ready"))
        r_mean_sq, r_var, r_std, r_rstd_ready, ret_centered, ret_whole, ret_normed, ret_gated = (
            sem(n) for n in ("r_mean_sq", "r_var", "r_std", "r_rstd_ready", "ret_centered", "ret_whole",
                             "ret_normed", "ret_gated"))
        ret_hi_done, ret_split = sem("ret_hi_done"), sem("ret_split")

        stick_consts, neg_loaded, beta_ready = sem("stick_consts"), sem("neg_loaded"), sem("beta_ready")
        sqkv_hi, stick_scanned, w_ready, wt_ready, wt_hi, wt_split, sbo_ready, sbo_stored = (
            sem(n) for n in ("sqkv_hi", "stick_scanned", "w_ready", "wt_ready", "wt_hi", "wt_split",
                             "sbo_ready", "sbo_stored"))
        sbo_hi_done, sbo_split, branch_summed = sem("sbo_hi_done"), sem("sbo_split"), sem("branch_summed")

        mem_loaded, mem_hi_done, mem_split = sem("mem_loaded"), sem("mem_hi_done"), sem("mem_split")
        mkq_hi, s_ready, max_ready, neg_ready, exp_done, inv_ready, prob_ready = (
            sem(n) for n in ("mkq_hi", "s_ready", "max_ready", "neg_ready", "exp_done", "inv_ready", "prob_ready"))
        turn_ready, turn_hi, turn_split = sem("turn_ready"), sem("turn_hi"), sem("turn_split")

        silu_read, hid_hi, hid_lo = sem("silu_read"), sem("hid_hi"), sem("hid_lo")
        y_ready, out_stored = sem("y_ready"), sem("out_stored")

        class Norm:

            def __init__(self, tag):
                (self.a_hi, self.a_split, self.summed, self.stat_hi, self.stat_sq, self.sqr_hi, self.stat_split, self.sums_taken,
                 self.mean_sq, self.var, self.std, self.rstd, self.centered, self.scaled, self.affine, self.hi,
                 self.done) = (sem(f"{tag}_{n}") for n in (
                     "a_hi", "a_split", "summed", "stat_hi", "stat_sq", "sqr_hi", "stat_split", "sums_taken", "mean_sq", "var",
                     "std", "rstd", "centered", "scaled", "affine", "hi", "done"))

        n1, n2, n3 = Norm("n1"), Norm("n2"), Norm("n3")

        block = ctx.enter_context(nc.Block())

        @block.sync
        def _(sp):
            sp.dma_start(ident[:], consts[0]).then_inc(consts_loaded, 16)
            sp.dma_start(causal[:], consts[1]).then_inc(consts_loaded, 16)
            sp.dma_start(par[:], params).then_inc(consts_loaded, 16)

            def stream(source, first, chunk, count, width):
                with sp.Fori(0, count // 2) as i:
                    for s in range(2):
                        sp.wait_ge(w_split, i * 2 + (chunk + s - 1))
                        sp.dma_start(w_raw[:, s, 0:width],
                                     source[bass.ds(i * 2 + (first + s), 1)].rearrange("a p w -> p (a w)")
                                     ).then_inc(w_loaded[s], 16)

            for s in range(2):
                sp.dma_start(w_raw[:, s, :], stream8[s]).then_inc(w_loaded[s], 16)
            stream(stream8, 2, 2, 140, 8 * P)
            stream(stream7, 0, 142, 8, 7 * P)
            stream(stream8, 142, 150, 14, 8 * P)
            stream(stream7, 8, 164, 8, 7 * P)
            for k in range(KT):
                sp.wait_ge(y_ready, k + 1)
                sp.dma_start(outT[k * P:(k + 1) * P, :], y_out[:, k, :]).then_inc(out_stored, 16)
            sp.wait_ge(out_stored, 16 * KT)

        @block.gpsimd
        def _(pool):
            def split(chunk, count, width):
                with pool.Fori(0, count // 2) as i:
                    for s in range(2):
                        c = i * 2 + (chunk + s)
                        pool.wait_ge(w_loaded[s], i * 16 + (chunk // 2 + 1) * 16)
                        pool.wait_ge(chunk_started, c)
                        pool.tensor_tensor(w_hi[s][:, 0:width], w_raw[:, s, 0:width], one[:].to_broadcast([P, width]),
                                           ALU.mult).then_inc(w_hi_done, 1)
                        pool.wait_ge(w_hi_done, c + 1)
                        pool.tensor_tensor(w_lo[s][:, 0:width], w_raw[:, s, 0:width], f32(w_hi[s][:, 0:width]),
                                           ALU.subtract).then_inc(w_split, 1)

            pool.memset(one[:], 1.0).then_inc(one_ready, 1)
            pool.wait_ge(one_ready, 1)
            for s in range(2):
                pool.wait_ge(w_loaded[s], 16)
                pool.tensor_tensor(w_hi[s][:], w_raw[:, s, :], one[:].to_broadcast([P, D]), ALU.mult
                                   ).then_inc(w_hi_done, 1)
                pool.wait_ge(w_hi_done, s + 1)
                pool.tensor_tensor(w_lo[s][:], w_raw[:, s, :], f32(w_hi[s][:]), ALU.subtract).then_inc(w_split, 1)
            split(2, 140, 8 * P)
            split(142, 8, 7 * P)
            split(150, 14, 8 * P)
            split(164, 8, 7 * P)

        @block.tensor
        def _(pe):
            def triple(out, l_hi, l_lo, r_hi, r_lo, start, stop):
                pe.matmul(out, l_hi, r_lo, start=start, stop=False, skip_group_check=True)
                pe.matmul(out, l_hi, r_hi, start=False, stop=False, skip_group_check=True)
                return pe.matmul(out, l_lo, r_hi, start=False, stop=stop, skip_group_check=True)

            def free_unit(first, per, i, k):
                pe.wait_ge(unit_drained[k % 2], i * (per // 2) + (first // 2 + k // 2))
                return unit[:, k % 2, :]

            def project(chunk, s, outs, hi, lo, kts=KT, w0=0, arrived=None, mid=None):
                pe.wait_ge(w_split, chunk + 1)
                last = None
                for k in range(kts):
                    if arrived:
                        pe.wait_ge(arrived, k + 1)
                    if mid and k == kts // 2:
                        mid()
                    wk = slice((w0 + k) * P, (w0 + k + 1) * P)
                    for j, (out, cols) in enumerate(outs):
                        first = k == 0
                        x = pe.matmul(out, w_hi[s][:, wk], lo[:, k, cols], start=first, stop=False,
                                      skip_group_check=True)
                        if k == 0 and j == 0 and w0 == 0:
                            x.then_inc(chunk_started, 1)
                        pe.matmul(out, w_hi[s][:, wk], hi[:, k, cols], start=False, stop=False,
                                  skip_group_check=True)
                        last = pe.matmul(out, w_lo[s][:, wk], hi[:, k, cols], start=False, stop=(k == kts - 1),
                                         skip_group_check=True)
                return last

            def halves(u):
                return [(u[:, h * HALF:(h + 1) * HALF], slice(h * HALF, (h + 1) * HALF)) for h in range(2)]

            with pe.Fori(0, RET_HEADS) as h:
                def proj(k, c, arrived=None):
                    u = free_unit(U_RET, RU, h, k)
                    project(h * 6 + c, c % 2, halves(u), x_hi, x_lo, arrived=arrived).then_inc(unit_ready, 1)

                def turn_v(k, source):
                    u = free_unit(U_RET, RU, h, k)
                    for b in range(QT):
                        t = pe.transpose(u[:, b * P:(b + 1) * P], source[:, b * P:(b + 1) * P], ident[:])
                    t.then_inc(unit_ready, 1)

                pe.wait_ge(consts_ready, 2)
                proj(0, 0, x_split)
                proj(1, 1)
                proj(2, 2)
                proj(3, 3)
                pe.wait_ge(unit_drained[0], h * 5 + 2)
                turn_v(4, tmp_a)
                proj(5, 4)
                pe.wait_ge(unit_drained[1], h * 5 + 2)
                turn_v(6, tmp_b)

                def score(t):
                    hf, kb, q0, n = ret_tile(t)
                    z = aux[:, t % 2, 0:n]
                    triple(z, rk_hi[:, kb * P:(kb + 1) * P], rk_lo[:, kb * P:(kb + 1) * P],
                           rq_hi[:, q0:q0 + n], rq_lo[:, q0:q0 + n], True, True).then_inc(rz_ready, 1)

                def values(t):
                    hf, kb, q0, n = ret_tile(t)
                    u = unit[:, (7 + hf) % 2, :]
                    if kb == 0:
                        free_unit(U_RET, RU, h, 7 + hf)
                    pe.wait_ge(rp_split, h * 12 + (t + 1))
                    last_kb = 3 if hf == 0 else 7
                    for e in range(2):
                        c0 = e * HALF + q0 - hf * HALF
                        x = triple(u[:, c0:c0 + n], rv_hi[:, kb, e * P:(e + 1) * P], rv_lo[:, kb, e * P:(e + 1) * P],
                                   rp_hi[:, t % 2, 0:n], rp_lo[:, t % 2, 0:n], kb == 0, kb == last_kb)
                    if kb == last_kb:
                        x.then_inc(unit_ready, 1)

                def norm_sums(hf):
                    pe.wait_ge(rs_split, h * 2 + (hf + 1))
                    pe.wait_ge(ret_centered, h * 2 + hf)
                    for b, (hi, lo) in enumerate(((ro_hi, ro_lo), (rs_hi, rs_lo))):
                        for e in range(2):
                            pe.matmul(aux[:, 2 + b, :], ret_ones[:], lo[:, e, :], start=(e == 0), stop=False,
                                      skip_group_check=True)
                            x = pe.matmul(aux[:, 2 + b, :], ret_ones[:], hi[:, e, :], start=False, stop=(e == 1),
                                          skip_group_check=True)
                    x.then_inc(norm_ready, 1)

                pe.wait_ge(unit_drained[0], h * 5 + 4)
                pe.wait_ge(rot_split, h * 2 + 2)
                score(0)
                for t in range(1, 12):
                    score(t)
                    values(t - 1)
                values(11)
                norm_sums(0)
                proj(9, 5)
                norm_sums(1)

            with pe.Fori(0, KT) as n:
                u = free_unit(U_GRET, 2, n, 0)
                project(n * 2 + CH_GRET, 0, halves(u), x_hi, x_lo).then_inc(unit_ready, 1)
                u = free_unit(U_GRET, 2, n, 1)
                project(n * 2 + (CH_GRET + 1), 1, halves(u), ret_hi, ret_lo, arrived=ret_split).then_inc(unit_ready, 1)

            pe.wait_ge(stick_consts, 4)
            with pe.Fori(0, SB_PAIRS // 2) as i:
                for pp in range(2):
                    def sbu(k):
                        return free_unit(U_SB + SU * pp, 2 * SU, i, k)

                    def drained(k):
                        pe.wait_ge(unit_drained[k % 2], i * SU + (U_SB + SU * pp) // 2 + (k // 2 + 1))

                    def count(per_pair, k):
                        return i * (2 * per_pair) + (per_pair * pp + k)

                    for k in range(3):
                        c = 3 * pp + k
                        u = sbu(k)
                        project(i * 6 + (CH_SB + c), c % 2, halves(u), x_hi, x_lo).then_inc(unit_ready, 1)
                    drained(1)
                    u = sbu(3)
                    for b in range(QT):
                        t = pe.transpose(u[:, b * P:(b + 1) * P], sv_T[:, b * P:(b + 1) * P], ident[:])
                    t.then_inc(unit_ready, 1)
                    drained(0)
                    drained(2)

                    def logits(s):
                        qt, hd, n = stick_step(s)
                        rows = slice(hd * SB_DIM, (hd + 1) * SB_DIM)
                        q = slice(qt * P, (qt + 1) * P)
                        u = sbu(4 + s)
                        for c0 in range(0, n, HALF):
                            c1 = min(n, c0 + HALF)
                            x = triple(u[:, c0:c1], sq_hi[rows, q], sq_lo[rows, q], sk_hi[rows, c0:c1],
                                       sk_lo[rows, c0:c1], True, False)
                        pe.matmul(u[:, n - P:n], ident_r[:], neg_r[:], start=False, stop=True,
                                  skip_group_check=True).then_inc(unit_ready, 1)

                    def turn_w(s):
                        qt, hd, n = stick_step(s)
                        pe.wait_ge(w_ready, count(16, s + 1))
                        pe.wait_ge(wt_split, count(16, s))
                        for b in range(qt + 1):
                            x = pe.transpose(aux[:, b // 4, b % 4 * P:(b % 4 + 1) * P],
                                             beta[:, s % 2, b * P:(b + 1) * P], ident[:])
                        x.then_inc(wt_ready, 1)

                    def values(s):
                        qt, hd, n = stick_step(s)
                        pe.wait_ge(wt_split, count(16, s + 1))
                        if qt == 0 and hd == 0:
                            drained(3)
                        if qt == 4:
                            pe.wait_ge(sbo_stored, count(4, hd + 1))
                        out = aux[0:SB_DIM, 2 + hd, qt % 4 * P:(qt % 4 + 1) * P]
                        for b in range(qt + 1):
                            v = slice(hd * SB_DIM, (hd + 1) * SB_DIM)
                            x = triple(out, sv_hi[:, b, v], sv_lo[:, b, v], wT_hi[:, s % 2, b * P:(b + 1) * P],
                                       wT_lo[:, s % 2, b * P:(b + 1) * P], b == 0, b == qt)
                        if qt % 4 == 3:
                            x.then_inc(sbo_ready, 1)

                    for s in range(18):
                        if s < 16:
                            logits(s)
                        if 1 <= s <= 16:
                            turn_w(s - 1)
                        if s >= 2:
                            values(s - 2)

            with pe.Fori(0, 2) as i:
                for g in range(2):
                    for j in range(2):
                        c = 3 * g + j
                        u = free_unit(U_GSB, GU, i, 4 * g + j)
                        project(i * 6 + (CH_GSB + c), c % 2, halves(u), x_hi, x_lo).then_inc(unit_ready, 1)
                    c = 3 * g + 2
                    for j in range(2):
                        u = free_unit(U_GSB, GU, i, 4 * g + 2 + j)
                        project(i * 6 + (CH_GSB + c), c % 2, halves(u), sbo_hi, sbo_lo, kts=4, w0=4 * j,
                                arrived=sbo_split).then_inc(unit_ready, 1)

            def residual(m, chunk, first, kts, arrived, stats):

                def sums(count, half, n0, n7):
                    pe.wait_ge(m.stat_split, count)
                    for b, (hi, lo) in enumerate(((st_hi, st_lo), (sqr_hi, sqr_lo))):
                        pe.matmul(aux[:, 2 * b + half, :], ln_ones[:], lo[:], start=n0, stop=False,
                                  skip_group_check=True)
                        x = pe.matmul(aux[:, 2 * b + half, :], ln_ones[:], hi[:], start=False, stop=n7,
                                      skip_group_check=True)
                    x.then_inc(m.sums_taken, 1)

                def body(i, is_first):
                    for j in range(2):
                        mid = None
                        if stats and (j or not is_first):
                            def mid(j=j):
                                sums(i * 4 + (1 if j else -1), 0, bool(is_first and j), False)
                        u = free_unit(first, 2, i, j)
                        last = project(i * 2 + (chunk + j), j, halves(u), a_hi, a_lo, kts=kts, arrived=arrived, mid=mid)
                        last.then_inc(unit_ready, 1)
                        if mid:
                            sums(i * 4 + (2 if j else 0), 1, bool(is_first and j), False)

                if not stats:
                    with pe.Fori(0, 4) as i:
                        body(i, False)
                    return
                body(0, True)
                with pe.Fori(1, 4) as i:
                    body(i, False)
                sums(15, 0, False, True)
                sums(16, 1, False, True)

            residual(n1, CH_MIX, U_MIX, KT, n1.a_split, True)

            with pe.Fori(0, MEM_HEADS) as h:
                pe.wait_ge(mem_split, KT)
                for k in range(2):
                    u = free_unit(U_MEM, XU, h, k)
                    for j in range(2):
                        c = 2 * k + j
                        last = project(h * 6 + (CH_MEM + c), c % 2, [(u[:, j * HALF:j * HALF + MEM], slice(0, MEM))],
                                       mem_hi, mem_lo)
                    last.then_inc(unit_ready, 1)
                u = free_unit(U_MEM, XU, h, 2)
                project(h * 6 + (CH_MEM + 4), 0, halves(u), x_hi, x_lo, arrived=n1.done).then_inc(unit_ready, 1)
                pe.wait_ge(unit_drained[1], h * 3 + (U_MEM // 2 + 1))
                pe.wait_ge(turn_split, h * 3)
                for dt in range(2):
                    for mt in range(2):
                        t = pe.transpose(aux[:, 2 + mt, dt * P:(dt + 1) * P], mv_T[:, dt, mt * P:(mt + 1) * P], ident[:])
                t.then_inc(turn_ready, 1)
                u = free_unit(U_MEM, XU, h, 3)
                project(h * 6 + (CH_MEM + 5), 1, halves(u), x_hi, x_lo).then_inc(unit_ready, 1)

                def scores(hf):
                    pe.wait_ge(exp_done, h * 2 + hf)
                    for tt in range(4):
                        tok = slice((hf * 4 + tt) * P, (hf * 4 + tt + 1) * P)
                        out = aux[:, tt // 2, tt % 2 * MEM:(tt % 2 + 1) * MEM]
                        for dt in range(2):
                            x = triple(out, mq_hi[:, dt, tok], mq_lo[:, dt, tok], mk_hi[:, dt, :], mk_lo[:, dt, :],
                                       dt == 0, dt == 1)
                    x.then_inc(s_ready, 1)

                def turn_p(hf):
                    pe.wait_ge(prob_ready, h * 2 + (hf + 1))
                    pe.wait_ge(turn_split, h * 3 + (hf + 1))
                    for tt in range(4):
                        for mt in range(2):
                            x = pe.transpose(aux[:, 2 + mt, tt * P:(tt + 1) * P], prob[:, tt, mt * P:(mt + 1) * P],
                                             ident[:])
                    x.then_inc(turn_ready, 1)

                def values(hf):
                    u = free_unit(U_MEM, XU, h, 4 + hf)
                    pe.wait_ge(turn_split, h * 3 + (hf + 2))
                    for dt in range(2):
                        for mt in range(2):
                            x = triple(u[:, dt * HALF:(dt + 1) * HALF], mv_hi[:, mt, dt * P:(dt + 1) * P],
                                       mv_lo[:, mt, dt * P:(dt + 1) * P], pT_hi[:, mt, :], pT_lo[:, mt, :],
                                       mt == 0, mt == 1)
                    x.then_inc(unit_ready, 1)

                pe.wait_ge(unit_drained[0], h * 3 + (U_MEM // 2 + 2))
                pe.wait_ge(unit_drained[1], h * 3 + (U_MEM // 2 + 2))
                scores(0)
                scores(1)
                turn_p(0)
                values(0)
                turn_p(1)
                values(1)

            residual(n2, CH_MO, U_MO, KT, n2.a_split, True)

            chunk, first, tiles = CH_FFN, U_FFN, 0
            for part, kts in enumerate(FFN_PARTS):
                with pe.Fori(0, kts) as j:
                    for g in range(2):
                        u = free_unit(first, 2, j, g)
                        project(j * 2 + (chunk + g), g, halves(u), x_hi, x_lo,
                                arrived=n2.done if part == 0 and g == 0 else None).then_inc(unit_ready, 1)
                chunk, first, tiles = chunk + 2 * kts, first + 2 * kts, tiles + kts
                pe.wait_ge(hid_lo, tiles)
                residual(n3, chunk, first, kts, None, part == 2)
                chunk, first = chunk + 8, first + 8

        @block.scalar
        def _(act):
            for j in range(4):
                act.dma_start(acc[:, 2 * j:2 * j + 2, :],
                              xT[2 * j * P:(2 * j + 2) * P, :].rearrange("(a p) t -> p a t", p=P)
                              ).then_inc(x_loaded[j], 16)
            for k in range(KT):
                act.wait_ge(x_loaded[k // 2], 16)
                act.activation(x_hi[:, k, :], acc[:, k, :], ACT.Copy).then_inc(x_hi_done, 1)

            with act.Fori(0, RET_HEADS) as h:
                def ready(k):
                    act.wait_ge(unit_ready, h * RU + (U_RET + k + 1))

                for w in range(2):
                    act.wait_ge(rotated, h * 2 + w)
                    act.dma_start(rope_sb[:].rearrange("p a t -> p (a t)"),
                                  rope[bass.ds(h * 2 + w, 1)].rearrange("a p t -> p (a t)")).then_inc(rope_loaded, 16)
                    act.wait_ge(rotated, h * 2 + (w + 1))
                    act.activation((rq_hi, rk_hi)[w][:], tmp_a[:], ACT.Copy).then_inc(rot_hi, 1)
                ready(2)
                act.wait_ge(rot_split, h * 2 + 2)
                act.activation(tmp_a[:], unit[:, 0, :], ACT.Copy).then_inc(unit_drained[0], 1)
                ready(3)
                act.activation(tmp_b[:], unit[:, 1, :], ACT.Copy).then_inc(unit_drained[1], 1)
                ready(4)
                act.activation(rv_hi[:, :, 0:P], unit[:, 0, :].rearrange("p (b d) -> p b d", d=P), ACT.Copy
                               ).then_inc(rv_hi_done, 1)
                ready(5)
                act.wait_ge(ret_gated, h * 2)
                act.activation(silu_g[:, 0, :], unit[:, 1, :], ACT.Silu).then_inc(unit_drained[1], 1)
                ready(6)
                act.activation(rv_hi[:, :, P:2 * P], unit[:, 0, :].rearrange("p (b d) -> p b d", d=P), ACT.Copy
                               ).then_inc(rv_hi_done, 1)

                def split_output(hf):
                    ready(7 + hf)
                    u = unit[:, (7 + hf) % 2, :]
                    act.wait_ge(ret_centered, h * 2 + hf)
                    act.wait_ge(norm_ready, h * 2 + hf)
                    act.activation(ro_hi[:].rearrange("p e t -> p (e t)"), u, ACT.Copy).then_inc(ro_copied, 1)
                    act.activation(tmp_b[:], u, ACT.Square).then_inc(ro_copied, 1)

                def deviation(hf):
                    act.wait_ge(norm_ready, h * 2 + (hf + 1))
                    act.wait_ge(r_rstd_ready, h * 2 + hf)
                    act.activation(r_mean2[:], aux[:, 2, :], ACT.Square).then_inc(r_mean_sq, 1)
                    act.wait_ge(r_var, h * 2 + (hf + 1))
                    act.activation(r_mean2[:], r_rstd[:], ACT.Sqrt).then_inc(r_std, 1)

                diags = 0
                for t in range(12):
                    hf, kb, q0, n = ret_tile(t)
                    a = P if q0 == kb * P else 0
                    if a:
                        diags += 1
                        if n > a:
                            act.wait_ge(diag_masked, h * 8 + diags)
                    if n > a:
                        act.wait_ge(rz_ready, h * 12 + (t + 1))
                        act.activation(rp_hi[:, t % 2, a:n], aux[:, t % 2, a:n], ACT.Copy).then_inc(rp_hi_done, 1)
                    if t == 3:
                        split_output(0)
                deviation(0)
                split_output(1)
                ready(9)
                act.activation(silu_g[:, 1, :], unit[:, 1, :], ACT.Silu).then_inc(unit_drained[1], 1)
                deviation(1)

            for k in range(KT):
                act.wait_ge(ret_gated, 2 * RET_HEADS)
                act.activation(ret_hi[:, k, :], acc[:, k, :], ACT.Copy).then_inc(ret_hi_done, 1)
            with act.Fori(0, KT) as n:
                act.wait_ge(unit_ready, n * 2 + (U_GRET + 1))
                act.wait_ge(unit_drained[1], n + U_GRET // 2)
                act.activation(gate_ret[:], unit[:, 0, :], ACT.Sigmoid, bias=par[:, bass.ds(n + 56, 1)]
                               ).then_inc(unit_drained[0], 1)

            act.wait_ge(unit_drained[1], U_SB // 2)
            act.dma_start(neg[:], consts[2]).then_inc(neg_loaded, 16)
            with act.Fori(0, SB_PAIRS // 2) as i:
                for pp in range(2):
                    def ready(k):
                        act.wait_ge(unit_ready, i * (2 * SU) + (U_SB + SU * pp + k + 1))

                    def count(per_pair, k):
                        return i * (2 * per_pair) + (per_pair * pp + k)

                    ready(0)
                    act.activation(sq_hi[:], unit[:, 0, :], ACT.Copy, scale=SB_DIM ** -0.5).then_inc(sqkv_hi, 1)
                    ready(1)
                    act.activation(sv_T[:], unit[:, 1, :], ACT.Copy).then_inc(unit_drained[1], 1)
                    ready(2)
                    act.activation(sk_hi[:], unit[:, 0, :], ACT.Copy).then_inc(sqkv_hi, 1)
                    ready(3)
                    act.activation(sv_hi[:].rearrange("p b d -> p (b d)"), unit[:, 1, :], ACT.Copy).then_inc(sqkv_hi, 1)

                    def split_w(s):
                        qt, hd, n = stick_step(s)
                        act.wait_ge(wt_ready, count(16, s + 1))
                        act.activation(wT_hi[:, s % 2, 0:n], aux[:, 0:2, :].rearrange("p b t -> p (b t)")[:, 0:n],
                                       ACT.Copy).then_inc(wt_hi, 1)

                    def store(s):
                        qt, hd, n = stick_step(s)
                        hf = qt // 4
                        act.wait_ge(sbo_ready, count(4, 2 * hf + hd + 1))
                        act.activation(sb_out[hd * SB_DIM:(hd + 1) * SB_DIM, bass.ds(i * 2 + pp, 1),
                                              hf * HALF:(hf + 1) * HALF].rearrange("p a t -> p (a t)"),
                                       aux[0:SB_DIM, 2 + hd, :], ACT.Copy).then_inc(sbo_stored, 1)

                    for s in range(18):
                        if s < 16:
                            qt, hd, n = stick_step(s)
                            slot = s % 2
                            ready(4 + s)
                            act.activation(beta[:, slot, 0:n], unit[:, slot, 0:n], ACT.Sigmoid).then_inc(beta_ready, 1)
                            act.wait_ge(stick_scanned, count(16, s))
                            act.activation(remain[:, 0:n], unit[:, slot, 0:n], ACT.Sigmoid, scale=-1.0
                                           ).then_inc(unit_drained[slot], 1)
                        if 1 <= s <= 16:
                            split_w(s - 1)
                        if s >= 2 and stick_step(s - 2)[0] % 4 == 3:
                            store(s - 2)

            for k in range(4):
                act.wait_ge(sbo_stored, 4 * SB_PAIRS)
                act.activation(sbo_hi[:, k, :], sb_out[:, k, :], ACT.Copy).then_inc(sbo_hi_done, 1)
            with act.Fori(0, 2) as i:
                for g in range(2):
                    for j in range(2):
                        act.wait_ge(unit_ready, i * GU + (U_GSB + 4 * g + j + 1))
                        act.wait_ge(branch_summed, i * 4 + 2 * g)
                        act.activation(gate_sb[:, j, :], unit[:, j, :], ACT.Sigmoid,
                                       bias=par[:, bass.ds(i * 4 + (48 + 2 * g + j), 1)]).then_inc(unit_drained[j], 1)

            def split_a(m, before, value):
                for k in range(KT):
                    act.wait_ge(before, value)
                    act.activation(a_hi[:, k, :], acc[:, k, :], ACT.Copy).then_inc(m.a_hi, 1)

            def statistics(m, first, by_drain):
                with act.Fori(0, KT // 2) as i:
                    for j in range(2):
                        if by_drain:
                            act.wait_ge(unit_drained[j], i + (first // 2 + 1))
                        else:
                            act.wait_ge(m.summed, i * 2 + (j + 1))
                        for hf in range(2):
                            r = acc[:, bass.ds(i * 2 + j, 1), hf * HALF:(hf + 1) * HALF].rearrange("p a t -> p (a t)")
                            act.wait_ge(m.sums_taken, i * 4 + (2 * j + hf))
                            act.activation(st_hi[:], r, ACT.Copy).then_inc(m.stat_hi, 1)
                            act.activation(sqr[:], r, ACT.Square).then_inc(m.stat_sq, 1)

            def deviation_ln(m):
                act.wait_ge(m.sums_taken, 2 * KT)
                act.activation(ln_mean2[:], aux[:, 0:2, :].rearrange("p b t -> p (b t)"), ACT.Square
                               ).then_inc(m.mean_sq, 1)
                act.wait_ge(m.var, 1)
                act.activation(ln_mean2[:], ln_rstd[:], ACT.Sqrt).then_inc(m.std, 1)

            def layer_norm(m, which):
                for k in range(KT):
                    g, b = par[:, 16 * which + k:16 * which + k + 1], par[:, 16 * which + 8 + k:16 * which + 9 + k]
                    act.wait_ge(m.scaled, k + 1)
                    if which == 2:
                        act.activation(y_out[:, k, :], ln_t[:, k % 2, :], ACT.Identity, scale=g, bias=b
                                       ).then_inc(y_ready, 1)
                        continue
                    if k >= 2:
                        act.wait_ge(m.done, k - 1)
                    act.activation(ln_x[:, k % 2, :], ln_t[:, k % 2, :], ACT.Identity, scale=g, bias=b
                                   ).then_inc(m.affine, 1)
                    act.wait_ge(m.affine, k + 1)
                    act.activation(x_hi[:, k, :], ln_x[:, k % 2, :], ACT.Copy).then_inc(m.hi, 1)

            split_a(n1, branch_summed, KT)
            statistics(n1, U_MIX, False)
            act.wait_ge(n1.sums_taken, 2 * KT)
            act.dma_start(mem_raw[:], memT.rearrange("(a p) t -> p a t", p=P)).then_inc(mem_loaded, 16)
            deviation_ln(n1)
            act.wait_ge(mem_loaded, 16)
            for k in range(0, KT, 4):
                act.activation(mem_hi[:, k:k + 4, :], mem_raw[:, k:k + 4, :], ACT.Copy).then_inc(mem_hi_done, 4)
            layer_norm(n1, 0)

            with act.Fori(0, MEM_HEADS) as h:
                def ready(k):
                    act.wait_ge(unit_ready, h * XU + (U_MEM + k + 1))

                def mem_unit(s):
                    return unit[:, s, :].rearrange("p (a t) -> p a t", a=2)[:, :, 0:MEM]

                ready(0)
                act.activation(mk_hi[:], mem_unit(0), ACT.Copy, scale=MEM_DIM ** -0.5).then_inc(mkq_hi, 1)
                ready(1)
                act.activation(mv_T[:], mem_unit(1), ACT.Copy).then_inc(unit_drained[1], 1)
                ready(2)
                act.activation(mq_hi[:, 0, :], unit[:, 0, :], ACT.Copy).then_inc(mkq_hi, 1)
                act.wait_ge(turn_ready, h * 3 + 1)
                act.activation(mv_hi[:], aux[:, 2:4, 0:MEM_DIM], ACT.Copy).then_inc(turn_hi, 1)
                ready(3)
                act.activation(mq_hi[:, 1, :], unit[:, 1, :], ACT.Copy).then_inc(mkq_hi, 1)

                def exponent(hf):
                    act.wait_ge(neg_ready, h * 2 + (hf + 1))
                    act.wait_ge(turn_ready, h * 3 + (hf + 1))
                    for tt in range(4):
                        x = act.activation(prob[:, tt, :], aux[:, tt // 2, tt % 2 * MEM:(tt % 2 + 1) * MEM], ACT.Exp,
                                           bias=neg_max[:, tt:tt + 1], accum_out=row_sum[:, tt:tt + 1])
                    x.then_inc(exp_done, 1)

                def split_p(hf):
                    act.wait_ge(turn_ready, h * 3 + (hf + 2))
                    if hf:
                        ready(4)
                    act.activation(pT_hi[:], aux[:, 2:4, :], ACT.Copy).then_inc(turn_hi, 1)

                def store(hf):
                    ready(4 + hf)
                    act.activation(acc[:, bass.ds(h * 2, 2), hf * HALF:(hf + 1) * HALF],
                                   unit[:, hf, :].rearrange("p (a t) -> p a t", a=2), ACT.Copy
                                   ).then_inc(unit_drained[hf], 1)

                exponent(0)
                split_p(0)
                exponent(1)
                store(0)
                split_p(1)
                store(1)

            split_a(n2, unit_drained[1], U_MO // 2)
            statistics(n2, U_MO, False)
            deviation_ln(n2)
            layer_norm(n2, 1)

            first, tiles = U_FFN, 0
            for part, kts in enumerate(FFN_PARTS):
                with act.Fori(0, kts) as j:
                    act.wait_ge(unit_ready, j * 2 + (first + 1))
                    act.activation(silu_h[:], unit[:, 0, :], ACT.Silu).then_inc(unit_drained[0], 1)
                    act.wait_ge(unit_drained[1], j + (first // 2 + 1))
                    act.activation(a_hi[:, bass.ds(j, 1), :].rearrange("p a t -> p (a t)"), hidden[:], ACT.Copy
                                   ).then_inc(hid_hi, 1)
                first, tiles = first + 2 * kts + 8, tiles + kts
            statistics(n3, first - 8, True)
            deviation_ln(n3)
            layer_norm(n3, 2)

        @block.vector
        def _(dve):
            dve.memset(f32(ret_ones[:]), 1.0 / RET_V).then_inc(consts_ready, 1)
            dve.memset(f32(ln_ones[:]), 1.0 / D)
            dve.wait_ge(consts_loaded, 48)
            for k in range(KT):
                dve.wait_ge(x_hi_done, k + 1)
                dve.tensor_tensor(x_lo[:, k, :], acc[:, k, :], f32(x_hi[:, k, :]), ALU.subtract).then_inc(x_split, 1)
                if k == 0:
                    dve.memset(diag[:], 0.0).then_inc(consts_ready, 1)

            with dve.Fori(0, RET_HEADS) as h:
                def ready(k):
                    dve.wait_ge(unit_ready, h * RU + (U_RET + k + 1))

                for w in range(2):
                    u = unit[:, w, :]
                    ready(w)
                    dve.wait_ge(rope_loaded, h * 32 + 16 * (w + 1))
                    if w:
                        dve.wait_ge(rot_split, h * 2 + 1)
                    dve.tensor_tensor(tmp_a[:], u, rope_sb[:, 0, :], ALU.mult).then_inc(rope_products, 1)
                    dve.tensor_tensor(tmp_b[0:64, :], u[64:128, :], rope_sb[64:128, 1, :], ALU.mult
                                      ).then_inc(rope_products, 1)
                    dve.tensor_tensor(tmp_b[64:128, :], u[0:64, :], rope_sb[0:64, 1, :], ALU.mult
                                      ).then_inc(unit_drained[w], 1)
                    dve.wait_ge(rope_products, h * 4 + 2 * (w + 1))
                    dve.wait_ge(unit_drained[w], h * 5 + 1)
                    dve.tensor_tensor(tmp_a[:], tmp_a[:], tmp_b[:], ALU.add).then_inc(rotated, 1)
                    dve.wait_ge(rot_hi, h * 2 + (w + 1))
                    dve.tensor_tensor((rq_lo, rk_lo)[w][:], tmp_a[:], f32((rq_hi, rk_hi)[w][:]), ALU.subtract
                                      ).then_inc(rot_split, 1)
                for k, e in ((4, 0), (6, 1)):
                    dve.wait_ge(rv_hi_done, h * 2 + (e + 1))
                    dve.tensor_tensor(rv_lo[:, :, e * P:(e + 1) * P], unit[:, 0, :].rearrange("p (b d) -> p b d", d=P),
                                      f32(rv_hi[:, :, e * P:(e + 1) * P]), ALU.subtract).then_inc(unit_drained[0], 1)

                def split_output(hf):
                    u = unit[:, (7 + hf) % 2, :]
                    dve.wait_ge(ro_copied, h * 4 + 2 * (hf + 1))
                    dve.tensor_tensor(ro_lo[:].rearrange("p e t -> p (e t)"), u,
                                      f32(ro_hi[:].rearrange("p e t -> p (e t)")), ALU.subtract
                                      ).then_inc(unit_drained[(7 + hf) % 2], 1)
                    dve.tensor_copy(rs_hi[:].rearrange("p e t -> p (e t)"), tmp_b[:]).then_inc(rs_hi_done, 1)
                    dve.wait_ge(rs_hi_done, h * 2 + (hf + 1))
                    dve.tensor_tensor(rs_lo[:].rearrange("p e t -> p (e t)"), tmp_b[:],
                                      f32(rs_hi[:].rearrange("p e t -> p (e t)")), ALU.subtract).then_inc(rs_split, 1)

                def normalise(hf):
                    m = h * 2 + (hf + 1)
                    wide = tmp_a[:].rearrange("p (e t) -> p e t", e=2)
                    dve.wait_ge(ret_normed, h * 2 + hf)
                    dve.wait_ge(r_mean_sq, m)
                    dve.scalar_tensor_tensor(out=r_rstd[:], in0=aux[:, 3, :], scalar=EPS, in1=r_mean2[:],
                                             op0=ALU.add, op1=ALU.subtract).then_inc(r_var, 1)
                    dve.tensor_tensor(wide, f32(ro_hi[:]), aux[:, 2:3, :].to_broadcast([P, 2, HALF]), ALU.subtract
                                      ).then_inc(ret_centered, 1)
                    dve.wait_ge(ret_centered, m)
                    dve.tensor_tensor(wide, wide, f32(ro_lo[:]), ALU.add).then_inc(ret_whole, 1)
                    dve.wait_ge(r_std, m)
                    dve.reciprocal(r_rstd[:], r_mean2[:]).then_inc(r_rstd_ready, 1)
                    dve.wait_ge(r_rstd_ready, m)
                    dve.wait_ge(ret_whole, m)
                    dve.tensor_tensor(acc[:, bass.ds(h * 2, 2), hf * HALF:(hf + 1) * HALF], wide,
                                      r_rstd[:, None, :].to_broadcast([P, 2, HALF]), ALU.mult).then_inc(ret_normed, 1)

                tiles_hi = diags = pure_diags = 0
                for t in range(12):
                    hf, kb, q0, n = ret_tile(t)
                    a = P if q0 == kb * P else 0
                    if a:
                        dve.wait_ge(rp_split, h * 12 + t)
                        dve.wait_ge(rz_ready, h * 12 + (t + 1))
                        dve.tensor_tensor(diag[:], aux[:, t % 2, 0:P], causal[:], ALU.mult).then_inc(diag_masked, 1)
                        dve.wait_ge(diag_masked, h * 8 + (diags + 1))
                        dve.tensor_copy(rp_hi[:, t % 2, 0:P], diag[:]).then_inc(diag_hi, 1)
                        dve.wait_ge(diag_hi, h * 8 + (diags + 1))
                        dve.tensor_tensor(rp_lo[:, t % 2, 0:P], diag[:], f32(rp_hi[:, t % 2, 0:P]), ALU.subtract
                                          ).then_inc(diag_lo if n > a else rp_split, 1)
                        diags += 1
                    if n > a:
                        tiles_hi += 1
                        dve.wait_ge(rp_hi_done, h * 10 + tiles_hi)
                        dve.tensor_tensor(rp_lo[:, t % 2, a:n], aux[:, t % 2, a:n], f32(rp_hi[:, t % 2, a:n]),
                                          ALU.subtract).then_inc(rp_split, 1)
                    if t == 3:
                        split_output(0)
                normalise(0)
                split_output(1)
                normalise(1)
                dve.wait_ge(ret_normed, h * 2 + 2)
                dve.wait_ge(unit_drained[1], h * 5 + 5)
                for e in range(2):
                    r = acc[:, bass.ds(h * 2 + e, 1), :].rearrange("p a t -> p (a t)")
                    dve.tensor_tensor(r, r, silu_g[:, e, :], ALU.mult).then_inc(ret_gated, 1)

            for k in range(KT):
                dve.wait_ge(ret_hi_done, k + 1)
                dve.tensor_tensor(ret_lo[:, k, :], acc[:, k, :], f32(ret_hi[:, k, :]), ALU.subtract).then_inc(ret_split, 1)
            with dve.Fori(0, KT) as n:
                dve.wait_ge(unit_ready, n * 2 + (U_GRET + 2))
                dve.wait_ge(unit_drained[0], n + (U_GRET // 2 + 1))
                dve.tensor_tensor(acc[:, bass.ds(n, 1), :].rearrange("p a t -> p (a t)"), unit[:, 1, :], gate_ret[:],
                                  ALU.mult).then_inc(unit_drained[1], 1)

            dve.memset(stick[:, SEQ:SEQ + 1], 1.0).then_inc(stick_consts, 1)
            dve.tensor_copy(ident_r[:], ident[:]).then_inc(stick_consts, 1)
            dve.wait_ge(neg_loaded, 16)
            dve.tensor_copy(neg_r[:], neg[:]).then_inc(stick_consts, 2)
            with dve.Fori(0, SB_PAIRS // 2) as i:
                for pp in range(2):
                    def count(per_pair, k):
                        return i * (2 * per_pair) + (per_pair * pp + k)

                    dve.wait_ge(sqkv_hi, count(3, 1))
                    dve.scalar_tensor_tensor(out=sq_lo[:], in0=unit[:, 0, :], scalar=SB_DIM ** -0.5, in1=f32(sq_hi[:]),
                                             op0=ALU.mult, op1=ALU.subtract).then_inc(unit_drained[0], 1)
                    dve.wait_ge(sqkv_hi, count(3, 2))
                    dve.tensor_tensor(sk_lo[:], unit[:, 0, :], f32(sk_hi[:]), ALU.subtract).then_inc(unit_drained[0], 1)
                    dve.wait_ge(sqkv_hi, count(3, 3))
                    dve.tensor_tensor(sv_lo[:].rearrange("p b d -> p (b d)"), unit[:, 1, :],
                                      f32(sv_hi[:].rearrange("p b d -> p (b d)")), ALU.subtract
                                      ).then_inc(unit_drained[1], 1)
                    for s in range(17):
                        if s < 16:
                            qt, hd, n = stick_step(s)
                            slot = s % 2
                            dve.wait_ge(unit_drained[slot], i * SU + ((U_SB + SU * pp + 4 + s) // 2 + 1))
                            dve.wait_ge(w_ready, count(16, s))
                            left = stick[:, SEQ - n:SEQ]
                            dve.tensor_tensor_scan(left[:, ::-1], remain[:, 0:n][:, ::-1], remain[:, 0:n][:, ::-1], 1.0,
                                                   ALU.mult, ALU.bypass).then_inc(stick_scanned, 1)
                            dve.wait_ge(stick_scanned, count(16, s + 1))
                            dve.tensor_tensor(beta[:, slot, 0:n], beta[:, slot, 0:n], stick[:, SEQ - n + 1:SEQ + 1],
                                              ALU.mult).then_inc(w_ready, 1)
                        if s >= 1:
                            qt, hd, n = stick_step(s - 1)
                            dve.wait_ge(wt_hi, count(16, s))
                            dve.tensor_tensor(wT_lo[:, (s - 1) % 2, 0:n],
                                              aux[:, 0:2, :].rearrange("p b t -> p (b t)")[:, 0:n],
                                              f32(wT_hi[:, (s - 1) % 2, 0:n]), ALU.subtract).then_inc(wt_split, 1)

            for k in range(4):
                dve.wait_ge(sbo_hi_done, k + 1)
                dve.tensor_tensor(sbo_lo[:, k, :], sb_out[:, k, :], f32(sbo_hi[:, k, :]), ALU.subtract
                                  ).then_inc(sbo_split, 1)
            with dve.Fori(0, 2) as i:
                for g in range(2):
                    for j in range(2):
                        k = 4 * g + 2 + j
                        dve.wait_ge(unit_ready, i * GU + (U_GSB + k + 1))
                        dve.wait_ge(unit_drained[j], i * (GU // 2) + (U_GSB // 2 + 2 * g + 1))
                        dve.tensor_tensor(gate_sb[:, j, :], gate_sb[:, j, :], unit[:, j, :], ALU.mult
                                          ).then_inc(unit_drained[j], 1)
                        dve.wait_ge(unit_drained[j], i * (GU // 2) + (U_GSB // 2 + 2 * g + 2))
                        r = acc[:, bass.ds(i * 4 + (2 * g + j), 1), :].rearrange("p a t -> p (a t)")
                        dve.tensor_tensor(r, r, gate_sb[:, j, :], ALU.add).then_inc(branch_summed, 1)

            def split_a(m):
                for k in range(KT):
                    dve.wait_ge(m.a_hi, k + 1)
                    dve.tensor_tensor(a_lo[:, k, :], acc[:, k, :], f32(a_hi[:, k, :]), ALU.subtract
                                      ).then_inc(m.a_split, 1)

            def residual(m, first, add_x, stats):
                with dve.Fori(0, 4) as i:
                    for j in range(2):
                        n = i * 2 + j
                        r = acc[:, bass.ds(n, 1), :].rearrange("p a t -> p (a t)")
                        dve.wait_ge(unit_ready, i * 2 + (first + j + 1))
                        if add_x:
                            xh = f32(x_hi[:, bass.ds(n, 1), :].rearrange("p a t -> p (a t)"))
                            xl = f32(x_lo[:, bass.ds(n, 1), :].rearrange("p a t -> p (a t)"))
                            dve.scalar_tensor_tensor(out=r, in0=xh, scalar=ALPHA, in1=unit[:, j, :], op0=ALU.mult,
                                                     op1=ALU.add).then_inc(unit_drained[j], 1)
                            dve.wait_ge(unit_drained[j], i + (first // 2 + 1))
                            dve.scalar_tensor_tensor(out=r, in0=xl, scalar=ALPHA, in1=r, op0=ALU.mult, op1=ALU.add
                                                     ).then_inc(m.summed, 1)
                        else:
                            dve.tensor_tensor(r, r, unit[:, j, :], ALU.add).then_inc(unit_drained[j], 1)
                        if not stats:
                            continue
                        for hf in range(2):
                            c = i * 4 + (2 * j + hf + 1)
                            dve.wait_ge(m.stat_sq, c)
                            dve.tensor_tensor(st_lo[:], r[:, hf * HALF:(hf + 1) * HALF], f32(st_hi[:]), ALU.subtract)
                            dve.tensor_copy(sqr_hi[:], sqr[:]).then_inc(m.sqr_hi, 1)
                            dve.wait_ge(m.sqr_hi, c)
                            dve.tensor_tensor(sqr_lo[:], sqr[:], f32(sqr_hi[:]), ALU.subtract).then_inc(m.stat_split, 1)

            def deviation(m):
                dve.wait_ge(m.mean_sq, 1)
                dve.scalar_tensor_tensor(out=ln_rstd[:], in0=aux[:, 2:4, :].rearrange("p b t -> p (b t)"), scalar=EPS,
                                         in1=ln_mean2[:], op0=ALU.add, op1=ALU.subtract).then_inc(m.var, 1)
                dve.wait_ge(m.std, 1)
                dve.reciprocal(ln_rstd[:], ln_mean2[:]).then_inc(m.rstd, 1)
                dve.wait_ge(m.rstd, 1)

            def layer_norm(m, last):
                for k in range(KT + 1):
                    if k < KT:
                        t = ln_t[:, k % 2, :]
                        if k >= 2:
                            dve.wait_ge(y_ready if last else m.affine, k - 1)
                        dve.tensor_tensor(t, acc[:, k, :], aux[:, 0:2, :].rearrange("p b t -> p (b t)"), ALU.subtract
                                          ).then_inc(m.centered, 1)
                        dve.wait_ge(m.centered, k + 1)
                        dve.tensor_tensor(t, t, ln_rstd[:], ALU.mult).then_inc(m.scaled, 1)
                    if k and not last:
                        dve.wait_ge(m.hi, k)
                        dve.tensor_tensor(x_lo[:, k - 1, :], ln_x[:, (k - 1) % 2, :], f32(x_hi[:, k - 1, :]),
                                          ALU.subtract).then_inc(m.done, 1)

            split_a(n1)
            residual(n1, U_MIX, True, True)
            deviation(n1)
            for k in range(0, KT, 4):
                dve.wait_ge(mem_hi_done, k + 4)
                dve.tensor_tensor(mem_lo[:, k:k + 4, :], mem_raw[:, k:k + 4, :], f32(mem_hi[:, k:k + 4, :]),
                                  ALU.subtract).then_inc(mem_split, 4)
            layer_norm(n1, False)

            with dve.Fori(0, MEM_HEADS) as h:
                dve.wait_ge(mkq_hi, h * 3 + 1)
                dve.scalar_tensor_tensor(out=mk_lo[:], in0=unit[:, 0, :].rearrange("p (a t) -> p a t", a=2)[:, :, 0:MEM],
                                         scalar=MEM_DIM ** -0.5, in1=f32(mk_hi[:]), op0=ALU.mult, op1=ALU.subtract
                                         ).then_inc(unit_drained[0], 1)
                dve.wait_ge(mkq_hi, h * 3 + 2)
                dve.tensor_tensor(mq_lo[:, 0, :], unit[:, 0, :], f32(mq_hi[:, 0, :]), ALU.subtract
                                  ).then_inc(unit_drained[0], 1)
                dve.wait_ge(turn_hi, h * 3 + 1)
                dve.tensor_tensor(mv_lo[:], aux[:, 2:4, 0:MEM_DIM], f32(mv_hi[:]), ALU.subtract).then_inc(turn_split, 1)
                dve.wait_ge(mkq_hi, h * 3 + 3)
                dve.tensor_tensor(mq_lo[:, 1, :], unit[:, 1, :], f32(mq_hi[:, 1, :]), ALU.subtract
                                  ).then_inc(unit_drained[1], 1)

                def maxima(hf):
                    m = h * 2 + (hf + 1)
                    dve.wait_ge(s_ready, m)
                    dve.tensor_reduce(neg_max[:], aux[:, 0:2, :].rearrange("p b (t m) -> p (b t) m", m=MEM), AX_X, ALU.max
                                      ).then_inc(max_ready, 1)
                    dve.wait_ge(max_ready, m)
                    dve.tensor_scalar(neg_max[:], neg_max[:], -1.0, None, ALU.mult).then_inc(neg_ready, 1)

                def probabilities(hf):
                    m = h * 2 + (hf + 1)
                    dve.wait_ge(exp_done, m)
                    dve.reciprocal(inv_sum[:], row_sum[:]).then_inc(inv_ready, 1)
                    dve.wait_ge(inv_ready, m)
                    for tt in range(4):
                        x = dve.tensor_scalar(prob[:, tt, :], prob[:, tt, :], inv_sum[:, tt:tt + 1], None, ALU.mult)
                    x.then_inc(prob_ready, 1)

                def split_p(hf):
                    dve.wait_ge(turn_hi, h * 3 + (hf + 2))
                    dve.tensor_tensor(pT_lo[:], aux[:, 2:4, :], f32(pT_hi[:]), ALU.subtract).then_inc(turn_split, 1)

                maxima(0)
                probabilities(0)
                maxima(1)
                split_p(0)
                probabilities(1)
                split_p(1)

            split_a(n2)
            residual(n2, U_MO, True, True)
            deviation(n2)
            layer_norm(n2, False)

            first, tiles = U_FFN, 0
            for part, kts in enumerate(FFN_PARTS):
                with dve.Fori(0, kts) as j:
                    dve.wait_ge(unit_ready, j * 2 + (first + 2))
                    dve.wait_ge(unit_drained[0], j + (first // 2 + 1))
                    dve.wait_ge(hid_lo, j + tiles)
                    dve.tensor_tensor(hidden[:], unit[:, 1, :], silu_h[:], ALU.mult).then_inc(unit_drained[1], 1)
                    dve.wait_ge(hid_hi, j + (tiles + 1))
                    dve.tensor_tensor(a_lo[:, bass.ds(j, 1), :].rearrange("p a t -> p (a t)"), hidden[:],
                                      f32(a_hi[:, bass.ds(j, 1), :].rearrange("p a t -> p (a t)")), ALU.subtract
                                      ).then_inc(hid_lo, 1)
                first, tiles = first + 2 * kts, tiles + kts
                residual(n3, first, part == 0, part == 2)
                first += 8
            deviation(n3)
            layer_norm(n3, True)


def ret_tile(t):
    hf, kb = (0, t) if t < 4 else (1, t - 4)
    q0 = max(hf * HALF, kb * P)
    return hf, kb, q0, (hf + 1) * HALF - q0


def stick_step(s):
    return s // 2, s % 2, (s // 2 + 1) * P


def blocks_of(w):
    k, n = w.shape
    return np.ascontiguousarray(w.reshape(k // P, P, n // P, P).transpose(2, 1, 0, 3))


def weight_streams(w_in, w_sb_o, w_ret_o, w_mix_o, w_mem_q, w_mem_kv, w_mem_o, w_ffn_in, w_ffn_out):
    win, kv, q = blocks_of(w_in), blocks_of(w_mem_kv), blocks_of(w_mem_q)
    ret_o, sb_o, ffn_in, ffn_out = blocks_of(w_ret_o), blocks_of(w_sb_o), blocks_of(w_ffn_in), blocks_of(w_ffn_out)
    eight, seven = [], []
    for h in range(RET_HEADS):
        v, g = BLK_RET_V + 2 * h, BLK_RET_G + 2 * h
        eight += [win[BLK_RET_Q + h], win[BLK_RET_K + h], win[v], win[v + 1], win[g], win[g + 1]]
    for n in range(KT):
        eight += [win[BLK_GATE_RET + n], ret_o[n]]
    for p in range(SB_PAIRS):
        eight += [win[BLK_SB_Q + p], win[BLK_SB_V + p], win[BLK_SB_K + p]]
    for n in range(0, KT, 2):
        eight += [win[BLK_GATE_SB + n], win[BLK_GATE_SB + n + 1], np.concatenate([sb_o[n], sb_o[n + 1]], 1)]
    eight += list(blocks_of(w_mix_o))
    for h in range(MEM_HEADS):
        eight += [kv[2 * h], kv[2 * h + 1], kv[KT + 2 * h], kv[KT + 2 * h + 1], q[2 * h], q[2 * h + 1]]
    eight += list(blocks_of(w_mem_o))
    j0 = 0
    for kts in FFN_PARTS:
        for j in range(j0, j0 + kts):
            eight += [ffn_in[j], ffn_in[FFN_TILES + j]]
        (eight if kts == 8 else seven).extend(ffn_out[n][:, j0:j0 + kts] for n in range(KT))
        j0 += kts
    return (np.ascontiguousarray(np.stack(eight).reshape(len(eight), P, 8 * P)),
            np.ascontiguousarray(np.stack(seven).reshape(len(seven), P, 7 * P)))


def rope_tables():
    half = RET_QK // 2
    inv = (1.0 / (np.float32(10000.0) ** (np.arange(half, dtype=np.float32) / np.float32(half)))).astype(np.float32)
    pos = np.arange(SEQ, dtype=np.float32)
    ang = (pos[None, :] * inv[:, None]).astype(np.float64)
    cos = np.concatenate([np.cos(ang), np.cos(ang)], 0)
    sin = np.concatenate([np.sin(ang), -np.sin(ang)], 0)
    out = np.empty((RET_HEADS, 2, P, 2, SEQ), np.float64)
    for h in range(RET_HEADS):
        log_gamma = float(np.float32(np.log1p(-(2.0 ** (-5.0 - h)))))
        rel = log_gamma * (np.arange(SEQ) - SEQ // 2)
        for w, f in enumerate((np.exp(rel) * RET_QK ** -0.5, np.exp(-rel))):
            out[h, w, :, 0], out[h, w, :, 1] = cos * f, sin * f
    return out.astype(np.float32).reshape(2 * RET_HEADS, P, 2 * SEQ)


def kernel(x, mem, w_in, b_gate, w_sb_o, w_ret_o, w_mix_o, ln1_g, ln1_b, w_mem_q, w_mem_kv, w_mem_o, ln2_g, ln2_b,
           w_ffn_in, w_ffn_out, ln3_g, ln3_b):
    import concourse.bacc as _bacc
    from concourse.bass_utils import run_bass_kernel_spmd as _run

    x, mem = np.asarray(x), np.asarray(mem)
    eight, seven = weight_streams(*(np.asarray(w)[0] for w in (
        w_in, w_sb_o, w_ret_o, w_mix_o, w_mem_q, w_mem_kv, w_mem_o, w_ffn_in, w_ffn_out)))
    vectors = [np.asarray(v)[0].reshape(-1, P).T for v in (ln1_g, ln1_b, ln2_g, ln2_b, ln3_g, ln3_b, b_gate)]
    row, col = np.arange(P)[:, None], np.arange(P)[None, :]
    arrays = {
        "xT": np.ascontiguousarray(x[0].T),
        "memT": np.ascontiguousarray(mem[0].T),
        "stream8": eight,
        "stream7": seven,
        "params": np.ascontiguousarray(np.concatenate(vectors, 1)),
        "rope": rope_tables(),
        "consts": np.stack([row == col, col >= row, MASKED * (col >= row)]).astype(np.float32),
    }
    nc = _bacc.Bacc("TRN2", target_bir_lowering=False, num_devices=1)
    args = [nc.dram_tensor(n, a.shape, mybir.dt.from_np(a.dtype), kind="ExternalInput").ap() for n, a in arrays.items()]
    args.append(nc.dram_tensor("outT", (D, SEQ), F32, kind="ExternalOutput").ap())
    layer_program(nc, *args)
    r = _run(nc, [arrays], core_ids=[0])
    return np.ascontiguousarray(r.results[0]["outT"].T)[None]
```

```python
from contextlib import ExitStack

import numpy as np

import concourse.bass as bass
from concourse import mybir

ALU = mybir.AluOpType
ACT = mybir.ActivationFunctionType
F32 = mybir.dt.float32
F32R = mybir.dt.float32r
AX_X = mybir.AxisListType.X

P = 128
D = 1024
SEQ = 1024
HALF = 512
KT = D // P
MEM = 256
SB_HEADS, SB_DIM = 8, 64
SB_PAIRS = SB_HEADS // 2
SB_WIDTH = SB_HEADS * SB_DIM
RET_HEADS, RET_QK, RET_V = 4, 128, 256
RET_WIDTH = RET_HEADS * RET_V
MEM_HEADS, MEM_DIM = 4, 256
FFN = 2816
FFN_TILES = FFN // P
FFN_PARTS = (8, 7, 7)
ALPHA = 2.0 ** 0.25
EPS = 1e-5
QT = SEQ // P
MASKED = -1e30

BLK_SB_Q, BLK_SB_K, BLK_SB_V = 0, 4, 8
BLK_RET_Q, BLK_RET_K, BLK_RET_V, BLK_RET_G = 12, 16, 20, 28
BLK_GATE_SB, BLK_GATE_RET = 36, 44

CH_RET, CH_GRET, CH_SB, CH_GSB, CH_MIX, CH_MEM, CH_MO, CH_FFN = 0, 24, 40, 56, 64, 72, 96, 104
U_RET, U_GRET, U_SB, U_GSB, U_MIX, U_MEM, U_MO, U_FFN = 0, 40, 56, 136, 148, 156, 180, 188
RU, SU, GU, XU = 10, 20, 6, 6


def f32(ap):
    return ap.bitcast(F32)


def half(hf):
    return slice(hf * HALF, (hf + 1) * HALF)


def layer_program(nc, xT, memT, stream8, stream7, params, rope, consts, outT):
    ctx = ExitStack()
    with ctx:
        def sem(name):
            return ctx.enter_context(nc.semaphore(name))

        def sb(stack, name, shape, dt=F32):
            return stack.enter_context(nc.sbuf_tensor(name, shape, dt))

        x_hi = sb(ctx, "x_hi", [P, KT, SEQ], F32R)
        x_lo = sb(ctx, "x_lo", [P, KT, SEQ], F32R)
        acc = sb(ctx, "acc", [P, KT, SEQ])
        w_raw = sb(ctx, "w_raw", [P, 2, D])
        w_hi = [sb(ctx, f"w_hi{s}", [P, D], F32R) for s in range(2)]
        w_lo = [sb(ctx, f"w_lo{s}", [P, D], F32R) for s in range(2)]
        par = sb(ctx, "par", [P, 64])
        one = sb(ctx, "one", [P, 1])
        ident = sb(ctx, "ident", [P, P])
        causal = sb(ctx, "causal", [P, P])
        ln_ones = sb(ctx, "ln_ones", [P, P], F32R)

        with ExitStack() as st:
            rq_hi, rq_lo = sb(st, "rq_hi", [P, SEQ], F32R), sb(st, "rq_lo", [P, SEQ], F32R)
            rk_hi, rk_lo = sb(st, "rk_hi", [P, SEQ], F32R), sb(st, "rk_lo", [P, SEQ], F32R)
            rv_hi, rv_lo = sb(st, "rv_hi", [P, QT, RET_V], F32R), sb(st, "rv_lo", [P, QT, RET_V], F32R)
            tmp_a, tmp_b = sb(st, "tmp_a", [P, SEQ]), sb(st, "tmp_b", [P, SEQ])
            rope_sb = sb(st, "rope_sb", [P, 2, SEQ])
            rp_hi, rp_lo = sb(st, "rp_hi", [P, 2, HALF], F32R), sb(st, "rp_lo", [P, 2, HALF], F32R)
            ro_hi, ro_lo = sb(st, "ro_hi", [P, 2, HALF], F32R), sb(st, "ro_lo", [P, 2, HALF], F32R)
            rs_hi, rs_lo = sb(st, "rs_hi", [P, 2, HALF], F32R), sb(st, "rs_lo", [P, 2, HALF], F32R)
            r_mean2, r_rstd = sb(st, "r_mean2", [P, HALF]), sb(st, "r_rstd", [P, HALF])
            silu_g = sb(st, "silu_g", [P, 2, SEQ])
            diag = sb(st, "diag", [P, P])
            ret_ones = sb(st, "ret_ones", [P, P], F32R)
        with ExitStack() as st:
            ret_hi, ret_lo = sb(st, "ret_hi", [P, KT, SEQ], F32R), sb(st, "ret_lo", [P, KT, SEQ], F32R)
            gate_ret = sb(st, "gate_ret", [P, SEQ])
        with ExitStack() as st:
            sb_out = sb(st, "sb_out", [P, 4, SEQ])
            early_gate = sb(st, "early_gate", [P, 4, SEQ])
            with ExitStack() as s2:
                sq_hi, sq_lo = sb(s2, "sq_hi", [P, SEQ], F32R), sb(s2, "sq_lo", [P, SEQ], F32R)
                sk_hi, sk_lo = sb(s2, "sk_hi", [P, SEQ], F32R), sb(s2, "sk_lo", [P, SEQ], F32R)
                sv_hi, sv_lo = sb(s2, "sv_hi", [P, QT, P], F32R), sb(s2, "sv_lo", [P, QT, P], F32R)
                beta = sb(s2, "beta", [P, 2, SEQ])
                sv_T = beta[:, 1, :]
                stick = sb(s2, "stick", [P, SEQ + 1])
                wT_hi, wT_lo = sb(s2, "wT_hi", [P, 2, SEQ], F32R), sb(s2, "wT_lo", [P, 2, SEQ], F32R)
                ident_r = sb(s2, "ident_r", [P, P], F32R)
                neg_r = sb(s2, "neg_r", [P, P], F32R)
                neg = beta[:, 1, 0:P]
            with ExitStack() as s2:
                sbo_hi, sbo_lo = sb(s2, "sbo_hi", [P, 4, SEQ], F32R), sb(s2, "sbo_lo", [P, 4, SEQ], F32R)
                gate_sb = sb(s2, "gate_sb", [P, 2, SEQ])
        with ExitStack() as st:
            a_hi, a_lo = sb(st, "a_hi", [P, KT, SEQ], F32R), sb(st, "a_lo", [P, KT, SEQ], F32R)
            with ExitStack() as s2:
                st_hi, st_lo, sqr_hi, sqr_lo = ([sb(s2, f"{n}{hf}", [P, HALF], F32R) for hf in range(2)]
                                                for n in ("st_hi", "st_lo", "sqr_hi", "sqr_lo"))
                sqr = [sb(s2, f"sqr{hf}", [P, HALF]) for hf in range(2)]
            with ExitStack() as s2:
                silu_h = sb(s2, "silu_h", [P, SEQ])
                hidden = sb(s2, "hidden", [P, SEQ])
        with ExitStack() as st:
            y_out = sb(st, "y_out", [P, KT, SEQ])
        with ExitStack() as st:
            mem_raw = sb(st, "mem_raw", [P, KT, MEM])
            mem_hi, mem_lo = sb(st, "mem_hi", [P, KT, MEM], F32R), sb(st, "mem_lo", [P, KT, MEM], F32R)
            mk_hi, mk_lo = sb(st, "mk_hi", [P, 2, MEM], F32R), sb(st, "mk_lo", [P, 2, MEM], F32R)
            mv_T = sb(st, "mv_T", [P, 2, MEM])
            mv_hi, mv_lo = sb(st, "mv_hi", [P, 2, MEM_DIM], F32R), sb(st, "mv_lo", [P, 2, MEM_DIM], F32R)
            with ExitStack() as s2:
                ln_mean2, ln_rstd = sb(s2, "ln_mean2", [P, SEQ]), sb(s2, "ln_rstd", [P, SEQ])
                ln_t = sb(s2, "ln_t", [P, 4, HALF])
                ln_x = sb(s2, "ln_x", [P, 4, HALF])
                inv_col = sb(s2, "inv_col", [P, 2, 4])
            with ExitStack() as s2:
                mq_hi, mq_lo = sb(s2, "mq_hi", [P, 2, SEQ], F32R), sb(s2, "mq_lo", [P, 2, SEQ], F32R)
                prob = [sb(s2, f"prob{hf}", [P, 4, MEM]) for hf in range(2)]
                pT_hi = [sb(s2, f"pT_hi{hf}", [P, 2, HALF], F32R) for hf in range(2)]
                pT_lo = [sb(s2, f"pT_lo{hf}", [P, 2, HALF], F32R) for hf in range(2)]
                neg_max, row_sum, inv_sum = ([sb(s2, f"{n}{hf}", [P, 4]) for hf in range(2)]
                                             for n in ("neg_max", "row_sum", "inv_sum"))

        unit = ctx.enter_context(nc.psum_tensor("unit", [P, 2, SEQ], F32))
        aux = ctx.enter_context(nc.psum_tensor("aux", [P, 4, HALF], F32))

        w_loaded = [sem(f"w_loaded{s}") for s in range(2)]
        w_hi_done, w_split, chunk_started = sem("w_hi_done"), sem("w_split"), sem("chunk_started")
        one_ready = sem("one_ready")
        consts_loaded, consts_ready = sem("consts_loaded"), sem("consts_ready")
        x_loaded = [sem(f"x_loaded{k}") for k in range(KT)]
        x_hi_done, x_split = sem("x_hi_done"), sem("x_split")
        unit_ready = sem("unit_ready")
        unit_drained = [sem(f"unit_drained{s}") for s in range(2)]

        rope_loaded, rope_products, rotated, rot_hi, rot_split = (
            sem(n) for n in ("rope_loaded", "rope_products", "rotated", "rot_hi", "rot_split"))
        rv_hi_done = sem("rv_hi_done")
        rz_ready, rp_hi_done, diag_masked, diag_hi, diag_lo, rp_split = (
            sem(n) for n in ("rz_ready", "rp_hi_done", "diag_masked", "diag_hi", "diag_lo", "rp_split"))
        ro_copied, rs_hi_done, rs_split, norm_ready = (
            sem(n) for n in ("ro_copied", "rs_hi_done", "rs_split", "norm_ready"))
        r_mean_sq, r_var, r_std, r_rstd_ready, ret_centered, ret_whole, ret_normed, ret_gated = (
            sem(n) for n in ("r_mean_sq", "r_var", "r_std", "r_rstd_ready", "ret_centered", "ret_whole",
                             "ret_normed", "ret_gated"))
        ret_hi_done, ret_split = sem("ret_hi_done"), sem("ret_split")

        stick_consts, neg_loaded = sem("stick_consts"), sem("neg_loaded")
        gate_half_ready, gate_half_made = sem("gate_half_ready"), sem("gate_half_made")
        sqkv_hi, stick_scanned, w_ready, wt_ready, wt_hi, wt_split, sbo_ready, sbo_stored = (
            sem(n) for n in ("sqkv_hi", "stick_scanned", "w_ready", "wt_ready", "wt_hi", "wt_split",
                             "sbo_ready", "sbo_stored"))
        sbo_hi_done, sbo_split, branch_summed = sem("sbo_hi_done"), sem("sbo_split"), sem("branch_summed")

        mem_loaded, mem_hi_done, mem_split = sem("mem_loaded"), sem("mem_hi_done"), sem("mem_split")
        mkq_hi, s_ready, max_ready, neg_ready, exp_done, inv_ready, prob_ready = (
            sem(n) for n in ("mkq_hi", "s_ready", "max_ready", "neg_ready", "exp_done", "inv_ready", "prob_ready"))
        turn_ready, turn_hi, turn_split = sem("turn_ready"), sem("turn_hi"), sem("turn_split")

        silu_read, hid_hi, hid_lo = sem("silu_read"), sem("hid_hi"), sem("hid_lo")
        scaled_odd, y_ready, out_stored = sem("scaled_odd"), sem("y_ready"), sem("out_stored")

        class Norm:

            def __init__(self, tag):
                (self.a_hi, self.a_split, self.summed, self.first_half, self.added, self.last_summed, self.stat_hi,
                 self.stat_sq, self.sqr_hi, self.stat_split, self.sums_taken, self.mean_sq, self.var, self.std,
                 self.turned, self.inverted, self.rstd, self.rstd_copied, self.centered, self.scaled, self.affine, self.hi, self.done) = (
                    sem(f"{tag}_{n}") for n in (
                        "a_hi", "a_split", "summed", "first_half", "added", "last_summed", "stat_hi", "stat_sq",
                        "sqr_hi", "stat_split", "sums_taken", "mean_sq", "var", "std", "turned", "inverted", "rstd",
                        "rstd_copied", "centered", "scaled",
                        "affine", "hi", "done"))

        n1, n2, n3 = Norm("n1"), Norm("n2"), Norm("n3")

        block = ctx.enter_context(nc.Block())

        @block.sync
        def _(sp):
            def stream(source, first, chunk, count, width):
                with sp.Fori(0, count // 2) as i:
                    for s in range(2):
                        sp.wait_ge(w_split, i * 2 + (chunk + s - 1))
                        sp.dma_start(w_raw[:, s, 0:width],
                                     source[bass.ds(i * 2 + (first + s), 1)].rearrange("a p w -> p (a w)")
                                     ).then_inc(w_loaded[s], 16)

            sp.dma_start(w_raw[:, 0, :], stream8[0]).then_inc(w_loaded[0], 16)
            sp.dma_start(w_raw[:, 1, :], stream8[1]).then_inc(w_loaded[1], 16)
            sp.dma_start(ident[:], consts[0]).then_inc(consts_loaded, 16)
            sp.dma_start(causal[:], consts[1]).then_inc(consts_loaded, 16)
            sp.dma_start(par[:], params).then_inc(consts_loaded, 16)
            stream(stream8, 2, 2, 140, 8 * P)
            stream(stream7, 0, 142, 8, 7 * P)
            stream(stream8, 142, 150, 14, 8 * P)
            stream(stream7, 8, 164, 8, 7 * P)
            for q in range(2 * KT):
                hf, k = divmod(q, KT)
                sp.wait_ge(y_ready, q + 1)
                sp.dma_start(outT[k * P:(k + 1) * P, half(hf)], y_out[:, k, half(hf)]).then_inc(out_stored, 16)
            sp.wait_ge(out_stored, 16 * 2 * KT)

        @block.gpsimd
        def _(pool):
            def split(chunk, count, width):
                with pool.Fori(0, count // 2) as i:
                    for s in range(2):
                        c = i * 2 + (chunk + s)
                        pool.wait_ge(w_loaded[s], i * 16 + (chunk // 2 + 1) * 16)
                        pool.wait_ge(chunk_started, c)
                        pool.tensor_tensor(w_hi[s][:, 0:width], w_raw[:, s, 0:width], one[:].to_broadcast([P, width]),
                                           ALU.mult).then_inc(w_hi_done, 1)
                        pool.wait_ge(w_hi_done, c + 1)
                        pool.tensor_tensor(w_lo[s][:, 0:width], w_raw[:, s, 0:width], f32(w_hi[s][:, 0:width]),
                                           ALU.subtract).then_inc(w_split, 1)

            pool.memset(one[:], 1.0).then_inc(one_ready, 1)
            pool.wait_ge(one_ready, 1)
            for s in range(2):
                pool.wait_ge(w_loaded[s], 16)
                pool.tensor_tensor(w_hi[s][:], w_raw[:, s, :], one[:].to_broadcast([P, D]), ALU.mult
                                   ).then_inc(w_hi_done, 1)
                pool.wait_ge(w_hi_done, s + 1)
                pool.tensor_tensor(w_lo[s][:], w_raw[:, s, :], f32(w_hi[s][:]), ALU.subtract).then_inc(w_split, 1)

            def normed_lo(m, qs):
                for q in qs:
                    hf, k = divmod(q, KT)
                    pool.wait_ge(m.hi, q + 1)
                    pool.tensor_tensor(x_lo[:, k, half(hf)], ln_x[:, q % 4, :], f32(x_hi[:, k, half(hf)]), ALU.subtract
                                       ).then_inc(m.done, 1)

            split(2, CH_MEM, 8 * P)
            normed_lo(n1, range(2 * KT))
            split(CH_MEM + 4, CH_FFN + 2 - CH_MEM - 4, 8 * P)
            normed_lo(n2, range(2 * KT))
            split(CH_FFN + 2, 142 - CH_FFN - 2, 8 * P)
            split(142, 8, 7 * P)
            split(150, 14, 8 * P)
            split(164, 8, 7 * P)
            for q in range(1, 2 * KT, 2):
                hf = q // KT
                pool.wait_ge(n3.centered, q + 1)
                pool.wait_ge(n3.rstd_copied, hf + 1)
                pool.tensor_tensor(ln_t[:, q % 4, :], ln_t[:, q % 4, :], ln_rstd[:, half(hf)], ALU.mult
                                   ).then_inc(scaled_odd, 1)

        @block.tensor
        def _(pe):
            def triple(out, l_hi, l_lo, r_hi, r_lo, start, stop):
                pe.matmul(out, l_hi, r_lo, start=start, stop=False, skip_group_check=True)
                pe.matmul(out, l_hi, r_hi, start=False, stop=False, skip_group_check=True)
                return pe.matmul(out, l_lo, r_hi, start=False, stop=stop, skip_group_check=True)

            def free_unit(first, per, i, k):
                pe.wait_ge(unit_drained[k % 2], i * (per // 2) + (first // 2 + k // 2))
                return unit[:, k % 2, :]

            def project(chunk, s, outs, hi, lo, kts=KT, w0=0, arrived=None, before=0, mid=None, begins=True):
                pe.wait_ge(w_split, chunk + 1)
                last = None
                for k in range(kts):
                    if arrived:
                        pe.wait_ge(arrived, before + k + 1)
                    if mid and k == kts // 2:
                        mid()
                    wk = slice((w0 + k) * P, (w0 + k + 1) * P)
                    for j, (out, cols) in enumerate(outs):
                        first = k == 0
                        x = pe.matmul(out, w_hi[s][:, wk], lo[:, k, cols], start=first, stop=False,
                                      skip_group_check=True)
                        if k == 0 and j == 0 and w0 == 0 and begins:
                            x.then_inc(chunk_started, 1)
                        pe.matmul(out, w_hi[s][:, wk], hi[:, k, cols], start=False, stop=False,
                                  skip_group_check=True)
                        last = pe.matmul(out, w_lo[s][:, wk], hi[:, k, cols], start=False, stop=(k == kts - 1),
                                         skip_group_check=True)
                return last

            def halves(u):
                return [(u[:, h * HALF:(h + 1) * HALF], slice(h * HALF, (h + 1) * HALF)) for h in range(2)]

            with pe.Fori(0, RET_HEADS) as h:
                def proj(k, c, arrived=None):
                    u = free_unit(U_RET, RU, h, k)
                    project(h * 6 + c, c % 2, halves(u), x_hi, x_lo, arrived=arrived).then_inc(unit_ready, 1)

                def turn_v(k, source):
                    u = free_unit(U_RET, RU, h, k)
                    for b in range(QT):
                        t = pe.transpose(u[:, b * P:(b + 1) * P], source[:, b * P:(b + 1) * P], ident[:])
                    t.then_inc(unit_ready, 1)

                pe.wait_ge(consts_ready, 2)
                proj(0, 0, x_split)
                proj(1, 1)
                proj(2, 2)
                proj(3, 3)
                pe.wait_ge(unit_drained[0], h * 5 + 2)
                turn_v(4, tmp_a)
                pe.wait_ge(unit_drained[1], h * 5 + 2)
                turn_v(5, tmp_b)

                def score(t):
                    hf, kb, q0, n = ret_tile(t)
                    z = aux[:, t % 2, 0:n]
                    triple(z, rk_hi[:, kb * P:(kb + 1) * P], rk_lo[:, kb * P:(kb + 1) * P],
                           rq_hi[:, q0:q0 + n], rq_lo[:, q0:q0 + n], True, True).then_inc(rz_ready, 1)

                def values(t):
                    hf, kb, q0, n = ret_tile(t)
                    u = unit[:, (7 + hf) % 2, :]
                    if kb == 0:
                        free_unit(U_RET, RU, h, 7 + hf)
                    pe.wait_ge(rp_split, h * 12 + (t + 1))
                    last_kb = 3 if hf == 0 else 7
                    for e in range(2):
                        c0 = e * HALF + q0 - hf * HALF
                        x = triple(u[:, c0:c0 + n], rv_hi[:, kb, e * P:(e + 1) * P], rv_lo[:, kb, e * P:(e + 1) * P],
                                   rp_hi[:, t % 2, 0:n], rp_lo[:, t % 2, 0:n], kb == 0, kb == last_kb)
                    if kb == last_kb:
                        x.then_inc(unit_ready, 1)

                def norm_sums(hf):
                    pe.wait_ge(rs_split, h * 2 + (hf + 1))
                    pe.wait_ge(ret_centered, h * 2 + hf)
                    for b, (hi, lo) in enumerate(((ro_hi, ro_lo), (rs_hi, rs_lo))):
                        for e in range(2):
                            pe.matmul(aux[:, 2 + b, :], ret_ones[:], lo[:, e, :], start=(e == 0), stop=False,
                                      skip_group_check=True)
                            x = pe.matmul(aux[:, 2 + b, :], ret_ones[:], hi[:, e, :], start=False, stop=(e == 1),
                                          skip_group_check=True)
                    x.then_inc(norm_ready, 1)

                pe.wait_ge(rot_split, h * 2 + 2)
                score(0)
                for t in range(1, 12):
                    score(t)
                    if t == 1:
                        proj(6, 4)
                    values(t - 1)
                    if t == 10:
                        norm_sums(0)
                values(11)
                proj(9, 5)
                norm_sums(1)

            with pe.Fori(0, KT) as n:
                u = free_unit(U_GRET, 2, n, 0)
                project(n * 2 + CH_GRET, 0, halves(u), x_hi, x_lo).then_inc(unit_ready, 1)
                u = free_unit(U_GRET, 2, n, 1)
                project(n * 2 + (CH_GRET + 1), 1, halves(u), ret_hi, ret_lo, arrived=ret_split).then_inc(unit_ready, 1)

            with pe.Fori(0, SB_PAIRS // 2) as i:
                for pp in range(2):
                    def sbu(k):
                        return free_unit(U_SB + SU * pp, 2 * SU, i, k)

                    def drained(k):
                        pe.wait_ge(unit_drained[k % 2], i * SU + (U_SB + SU * pp) // 2 + (k // 2 + 1))

                    def count(per_pair, k):
                        return i * (2 * per_pair) + (per_pair * pp + k)

                    for k in range(3):
                        c = 4 * pp + k
                        u = sbu(k)
                        project(i * 8 + (CH_SB + c), c % 2, halves(u), x_hi, x_lo).then_inc(unit_ready, 1)
                    drained(0)
                    drained(1)
                    pe.wait_ge(stick_consts, 4)

                    def logits(s):
                        qt, hd, n = stick_step(s)
                        q, rows = slice(qt * P, (qt + 1) * P), slice(hd * SB_DIM, (hd + 1) * SB_DIM)
                        u = sbu(4 + s if s else 3)
                        for c0 in range(0, n, HALF):
                            c1 = min(n, c0 + HALF)
                            triple(u[:, c0:c1], sq_hi[rows, q], sq_lo[rows, q], sk_hi[rows, c0:c1], sk_lo[rows, c0:c1],
                                   True, False)
                        pe.matmul(u[:, n - P:n], ident_r[:], neg_r[:], start=False, stop=True,
                                  skip_group_check=True).then_inc(unit_ready, 1)

                    def turn_w(s):
                        qt, hd, n = stick_step(s)
                        pe.wait_ge(w_ready, count(16, s + 1))
                        pe.wait_ge(wt_split, count(16, s))
                        for b in range(qt + 1):
                            x = pe.transpose(aux[:, b // 4, b % 4 * P:(b % 4 + 1) * P],
                                             beta[:, s % 2, b * P:(b + 1) * P], ident[:])
                        x.then_inc(wt_ready, 1)

                    def values(s):
                        qt, hd, n = stick_step(s)
                        pe.wait_ge(wt_split, count(16, s + 1))
                        if qt == 0 and hd == 0:
                            drained(4)
                        if qt and qt % 2 == 0 and hd == 0:
                            pe.wait_ge(sbo_stored, count(8, qt))
                        c0 = hd * 2 * P + qt % 2 * P
                        out = aux[0:SB_DIM, 2, c0:c0 + P]
                        for b in range(qt + 1):
                            v = slice(hd * SB_DIM, (hd + 1) * SB_DIM)
                            x = triple(out, sv_hi[:, b, v], sv_lo[:, b, v], wT_hi[:, s % 2, b * P:(b + 1) * P],
                                       wT_lo[:, s % 2, b * P:(b + 1) * P], b == 0, b == qt)
                        if qt % 2 and hd:
                            x.then_inc(sbo_ready, 1)

                    def early_gate_piece(hf, k):
                        c, wk, cols = 4 * pp + 3, slice(k * P, (k + 1) * P), slice(hf * HALF, (hf + 1) * HALF)
                        if k == 0:
                            pe.wait_ge(gate_half_made, count(2, hf))
                            if hf == 0:
                                pe.wait_ge(w_split, i * 8 + (CH_SB + c + 1))
                        x = pe.matmul(aux[:, 3, :], w_hi[1][:, wk], x_lo[:, k, cols], start=(k == 0), stop=False,
                                      skip_group_check=True)
                        if k == 0 and hf == 0:
                            x.then_inc(chunk_started, 1)
                        pe.matmul(aux[:, 3, :], w_hi[1][:, wk], x_hi[:, k, cols], start=False, stop=False,
                                  skip_group_check=True)
                        x = pe.matmul(aux[:, 3, :], w_lo[1][:, wk], x_hi[:, k, cols], start=False, stop=(k == KT - 1),
                                      skip_group_check=True)
                        if k == KT - 1:
                            x.then_inc(gate_half_ready, 1)

                    for s in range(19):
                        if 2 <= s <= 17:
                            turn_w(s - 2)
                        if s < 16:
                            logits(s)
                        if s == 0:
                            drained(2)
                            u = sbu(4)
                            for b in range(QT):
                                t = pe.transpose(u[:, b * P:(b + 1) * P], sv_T[:, b * P:(b + 1) * P], ident[:])
                            t.then_inc(unit_ready, 1)
                        if s >= 3:
                            values(s - 3)
                        for hf, k in gate_pieces(s):
                            early_gate_piece(hf, k)

            with pe.Fori(0, 2) as i:
                for c in range(2):
                    u = free_unit(U_GSB, GU, i, c)
                    project(i * 4 + (CH_GSB + c), c, halves(u), x_hi, x_lo).then_inc(unit_ready, 1)
                for c in range(2):
                    for j in range(2):
                        u = free_unit(U_GSB, GU, i, 2 + 2 * c + j)
                        project(i * 4 + (CH_GSB + 2 + c), c, halves(u), sbo_hi, sbo_lo, kts=4, w0=4 * j,
                                arrived=sbo_split).then_inc(unit_ready, 1)

            def spread_rstd(m, hf, counts_chunk=False):
                pe.wait_ge(m.std, hf + 1)
                for b in range(4):
                    x = pe.transpose(aux[:, 2 + hf, b * P:(b + 1) * P],
                                     ln_mean2[:, hf * HALF + b * P:hf * HALF + (b + 1) * P], ident[:])
                    if b == 0 and counts_chunk:
                        x.then_inc(chunk_started, 1)
                x.then_inc(m.turned, 1)
                pe.wait_ge(m.inverted, hf + 1)
                for b in range(4):
                    x = pe.transpose(aux[:, 2 + hf, b * P:(b + 1) * P],
                                     inv_col[:, hf, b:b + 1].to_broadcast([P, P]), ident[:])
                x.then_inc(m.rstd, 1)

            def residual(m, chunk, first, kts, arrived, stats, next_chunk=False, before=0):

                def sums(count, hf, n0, n7, counts_chunk=False):
                    pe.wait_ge(m.stat_split, count)
                    for b, (hi, lo) in enumerate(((st_hi, st_lo), (sqr_hi, sqr_lo))):
                        x = pe.matmul(aux[:, 2 * b + hf, :], ln_ones[:], lo[hf][:], start=n0, stop=False,
                                      skip_group_check=True)
                        if counts_chunk and b == 0:
                            x.then_inc(chunk_started, 1)
                        x = pe.matmul(aux[:, 2 * b + hf, :], ln_ones[:], hi[hf][:], start=False, stop=n7,
                                      skip_group_check=True)
                    x.then_inc(m.sums_taken, 1)

                def block(i, j, is_first=False):
                    mid = None
                    if stats and (j or not is_first):
                        def mid():
                            sums(i * 4 + (1 if j else -1), 0, is_first, False)
                    u = free_unit(first, 2, i, j)
                    last = project(i * 2 + (chunk + j), j, halves(u), a_hi, a_lo, kts=kts, arrived=arrived, before=before,
                                   mid=mid)
                    last.then_inc(unit_ready, 1)
                    if mid:
                        sums(i * 4 + (2 if j else 0), 1, is_first, False)

                if not stats:
                    with pe.Fori(0, 4) as i:
                        for j in range(2):
                            block(i, j)
                    return
                for j in range(2):
                    block(0, j, True)
                with pe.Fori(1, 3) as i:
                    for j in range(2):
                        block(i, j)
                block(3, 0)
                halves_u = halves(free_unit(first, 2, 3, 1))
                project(chunk + 7, 1, halves_u[0:1], a_hi, a_lo, kts=kts).then_inc(m.first_half, 1)
                sums(13, 0, False, False)
                project(chunk + 7, 1, halves_u[1:2], a_hi, a_lo, kts=kts, mid=lambda: sums(14, 1, False, False),
                        begins=False).then_inc(unit_ready, 1)
                sums(15, 0, False, True, counts_chunk=next_chunk)
                spread_rstd(m, 0)
                sums(16, 1, False, True)

            residual(n1, CH_MIX, U_MIX, KT, n1.a_split, True, next_chunk=True)

            def mem_chunk(h, c, u, j, begins=True):
                return project(h * 6 + (CH_MEM + c), c % 2, [(u[:, j * HALF:j * HALF + MEM], slice(0, MEM))],
                               mem_hi, mem_lo, begins=begins)

            def mem_queries(h, c, u):
                project(h * 6 + (CH_MEM + c), c % 2, halves(u), x_hi, x_lo).then_inc(unit_ready, 1)

            def as_normed(m, chunk, first, mid=None):
                slots = [(first + c) % 2 for c in range(2)]
                for c in range(2):
                    pe.wait_ge(unit_drained[slots[c]], (first + c) // 2)
                    pe.wait_ge(w_split, chunk + c + 1)
                for k in range(KT):
                    pe.wait_ge(m.done, k + 1)
                    wk = slice(k * P, (k + 1) * P)
                    for c in range(2):
                        out, start, stop = unit[:, slots[c], half(0)], k == 0, k == KT - 1
                        pe.matmul(out, w_hi[c][:, wk], x_lo[:, k, half(0)], start=start, stop=False,
                                  skip_group_check=True)
                        pe.matmul(out, w_hi[c][:, wk], x_hi[:, k, half(0)], start=False, stop=False,
                                  skip_group_check=True)
                        pe.matmul(out, w_lo[c][:, wk], x_hi[:, k, half(0)], start=False, stop=stop,
                                  skip_group_check=True)
                    if mid and k == 3:
                        mid()
                for c in range(2):
                    project(chunk + c, c, [(unit[:, slots[c], half(1)], half(1))], x_hi, x_lo,
                            arrived=m.done if c == 0 else None, before=KT, begins=c == 1).then_inc(unit_ready, 1)

            def turn_mem_v():
                for dt in range(2):
                    for mt in range(2):
                        t = pe.transpose(aux[:, mt, dt * P:(dt + 1) * P], mv_T[:, dt, mt * P:(mt + 1) * P], ident[:])
                t.then_inc(turn_ready, 1)

            def mem_head(h, more):
                base = U_MEM + 4

                def scores(hf):
                    for tt in range(4):
                        tok = slice((hf * 4 + tt) * P, (hf * 4 + tt + 1) * P)
                        out = aux[:, 2 * hf + tt // 2, tt % 2 * MEM:(tt % 2 + 1) * MEM]
                        for dt in range(2):
                            x = triple(out, mq_hi[:, dt, tok], mq_lo[:, dt, tok], mk_hi[:, dt, :], mk_lo[:, dt, :],
                                       dt == 0, dt == 1)
                    x.then_inc(s_ready, 1)

                def turn_p(hf):
                    pe.wait_ge(prob_ready, h * 2 + (hf + 1))
                    for tt in range(4):
                        for mt in range(2):
                            x = pe.transpose(aux[:, 2 * hf + mt, tt * P:(tt + 1) * P],
                                             prob[hf][:, tt, mt * P:(mt + 1) * P], ident[:])
                    x.then_inc(turn_ready, 1)

                def values(hf, k):
                    u = free_unit(base, XU, h, k)
                    pe.wait_ge(turn_split, h * 3 + (hf + 2))
                    for dt in range(2):
                        for mt in range(2):
                            x = triple(u[:, dt * HALF:(dt + 1) * HALF], mv_hi[:, mt, dt * P:(dt + 1) * P],
                                       mv_lo[:, mt, dt * P:(dt + 1) * P], pT_hi[hf][:, mt, :], pT_lo[hf][:, mt, :],
                                       mt == 0, mt == 1)
                    x.then_inc(unit_ready, 1)

                if more:
                    u = free_unit(base, XU, h, 0)
                    mem_chunk(h + 1, 0, u, 0)
                pe.wait_ge(unit_drained[0], h * 3 + (U_MEM // 2 + 2))
                pe.wait_ge(unit_drained[1], h * 3 + (U_MEM // 2 + 2))
                pe.wait_ge(turn_split, h * 3 + 1)
                scores(0)
                scores(1)
                if more:
                    mem_chunk(h + 1, 1, u, 1).then_inc(unit_ready, 1)
                turn_p(0)
                if more:
                    u = free_unit(base, XU, h, 2)
                    mem_chunk(h + 1, 2, u, 0)
                turn_p(1)
                values(0, 1 if more else 0)
                if more:
                    mem_chunk(h + 1, 3, u, 1).then_inc(unit_ready, 1)
                values(1, 3 if more else 1)
                if more:
                    mem_queries(h + 1, 4, free_unit(base, XU, h, 4))
                    turn_mem_v()
                    mem_queries(h + 1, 5, free_unit(base, XU, h, 5))

            pe.wait_ge(mem_split, KT)
            u = free_unit(U_MEM, XU, 0, 0)
            mem_chunk(0, 0, u, 0, begins=False)
            mem_chunk(0, 1, u, 1).then_inc(unit_ready, 1)
            spread_rstd(n1, 1, counts_chunk=True)
            as_normed(n1, CH_MEM + 2, U_MEM + 1)
            u = free_unit(U_MEM, XU, 0, 3)
            mem_chunk(0, 4, u, 0)
            mem_chunk(0, 5, u, 1).then_inc(unit_ready, 1)
            pe.wait_ge(unit_drained[1], U_MEM // 2 + 2)
            turn_mem_v()
            with pe.Fori(0, MEM_HEADS - 1) as h:
                mem_head(h, True)
            mem_head(MEM_HEADS - 1, False)

            residual(n2, CH_MO, U_MO, KT, n2.a_split, True, next_chunk=True)

            chunk, first, tiles = CH_FFN, U_FFN, 0
            for part, kts in enumerate(FFN_PARTS):
                if part == 0:
                    as_normed(n2, chunk, first, mid=lambda: spread_rstd(n2, 1))
                with pe.Fori(0 if part else 1, kts) as j:
                    for g in range(2):
                        u = free_unit(first, 2, j, g)
                        project(j * 2 + (chunk + g), g, halves(u), x_hi, x_lo).then_inc(unit_ready, 1)
                chunk, first, tiles = chunk + 2 * kts, first + 2 * kts, tiles + kts
                residual(n3, chunk, first, kts, hid_lo, part == 2, before=tiles - kts)
                chunk, first = chunk + 8, first + 8
            spread_rstd(n3, 1)

        @block.scalar
        def _(act):
            for k in range(KT):
                act.dma_start(acc[:, k, :], xT[k * P:(k + 1) * P, :]).then_inc(x_loaded[k], 16)
            for k in range(KT):
                act.wait_ge(x_loaded[k], 16)
                act.activation(x_hi[:, k, :], acc[:, k, :], ACT.Copy).then_inc(x_hi_done, 1)

            with act.Fori(0, RET_HEADS) as h:
                def ready(k):
                    act.wait_ge(unit_ready, h * RU + (U_RET + k + 1))

                for w in range(2):
                    act.wait_ge(rotated, h * 2 + w)
                    act.dma_start(rope_sb[:].rearrange("p a t -> p (a t)"),
                                  rope[bass.ds(h * 2 + w, 1)].rearrange("a p t -> p (a t)")).then_inc(rope_loaded, 16)
                    act.wait_ge(rotated, h * 2 + (w + 1))
                    act.activation((rq_hi, rk_hi)[w][:], tmp_a[:], ACT.Copy).then_inc(rot_hi, 1)
                ready(2)
                act.wait_ge(rot_split, h * 2 + 2)
                act.activation(tmp_a[:], unit[:, 0, :], ACT.Copy).then_inc(unit_drained[0], 1)
                ready(3)
                act.activation(tmp_b[:], unit[:, 1, :], ACT.Copy).then_inc(unit_drained[1], 1)
                ready(4)
                act.activation(rv_hi[:, :, 0:P], unit[:, 0, :].rearrange("p (b d) -> p b d", d=P), ACT.Copy
                               ).then_inc(rv_hi_done, 1)
                ready(5)
                act.activation(rv_hi[:, :, P:2 * P], unit[:, 1, :].rearrange("p (b d) -> p b d", d=P), ACT.Copy
                               ).then_inc(rv_hi_done, 1)

                def copy_output(hf):
                    ready(7 + hf)
                    act.wait_ge(ret_centered, h * 2 + hf)
                    act.wait_ge(norm_ready, h * 2 + hf)
                    act.activation(ro_hi[:].rearrange("p e t -> p (e t)"), unit[:, (7 + hf) % 2, :], ACT.Copy
                                   ).then_inc(ro_copied, 1)

                def square_output(hf):
                    act.activation(tmp_b[:], unit[:, (7 + hf) % 2, :], ACT.Square).then_inc(ro_copied, 1)

                def mean_square(hf):
                    act.wait_ge(norm_ready, h * 2 + (hf + 1))
                    act.wait_ge(r_rstd_ready, h * 2 + hf)
                    act.activation(r_mean2[:], aux[:, 2, :], ACT.Square).then_inc(r_mean_sq, 1)

                def root(hf):
                    act.wait_ge(r_var, h * 2 + (hf + 1))
                    act.activation(r_mean2[:], r_rstd[:], ACT.Sqrt).then_inc(r_std, 1)

                diags = 0
                for t in range(12):
                    if t == 2:
                        ready(6)
                        act.wait_ge(ret_gated, h * 2)
                        act.activation(silu_g[:, 0, :], unit[:, 0, :], ACT.Silu).then_inc(unit_drained[0], 1)
                    hf, kb, q0, n = ret_tile(t)
                    a = P if q0 == kb * P else 0
                    if a:
                        diags += 1
                        if n > a:
                            act.wait_ge(diag_masked, h * 8 + diags)
                    if n > a:
                        act.wait_ge(rz_ready, h * 12 + (t + 1))
                        act.activation(rp_hi[:, t % 2, a:n], aux[:, t % 2, a:n], ACT.Copy).then_inc(rp_hi_done, 1)
                    if t == 4:
                        copy_output(0)
                    if t == 5:
                        square_output(0)
                mean_square(0)
                copy_output(1)
                square_output(1)
                root(0)
                ready(9)
                act.activation(silu_g[:, 1, :], unit[:, 1, :], ACT.Silu).then_inc(unit_drained[1], 1)
                mean_square(1)
                root(1)

            for k in range(KT):
                act.wait_ge(ret_gated, max(k + 1, 2 * RET_HEADS - 2))
                act.activation(ret_hi[:, k, :], acc[:, k, :], ACT.Copy).then_inc(ret_hi_done, 1)
            with act.Fori(0, KT) as n:
                act.wait_ge(unit_ready, n * 2 + (U_GRET + 1))
                act.wait_ge(unit_drained[1], n + U_GRET // 2)
                act.activation(gate_ret[:], unit[:, 0, :], ACT.Sigmoid, bias=par[:, bass.ds(n + 56, 1)]
                               ).then_inc(unit_drained[0], 1)

            act.wait_ge(unit_drained[1], U_SB // 2)
            act.dma_start(neg[:], consts[2]).then_inc(neg_loaded, 16)
            with act.Fori(0, SB_PAIRS // 2) as i:
                for pp in range(2):
                    def ready(k):
                        act.wait_ge(unit_ready, i * (2 * SU) + (U_SB + SU * pp + k + 1))

                    def count(per_pair, k):
                        return i * (2 * per_pair) + (per_pair * pp + k)

                    ready(0)
                    act.activation(sq_hi[:], unit[:, 0, :], ACT.Copy, scale=SB_DIM ** -0.5).then_inc(sqkv_hi, 1)
                    ready(1)
                    act.activation(sk_hi[:], unit[:, 1, :], ACT.Copy).then_inc(sqkv_hi, 1)
                    ready(2)
                    if pp == 0:
                        act.wait_ge(stick_consts, 4)
                    act.activation(sv_T, unit[:, 0, :], ACT.Copy).then_inc(unit_drained[0], 1)

                    def split_w(s):
                        qt, hd, n = stick_step(s)
                        act.wait_ge(wt_ready, count(16, s + 1))
                        act.activation(wT_hi[:, s % 2, 0:n], aux[:, 0:2, :].rearrange("p b t -> p (b t)")[:, 0:n],
                                       ACT.Copy).then_inc(wt_hi, 1)

                    def store(s):
                        qt, hd, n = stick_step(s)
                        two = qt // 2
                        act.wait_ge(sbo_ready, count(4, two + 1))
                        for hd in range(2):
                            act.activation(sb_out[hd * SB_DIM:(hd + 1) * SB_DIM, bass.ds(i * 2 + pp, 1),
                                                  two * 2 * P:(two + 1) * 2 * P].rearrange("p a t -> p (a t)"),
                                           aux[0:SB_DIM, 2, hd * 2 * P:(hd + 1) * 2 * P], ACT.Copy
                                           ).then_inc(sbo_stored, 1)

                    for s in range(19):
                        if 2 <= s <= 17:
                            split_w(s - 2)
                        if s < 16:
                            qt, hd, n = stick_step(s)
                            slot = s % 2 if s else 1
                            ready(4 + s if s else 3)
                            act.activation(beta[:, s % 2, 0:n], unit[:, slot, 0:n], ACT.Sigmoid)
                            act.wait_ge(w_ready, count(16, s))
                            act.activation(stick[:, SEQ - n:SEQ], unit[:, slot, 0:n], ACT.Sigmoid, scale=-1.0
                                           ).then_inc(unit_drained[slot], 1)
                        if s == 0:
                            ready(4)
                            act.activation(sv_hi[:].rearrange("p b d -> p (b d)"), unit[:, 0, :], ACT.Copy
                                           ).then_inc(sqkv_hi, 1)
                        if s >= 3 and (s - 3) % 4 == 3:
                            store(s - 3)
                        for hf, k in gate_pieces(s - 1):
                            if k == KT - 1:
                                act.wait_ge(gate_half_ready, count(2, hf + 1))
                                act.activation(early_gate[:, bass.ds(i * 2 + pp, 1), hf * HALF:(hf + 1) * HALF
                                                          ].rearrange("p a t -> p (a t)"), aux[:, 3, :], ACT.Sigmoid,
                                               bias=par[:, bass.ds(i * 4 + (50 + pp), 1)]).then_inc(gate_half_made, 1)

            for k in range(4):
                act.wait_ge(sbo_stored, 8 * SB_PAIRS)
                act.activation(sbo_hi[:, k, :], sb_out[:, k, :], ACT.Copy).then_inc(sbo_hi_done, 1)
            with act.Fori(0, 2) as i:
                for j in range(2):
                    act.wait_ge(unit_ready, i * GU + (U_GSB + j + 1))
                    act.wait_ge(branch_summed, i * 4)
                    act.activation(gate_sb[:, j, :], unit[:, j, :], ACT.Sigmoid,
                                   bias=par[:, bass.ds(i * 4 + (48 + j), 1)]).then_inc(unit_drained[j], 1)

            def split_a(m, before, value):
                for k in range(KT):
                    act.wait_ge(before, value(k))
                    act.activation(a_hi[:, k, :], acc[:, k, :], ACT.Copy).then_inc(m.a_hi, 1)

            def root(m, hf):
                act.wait_ge(m.var, hf + 1)
                act.activation(ln_mean2[:, half(hf)], ln_rstd[:, half(hf)], ACT.Sqrt).then_inc(m.std, 1)

            def statistics(m, first, by_drain, between=None):
                def half_block(i, j, hf):
                    r = acc[:, bass.ds(i * 2 + j, 1), half(hf)].rearrange("p a t -> p (a t)") if not isinstance(i, int) else \
                        acc[:, 6 + j, half(hf)]
                    act.wait_ge(m.sums_taken, i * 4 + 2 * j)
                    act.activation(st_hi[hf][:], r, ACT.Copy).then_inc(m.stat_hi, 1)
                    act.activation(sqr[hf][:], r, ACT.Square).then_inc(m.stat_sq, 1)

                def block(i, j):
                    if by_drain:
                        act.wait_ge(unit_drained[j], i + (first // 2 + 1))
                    else:
                        act.wait_ge(m.summed, i * 2 + (j + 1))
                    for hf in range(2):
                        half_block(i, j, hf)

                def mean_square(hf):
                    act.wait_ge(m.sums_taken, 2 * KT - 1 + hf)
                    act.activation(ln_mean2[:, half(hf)], aux[:, hf, :], ACT.Square).then_inc(m.mean_sq, 1)

                with act.Fori(0, KT // 2 - 1) as i:
                    for j in range(2):
                        block(i, j)
                block(3, 0)
                act.wait_ge(m.last_summed, 1)
                half_block(3, 1, 0)
                if between:
                    between[0]()
                mean_square(0)
                if by_drain:
                    act.wait_ge(unit_drained[1], first // 2 + 4)
                else:
                    act.wait_ge(m.last_summed, 2)
                half_block(3, 1, 1)
                root(m, 0)
                if between:
                    between[1]()
                mean_square(1)

            def layer_norm(m, which, between=None):
                for q in range(2 * KT):
                    hf, k = divmod(q, KT)
                    if between and q in between:
                        between[q]()
                    if q == 2:
                        root(m, 1)
                    g, b = par[:, 16 * which + k:16 * which + k + 1], par[:, 16 * which + 8 + k:16 * which + 9 + k]
                    if which == 2:
                        if q % 2:
                            act.wait_ge(scaled_odd, q // 2 + 1)
                        else:
                            act.wait_ge(m.scaled, q // 2 + 1)
                        act.activation(y_out[:, k, half(hf)], ln_t[:, q % 4, :], ACT.Identity, scale=g, bias=b
                                       ).then_inc(y_ready, 1)
                        continue
                    act.wait_ge(m.scaled, q + 1)
                    if q >= 4:
                        act.wait_ge(m.done, q - 3)
                    act.activation(ln_x[:, q % 4, :], ln_t[:, q % 4, :], ACT.Identity, scale=g, bias=b
                                   ).then_inc(m.affine, 1)
                    act.wait_ge(m.affine, q + 1)
                    act.activation(x_hi[:, k, half(hf)], ln_x[:, q % 4, :], ACT.Copy).then_inc(m.hi, 1)

            split_a(n1, branch_summed, lambda k: k + 1)
            def load_memory():
                act.wait_ge(unit_ready, U_MIX + KT)
                act.dma_start(mem_raw[:], memT.rearrange("(a p) t -> p a t", p=P)).then_inc(mem_loaded, 16)

            def split_memory():
                act.wait_ge(mem_loaded, 16)
                for k in range(0, KT, 4):
                    act.activation(mem_hi[:, k:k + 4, :], mem_raw[:, k:k + 4, :], ACT.Copy).then_inc(mem_hi_done, 4)

            statistics(n1, U_MIX, False, (load_memory, split_memory))
            def mem_unit(s):
                return unit[:, s, :].rearrange("p (a t) -> p a t", a=2)[:, :, 0:MEM]

            def keys(h, k):
                act.wait_ge(unit_ready, h * XU + k)
                act.activation(mk_hi[:], mem_unit(0), ACT.Copy, scale=MEM_DIM ** -0.5).then_inc(mkq_hi, 1)

            def mem_values(h, k, s):
                act.wait_ge(unit_ready, h * XU + k)
                act.activation(mv_T[:], mem_unit(s), ACT.Copy).then_inc(unit_drained[s], 1)

            def queries_and_v(h, k):
                act.wait_ge(unit_ready, h * XU + k)
                act.activation(mq_hi[:, 0, :], unit[:, 0, :], ACT.Copy).then_inc(mkq_hi, 1)
                act.wait_ge(turn_ready, h * 3 + 4)
                act.activation(mv_hi[:], aux[:, 0:2, 0:MEM_DIM], ACT.Copy).then_inc(turn_hi, 1)
                act.wait_ge(unit_ready, h * XU + (k + 1))
                act.activation(mq_hi[:, 1, :], unit[:, 1, :], ACT.Copy).then_inc(mkq_hi, 1)

            def mem_head(h, more):
                base = U_MEM + 5

                def exponent(hf):
                    act.wait_ge(neg_ready, h * 2 + (hf + 1))
                    for tt in range(4):
                        x = act.activation(prob[hf][:, tt, :], aux[:, 2 * hf + tt // 2, tt % 2 * MEM:(tt % 2 + 1) * MEM],
                                           ACT.Exp, bias=neg_max[hf][:, tt:tt + 1],
                                           accum_out=row_sum[hf][:, tt:tt + 1])
                    x.then_inc(exp_done, 1)

                def split_p(hf):
                    act.wait_ge(turn_ready, h * 3 + (hf + 2))
                    act.activation(pT_hi[hf][:], aux[:, 2 * hf:2 * hf + 2, :], ACT.Copy).then_inc(turn_hi, 1)

                def store(hf, k):
                    act.wait_ge(unit_ready, h * XU + (base + k))
                    r = acc[:, bass.ds(h * 2, 2), hf * HALF:(hf + 1) * HALF] if more else \
                        acc[:, 2 * h:2 * h + 2, hf * HALF:(hf + 1) * HALF]
                    act.activation(r, unit[:, k % 2, :].rearrange("p (a t) -> p a t", a=2), ACT.Copy
                                   ).then_inc(unit_drained[k % 2], 1)

                exponent(0)
                exponent(1)
                if more:
                    keys(h, base)
                split_p(0)
                split_p(1)
                store(0, 1 if more else 0)
                if more:
                    mem_values(h, base + 2, 0)
                store(1, 3 if more else 1)
                if more:
                    queries_and_v(h, base + 4)

            layer_norm(n1, 0, {6: lambda: keys(0, U_MEM + 1)})
            for k in range(2):
                act.wait_ge(unit_ready, U_MEM + k + 2)
                act.activation(mq_hi[:, k, :], unit[:, 1 - k, :], ACT.Copy).then_inc(mkq_hi, 1)
            mem_values(0, U_MEM + 4, 1)
            act.wait_ge(turn_ready, 1)
            act.activation(mv_hi[:], aux[:, 0:2, 0:MEM_DIM], ACT.Copy).then_inc(turn_hi, 1)
            with act.Fori(0, MEM_HEADS - 1) as h:
                mem_head(h, True)
            mem_head(MEM_HEADS - 1, False)

            split_a(n2, unit_drained[1], lambda k: U_MO // 2)
            statistics(n2, U_MO, False)
            layer_norm(n2, 1)

            first, tiles = U_FFN, 0
            for part, kts in enumerate(FFN_PARTS):
                with act.Fori(0, kts) as j:
                    act.wait_ge(unit_ready, j * 2 + (first + 1))
                    act.activation(silu_h[:], unit[:, 0, :], ACT.Silu).then_inc(unit_drained[0], 1)
                    act.wait_ge(unit_drained[1], j + (first // 2 + 1))
                    act.activation(a_hi[:, bass.ds(j, 1), :].rearrange("p a t -> p (a t)"), hidden[:], ACT.Copy
                                   ).then_inc(hid_hi, 1)
                first, tiles = first + 2 * kts + 8, tiles + kts
            statistics(n3, first - 8, True)
            layer_norm(n3, 2)

        @block.vector
        def _(dve):
            dve.memset(f32(ret_ones[:]), 1.0 / RET_V).then_inc(consts_ready, 1)
            dve.memset(f32(ln_ones[:]), 1.0 / D)
            for k in range(KT):
                dve.wait_ge(x_hi_done, k + 1)
                dve.tensor_tensor(x_lo[:, k, :], acc[:, k, :], f32(x_hi[:, k, :]), ALU.subtract).then_inc(x_split, 1)
                if k == 0:
                    dve.memset(diag[:], 0.0).then_inc(consts_ready, 1)
            dve.wait_ge(consts_loaded, 48)

            with dve.Fori(0, RET_HEADS) as h:
                def ready(k):
                    dve.wait_ge(unit_ready, h * RU + (U_RET + k + 1))

                for w in range(2):
                    u = unit[:, w, :]
                    ready(w)
                    dve.wait_ge(rope_loaded, h * 32 + 16 * (w + 1))
                    if w:
                        dve.wait_ge(rot_split, h * 2 + 1)
                    dve.tensor_tensor(tmp_a[:], u, rope_sb[:, 0, :], ALU.mult).then_inc(rope_products, 1)
                    dve.tensor_tensor(tmp_b[0:64, :], u[64:128, :], rope_sb[64:128, 1, :], ALU.mult
                                      ).then_inc(rope_products, 1)
                    dve.tensor_tensor(tmp_b[64:128, :], u[0:64, :], rope_sb[0:64, 1, :], ALU.mult
                                      ).then_inc(unit_drained[w], 1)
                    dve.wait_ge(rope_products, h * 4 + 2 * (w + 1))
                    dve.wait_ge(unit_drained[w], h * 5 + 1)
                    dve.tensor_tensor(tmp_a[:], tmp_a[:], tmp_b[:], ALU.add).then_inc(rotated, 1)
                    dve.wait_ge(rot_hi, h * 2 + (w + 1))
                    dve.tensor_tensor((rq_lo, rk_lo)[w][:], tmp_a[:], f32((rq_hi, rk_hi)[w][:]), ALU.subtract
                                      ).then_inc(rot_split, 1)
                for e in range(2):
                    dve.wait_ge(rv_hi_done, h * 2 + (e + 1))
                    dve.tensor_tensor(rv_lo[:, :, e * P:(e + 1) * P], unit[:, e, :].rearrange("p (b d) -> p b d", d=P),
                                      f32(rv_hi[:, :, e * P:(e + 1) * P]), ALU.subtract).then_inc(unit_drained[e], 1)

                def output_lo(hf):
                    dve.wait_ge(ro_copied, h * 4 + (2 * hf + 2))
                    dve.wait_ge(ret_whole, h * 2 + hf)
                    dve.tensor_tensor(ro_lo[:].rearrange("p e t -> p (e t)"), unit[:, (7 + hf) % 2, :],
                                      f32(ro_hi[:].rearrange("p e t -> p (e t)")), ALU.subtract
                                      ).then_inc(unit_drained[(7 + hf) % 2], 1)

                def square_hi(hf):
                    dve.tensor_copy(rs_hi[:].rearrange("p e t -> p (e t)"), tmp_b[:]).then_inc(rs_hi_done, 1)

                def square_lo(hf):
                    dve.wait_ge(rs_hi_done, h * 2 + (hf + 1))
                    dve.tensor_tensor(rs_lo[:].rearrange("p e t -> p (e t)"), tmp_b[:],
                                      f32(rs_hi[:].rearrange("p e t -> p (e t)")), ALU.subtract).then_inc(rs_split, 1)

                wide = tmp_a[:].rearrange("p (e t) -> p e t", e=2)

                def center(hf):
                    m = h * 2 + (hf + 1)
                    dve.wait_ge(ret_normed, h * 2 + hf)
                    dve.wait_ge(r_mean_sq, m)
                    dve.scalar_tensor_tensor(out=r_rstd[:], in0=aux[:, 3, :], scalar=EPS, in1=r_mean2[:],
                                             op0=ALU.add, op1=ALU.subtract).then_inc(r_var, 1)
                    dve.tensor_tensor(wide, f32(ro_hi[:]), aux[:, 2:3, :].to_broadcast([P, 2, HALF]), ALU.subtract
                                      ).then_inc(ret_centered, 1)
                    dve.wait_ge(ret_centered, m)
                    dve.tensor_tensor(wide, wide, f32(ro_lo[:]), ALU.add).then_inc(ret_whole, 1)

                def scale(hf):
                    m = h * 2 + (hf + 1)
                    dve.wait_ge(r_std, m)
                    dve.reciprocal(r_rstd[:], r_mean2[:]).then_inc(r_rstd_ready, 1)
                    dve.wait_ge(r_rstd_ready, m)
                    dve.wait_ge(ret_whole, m)
                    dve.tensor_tensor(acc[:, bass.ds(h * 2, 2), hf * HALF:(hf + 1) * HALF], wide,
                                      r_rstd[:, None, :].to_broadcast([P, 2, HALF]), ALU.mult).then_inc(ret_normed, 1)

                tiles_hi = diags = 0
                for t in range(12):
                    hf, kb, q0, n = ret_tile(t)
                    a = P if q0 == kb * P else 0
                    if a:
                        dve.wait_ge(rp_split, h * 12 + t)
                        dve.wait_ge(rz_ready, h * 12 + (t + 1))
                        dve.tensor_tensor(diag[:], aux[:, t % 2, 0:P], causal[:], ALU.mult).then_inc(diag_masked, 1)
                        dve.wait_ge(diag_masked, h * 8 + (diags + 1))
                        dve.tensor_copy(rp_hi[:, t % 2, 0:P], diag[:]).then_inc(diag_hi, 1)
                        dve.wait_ge(diag_hi, h * 8 + (diags + 1))
                        dve.tensor_tensor(rp_lo[:, t % 2, 0:P], diag[:], f32(rp_hi[:, t % 2, 0:P]), ALU.subtract
                                          ).then_inc(diag_lo if n > a else rp_split, 1)
                        diags += 1
                    if n > a:
                        tiles_hi += 1
                        dve.wait_ge(rp_hi_done, h * 10 + tiles_hi)
                        dve.tensor_tensor(rp_lo[:, t % 2, a:n], aux[:, t % 2, a:n], f32(rp_hi[:, t % 2, a:n]),
                                          ALU.subtract).then_inc(rp_split, 1)
                    if t == 6:
                        output_lo(0)
                    if t == 7:
                        square_hi(0)
                    if t == 8:
                        square_lo(0)
                center(0)
                output_lo(1)
                square_hi(1)
                square_lo(1)
                scale(0)
                center(1)
                scale(1)
                dve.wait_ge(ret_normed, h * 2 + 2)
                dve.wait_ge(unit_drained[1], h * 5 + 5)
                for e in range(2):
                    r = acc[:, bass.ds(h * 2 + e, 1), :].rearrange("p a t -> p (a t)")
                    dve.tensor_tensor(r, r, silu_g[:, e, :], ALU.mult).then_inc(ret_gated, 1)

            for k in range(KT):
                dve.wait_ge(ret_hi_done, k + 1)
                dve.tensor_tensor(ret_lo[:, k, :], acc[:, k, :], f32(ret_hi[:, k, :]), ALU.subtract).then_inc(ret_split, 1)
            with dve.Fori(0, KT) as n:
                dve.wait_ge(unit_ready, n * 2 + (U_GRET + 2))
                dve.wait_ge(unit_drained[0], n + (U_GRET // 2 + 1))
                dve.tensor_tensor(acc[:, bass.ds(n, 1), :].rearrange("p a t -> p (a t)"), unit[:, 1, :], gate_ret[:],
                                  ALU.mult).then_inc(unit_drained[1], 1)

            dve.memset(stick[:, SEQ:SEQ + 1], 1.0).then_inc(stick_consts, 1)
            dve.tensor_copy(ident_r[:], ident[:]).then_inc(stick_consts, 1)
            dve.wait_ge(neg_loaded, 16)
            dve.tensor_copy(neg_r[:], neg[:]).then_inc(stick_consts, 2)
            with dve.Fori(0, SB_PAIRS // 2) as i:
                for pp in range(2):
                    def count(per_pair, k):
                        return i * (2 * per_pair) + (per_pair * pp + k)

                    dve.wait_ge(sqkv_hi, count(3, 1))
                    dve.scalar_tensor_tensor(out=sq_lo[:], in0=unit[:, 0, :], scalar=SB_DIM ** -0.5, in1=f32(sq_hi[:]),
                                             op0=ALU.mult, op1=ALU.subtract).then_inc(unit_drained[0], 1)
                    dve.wait_ge(sqkv_hi, count(3, 2))
                    dve.tensor_tensor(sk_lo[:], unit[:, 1, :], f32(sk_hi[:]), ALU.subtract).then_inc(unit_drained[1], 1)
                    for s in range(18):
                        if s >= 2:
                            r = s - 2
                            qt, hd, n = stick_step(r)
                            dve.wait_ge(wt_hi, count(16, r + 1))
                            dve.tensor_tensor(wT_lo[:, r % 2, 0:n], aux[:, 0:2, :].rearrange("p b t -> p (b t)")[:, 0:n],
                                              f32(wT_hi[:, r % 2, 0:n]), ALU.subtract).then_inc(wt_split, 1)
                        if s < 16:
                            qt, hd, n = stick_step(s)
                            slot = s % 2 if s else 1
                            dve.wait_ge(unit_drained[slot], i * SU + ((U_SB + SU * pp + (4 + s if s else 3)) // 2 + 1))
                            left = stick[:, SEQ - n:SEQ]
                            dve.tensor_tensor_scan(left[:, ::-1], left[:, ::-1], left[:, ::-1], 1.0,
                                                   ALU.mult, ALU.bypass).then_inc(stick_scanned, 1)
                            dve.wait_ge(stick_scanned, count(16, s + 1))
                            dve.tensor_tensor(beta[:, s % 2, 0:n], beta[:, s % 2, 0:n], stick[:, SEQ - n + 1:SEQ + 1],
                                              ALU.mult).then_inc(w_ready, 1)
                        if s == 0:
                            dve.wait_ge(sqkv_hi, count(3, 3))
                            dve.tensor_tensor(sv_lo[:].rearrange("p b d -> p (b d)"), unit[:, 0, :],
                                              f32(sv_hi[:].rearrange("p b d -> p (b d)")), ALU.subtract
                                              ).then_inc(unit_drained[0], 1)

            for k in range(4):
                dve.wait_ge(sbo_hi_done, k + 1)
                dve.tensor_tensor(sbo_lo[:, k, :], sb_out[:, k, :], f32(sbo_hi[:, k, :]), ALU.subtract
                                  ).then_inc(sbo_split, 1)
            def add_branch(i, g, j):
                k = 2 * g + j
                dve.wait_ge(unit_ready, i * GU + (U_GSB + k + 3))
                if g == 0:
                    dve.wait_ge(unit_drained[j], i * (GU // 2) + (U_GSB // 2 + 1))
                    gate = gate_sb[:, j, :]
                else:
                    gate = early_gate[:, 2 * i + j, :]
                dve.tensor_tensor(gate, gate, unit[:, j, :], ALU.mult).then_inc(unit_drained[j], 1)
                dve.wait_ge(unit_drained[j], i * (GU // 2) + (U_GSB // 2 + g + 2))
                r = acc[:, 4 * i + k, :]
                dve.tensor_tensor(r, r, gate, ALU.add).then_inc(branch_summed, 1)

            def split_a(m, ks):
                for k in ks:
                    dve.wait_ge(m.a_hi, k + 1)
                    dve.tensor_tensor(a_lo[:, k, :], acc[:, k, :], f32(a_hi[:, k, :]), ALU.subtract
                                      ).then_inc(m.a_split, 1)

            for i, g, j in ((0, 0, 0), (0, 0, 1), (0, 1, 0), (0, 1, 1), (1, 0, 0), (1, 0, 1), (1, 1, 0)):
                add_branch(i, g, j)
            dve.wait_ge(unit_ready, U_MIX)
            split_a(n1, range(2))
            add_branch(1, 1, 1)
            split_a(n1, range(2, KT))

            def residual(m, first, add_x, stats):
                def stat_split(r, hf, c):
                    dve.wait_ge(m.stat_sq, c)
                    dve.tensor_tensor(st_lo[hf][:], r, f32(st_hi[hf][:]), ALU.subtract)
                    dve.tensor_copy(sqr_hi[hf][:], sqr[hf][:]).then_inc(m.sqr_hi, 1)
                    dve.wait_ge(m.sqr_hi, c)
                    dve.tensor_tensor(sqr_lo[hf][:], sqr[hf][:], f32(sqr_hi[hf][:]), ALU.subtract
                                      ).then_inc(m.stat_split, 1)

                def block(i, j):
                    r, xh, xl = (t[:, bass.ds(i * 2 + j, 1), :].rearrange("p a t -> p (a t)") if not isinstance(i, int)
                                 else t[:, 2 * i + j, :] for t in (acc, x_hi, x_lo))
                    dve.wait_ge(unit_ready, i * 2 + (first + j + 1))
                    if add_x:
                        dve.scalar_tensor_tensor(out=r, in0=f32(xh), scalar=ALPHA, in1=unit[:, j, :], op0=ALU.mult,
                                                 op1=ALU.add).then_inc(unit_drained[j], 1)
                        dve.wait_ge(unit_drained[j], i + (first // 2 + 1))
                        dve.scalar_tensor_tensor(out=r, in0=f32(xl), scalar=ALPHA, in1=r, op0=ALU.mult, op1=ALU.add
                                                 ).then_inc(m.summed, 1)
                    else:
                        dve.tensor_tensor(r, r, unit[:, j, :], ALU.add).then_inc(unit_drained[j], 1)
                    if stats:
                        for hf in range(2):
                            stat_split(r[:, half(hf)], hf, i * 4 + (2 * j + hf + 1))

                if not stats:
                    with dve.Fori(0, 4) as i:
                        for j in range(2):
                            block(i, j)
                    return
                with dve.Fori(0, 3) as i:
                    for j in range(2):
                        block(i, j)
                block(3, 0)
                for hf in range(2):
                    r, u = acc[:, 7, half(hf)], unit[:, 1, half(hf)]
                    if hf:
                        dve.wait_ge(unit_ready, first + KT)
                    else:
                        dve.wait_ge(m.first_half, 1)
                    if add_x:
                        x = dve.scalar_tensor_tensor(out=r, in0=f32(x_hi[:, 7, half(hf)]), scalar=ALPHA, in1=u,
                                                     op0=ALU.mult, op1=ALU.add)
                        if hf:
                            x.then_inc(unit_drained[1], 1)
                            dve.wait_ge(unit_drained[1], first // 2 + 4)
                        else:
                            x.then_inc(m.added, 1)
                            dve.wait_ge(m.added, 1)
                        dve.scalar_tensor_tensor(out=r, in0=f32(x_lo[:, 7, half(hf)]), scalar=ALPHA, in1=r,
                                                 op0=ALU.mult, op1=ALU.add).then_inc(m.last_summed, 1)
                    else:
                        dve.tensor_tensor(r, r, u, ALU.add).then_inc(unit_drained[1] if hf else m.last_summed, 1)
                    if hf:
                        variance(m, 0)
                    stat_split(r, hf, 15 + hf)

            def variance(m, hf):
                dve.wait_ge(m.mean_sq, hf + 1)
                dve.scalar_tensor_tensor(out=ln_rstd[:, half(hf)], in0=aux[:, 2 + hf, :], scalar=EPS,
                                         in1=ln_mean2[:, half(hf)], op0=ALU.add, op1=ALU.subtract).then_inc(m.var, 1)

            def invert(m, hf):
                dve.wait_ge(m.turned, hf + 1)
                dve.reciprocal(inv_col[:, hf, :], aux[:, 2 + hf, :].rearrange("p (b t) -> p b t", t=P)[:, :, 0]
                               ).then_inc(m.inverted, 1)

            def center(m, q):
                hf, k = divmod(q, KT)
                dve.tensor_tensor(ln_t[:, q % 4, :], acc[:, k, half(hf)], aux[:, hf, :], ALU.subtract
                                  ).then_inc(m.centered, 1)

            def layer_norm(m, last, between=None, inverted_at=7):
                center(m, 0)
                center(m, 1)
                invert(m, 0)
                center(m, 2)
                center(m, 3)
                for q in range(2 * KT):
                    hf, k = divmod(q, KT)
                    if between and q in between:
                        between[q]()
                    if q == 1:
                        variance(m, 1)
                    if q >= 4:
                        dve.wait_ge(y_ready if last else m.affine, q - 3)
                        center(m, q)
                    if q == inverted_at:
                        invert(m, 1)
                    rstd = aux[:, 2 + hf, :]
                    dve.wait_ge(m.rstd, hf + 1)
                    if last:
                        rstd = ln_rstd[:, half(hf)]
                        if q % KT == 0:
                            dve.tensor_copy(rstd, aux[:, 2 + hf, :]).then_inc(m.rstd_copied, 1)
                        if q % 2:
                            continue
                        dve.wait_ge(m.rstd_copied, hf + 1)
                    dve.wait_ge(m.centered, q + 1)
                    dve.tensor_tensor(ln_t[:, q % 4, :], ln_t[:, q % 4, :], rstd, ALU.mult).then_inc(m.scaled, 1)

            residual(n1, U_MIX, True, True)
            def memory_lo():
                for k in range(0, KT, 4):
                    dve.wait_ge(mem_hi_done, k + 4)
                    dve.tensor_tensor(mem_lo[:, k:k + 4, :], mem_raw[:, k:k + 4, :], f32(mem_hi[:, k:k + 4, :]),
                                      ALU.subtract).then_inc(mem_split, 4)

            def split_chunk(c):
                s = c % 2
                dve.wait_ge(w_loaded[s], (c // 2 + 1) * 16)
                dve.wait_ge(chunk_started, c)
                dve.tensor_copy(w_hi[s][:], w_raw[:, s, :]).then_inc(w_hi_done, 1)
                dve.wait_ge(w_hi_done, c + 1)
                dve.tensor_tensor(w_lo[s][:], w_raw[:, s, :], f32(w_hi[s][:]), ALU.subtract).then_inc(w_split, 1)

            def keys(h):
                dve.wait_ge(mkq_hi, h * 3 + 1)
                dve.scalar_tensor_tensor(out=mk_lo[:], in0=unit[:, 0, :].rearrange("p (a t) -> p a t", a=2)[:, :, 0:MEM],
                                         scalar=MEM_DIM ** -0.5, in1=f32(mk_hi[:]), op0=ALU.mult, op1=ALU.subtract
                                         ).then_inc(unit_drained[0], 1)

            def queries_and_v(h):
                dve.wait_ge(mkq_hi, h * 3 + 2)
                dve.tensor_tensor(mq_lo[:, 0, :], unit[:, 0, :], f32(mq_hi[:, 0, :]), ALU.subtract
                                  ).then_inc(unit_drained[0], 1)
                dve.wait_ge(turn_hi, h * 3 + 1)
                dve.tensor_tensor(mv_lo[:], aux[:, 0:2, 0:MEM_DIM], f32(mv_hi[:]), ALU.subtract).then_inc(turn_split, 1)
                dve.wait_ge(mkq_hi, h * 3 + 3)
                dve.tensor_tensor(mq_lo[:, 1, :], unit[:, 1, :], f32(mq_hi[:, 1, :]), ALU.subtract
                                  ).then_inc(unit_drained[1], 1)

            def mem_head(h, more):
                def maxima(hf):
                    m = h * 2 + (hf + 1)
                    dve.wait_ge(s_ready, m)
                    dve.tensor_reduce(neg_max[hf][:], aux[:, 2 * hf:2 * hf + 2, :].rearrange("p b (t m) -> p (b t) m", m=MEM),
                                      AX_X, ALU.max).then_inc(max_ready, 1)
                    dve.wait_ge(max_ready, m)
                    dve.tensor_scalar(neg_max[hf][:], neg_max[hf][:], -1.0, None, ALU.mult).then_inc(neg_ready, 1)

                def probabilities(hf):
                    m = h * 2 + (hf + 1)
                    dve.wait_ge(exp_done, m)
                    dve.reciprocal(inv_sum[hf][:], row_sum[hf][:]).then_inc(inv_ready, 1)
                    dve.wait_ge(inv_ready, m)
                    for tt in range(4):
                        x = dve.tensor_scalar(prob[hf][:, tt, :], prob[hf][:, tt, :], inv_sum[hf][:, tt:tt + 1], None,
                                              ALU.mult)
                    x.then_inc(prob_ready, 1)

                def split_p(hf):
                    dve.wait_ge(turn_hi, h * 3 + (hf + 2))
                    dve.tensor_tensor(pT_lo[hf][:], aux[:, 2 * hf:2 * hf + 2, :], f32(pT_hi[hf][:]), ALU.subtract
                                      ).then_inc(turn_split, 1)

                maxima(0)
                maxima(1)
                probabilities(0)
                if more:
                    keys(h + 1)
                probabilities(1)
                split_p(0)
                split_p(1)
                if more:
                    queries_and_v(h + 1)

            layer_norm(n1, False, {0: memory_lo, 2: lambda: split_chunk(CH_MEM + 2), 4: lambda: split_chunk(CH_MEM + 3),
                                   7: lambda: keys(0)}, inverted_at=3)
            for k in range(2):
                dve.wait_ge(mkq_hi, k + 2)
                dve.tensor_tensor(mq_lo[:, k, :], unit[:, 1 - k, :], f32(mq_hi[:, k, :]), ALU.subtract
                                  ).then_inc(unit_drained[1 - k], 1)
            dve.wait_ge(turn_hi, 1)
            dve.tensor_tensor(mv_lo[:], aux[:, 0:2, 0:MEM_DIM], f32(mv_hi[:]), ALU.subtract).then_inc(turn_split, 1)
            with dve.Fori(0, MEM_HEADS - 1) as h:
                mem_head(h, True)
            mem_head(MEM_HEADS - 1, False)

            split_a(n2, range(KT))
            residual(n2, U_MO, True, True)
            layer_norm(n2, False)

            first, tiles = U_FFN, 0
            for part, kts in enumerate(FFN_PARTS):
                with dve.Fori(0, kts) as j:
                    dve.wait_ge(unit_ready, j * 2 + (first + 2))
                    dve.wait_ge(unit_drained[0], j + (first // 2 + 1))
                    dve.wait_ge(hid_lo, j + tiles)
                    dve.tensor_tensor(hidden[:], unit[:, 1, :], silu_h[:], ALU.mult).then_inc(unit_drained[1], 1)
                    dve.wait_ge(hid_hi, j + (tiles + 1))
                    dve.tensor_tensor(a_lo[:, bass.ds(j, 1), :].rearrange("p a t -> p (a t)"), hidden[:],
                                      f32(a_hi[:, bass.ds(j, 1), :].rearrange("p a t -> p (a t)")), ALU.subtract
                                      ).then_inc(hid_lo, 1)
                first, tiles = first + 2 * kts, tiles + kts
                residual(n3, first, part == 0, part == 2)
                first += 8
            layer_norm(n3, True)


def ret_tile(t):
    hf, kb = (0, t) if t < 4 else (1, t - 4)
    q0 = max(hf * HALF, kb * P)
    return hf, kb, q0, (hf + 1) * HALF - q0


def stick_step(s):
    return s // 2, s % 2, (s // 2 + 1) * P


def gate_pieces(s):
    if 0 <= s <= 6:
        return [(0, k) for k in ((0, 1) if s == 0 else (s + 1,))]
    return [(1, k) for k in {8: (0,), 9: (1,), 10: (2,), 11: (3,), 16: (4, 5), 17: (6, 7)}.get(s, ())]


def blocks_of(w):
    k, n = w.shape
    return np.ascontiguousarray(w.reshape(k // P, P, n // P, P).transpose(2, 1, 0, 3))


def weight_streams(w_in, w_sb_o, w_ret_o, w_mix_o, w_mem_q, w_mem_kv, w_mem_o, w_ffn_in, w_ffn_out):
    win, kv, q = blocks_of(w_in), blocks_of(w_mem_kv), blocks_of(w_mem_q)
    ret_o, sb_o, ffn_in, ffn_out = blocks_of(w_ret_o), blocks_of(w_sb_o), blocks_of(w_ffn_in), blocks_of(w_ffn_out)
    eight, seven = [], []
    for h in range(RET_HEADS):
        v, g = BLK_RET_V + 2 * h, BLK_RET_G + 2 * h
        eight += [win[BLK_RET_Q + h], win[BLK_RET_K + h], win[v], win[v + 1], win[g], win[g + 1]]
    for n in range(KT):
        eight += [win[BLK_GATE_RET + n], ret_o[n]]
    for p in range(SB_PAIRS):
        gate = BLK_GATE_SB + p // 2 * 4 + 2 + p % 2
        eight += [win[BLK_SB_Q + p], win[BLK_SB_K + p], win[BLK_SB_V + p], win[gate]]
    for n in range(0, KT, 4):
        eight += [win[BLK_GATE_SB + n], win[BLK_GATE_SB + n + 1],
                  np.concatenate([sb_o[n], sb_o[n + 1]], 1), np.concatenate([sb_o[n + 2], sb_o[n + 3]], 1)]
    eight += list(blocks_of(w_mix_o))
    for h in range(MEM_HEADS):
        k_h, v_h, q_h = kv[2 * h:2 * h + 2], kv[KT + 2 * h:KT + 2 * h + 2], q[2 * h:2 * h + 2]
        for w in (k_h, v_h, q_h) if h else (k_h, q_h, v_h):
            eight += list(w)
    eight += list(blocks_of(w_mem_o))
    j0 = 0
    for kts in FFN_PARTS:
        for j in range(j0, j0 + kts):
            eight += [ffn_in[j], ffn_in[FFN_TILES + j]]
        (eight if kts == 8 else seven).extend(ffn_out[n][:, j0:j0 + kts] for n in range(KT))
        j0 += kts
    return (np.ascontiguousarray(np.stack(eight).reshape(len(eight), P, 8 * P)),
            np.ascontiguousarray(np.stack(seven).reshape(len(seven), P, 7 * P)))


def rope_tables():
    half = RET_QK // 2
    inv = (1.0 / (np.float32(10000.0) ** (np.arange(half, dtype=np.float32) / np.float32(half)))).astype(np.float32)
    pos = np.arange(SEQ, dtype=np.float32)
    ang = (pos[None, :] * inv[:, None]).astype(np.float64)
    cos = np.concatenate([np.cos(ang), np.cos(ang)], 0)
    sin = np.concatenate([np.sin(ang), -np.sin(ang)], 0)
    out = np.empty((RET_HEADS, 2, P, 2, SEQ), np.float64)
    for h in range(RET_HEADS):
        log_gamma = float(np.float32(np.log1p(-(2.0 ** (-5.0 - h)))))
        rel = log_gamma * (np.arange(SEQ) - SEQ // 2)
        for w, f in enumerate((np.exp(rel) * RET_QK ** -0.5, np.exp(-rel))):
            out[h, w, :, 0], out[h, w, :, 1] = cos * f, sin * f
    return out.astype(np.float32).reshape(2 * RET_HEADS, P, 2 * SEQ)


def kernel(x, mem, w_in, b_gate, w_sb_o, w_ret_o, w_mix_o, ln1_g, ln1_b, w_mem_q, w_mem_kv, w_mem_o, ln2_g, ln2_b,
           w_ffn_in, w_ffn_out, ln3_g, ln3_b):
    import concourse.bacc as _bacc
    from concourse.bass_utils import run_bass_kernel_spmd as _run

    x, mem = np.asarray(x), np.asarray(mem)
    eight, seven = weight_streams(*(np.asarray(w)[0] for w in (
        w_in, w_sb_o, w_ret_o, w_mix_o, w_mem_q, w_mem_kv, w_mem_o, w_ffn_in, w_ffn_out)))
    vectors = [np.asarray(v)[0].reshape(-1, P).T for v in (ln1_g, ln1_b, ln2_g, ln2_b, ln3_g, ln3_b, b_gate)]
    row, col = np.arange(P)[:, None], np.arange(P)[None, :]
    arrays = {
        "xT": np.ascontiguousarray(x[0].T),
        "memT": np.ascontiguousarray(mem[0].T),
        "stream8": eight,
        "stream7": seven,
        "params": np.ascontiguousarray(np.concatenate(vectors, 1)),
        "rope": rope_tables(),
        "consts": np.stack([row == col, col >= row, MASKED * (col >= row)]).astype(np.float32),
    }
    nc = _bacc.Bacc("TRN2", target_bir_lowering=False, num_devices=1)
    args = [nc.dram_tensor(n, a.shape, mybir.dt.from_np(a.dtype), kind="ExternalInput").ap() for n, a in arrays.items()]
    args.append(nc.dram_tensor("outT", (D, SEQ), F32, kind="ExternalOutput").ap())
    layer_program(nc, *args)
    r = _run(nc, [arrays], core_ids=[0])
    return np.ascontiguousarray(r.results[0]["outT"].T)[None]
```

```python
from contextlib import ExitStack

import numpy as np

import concourse.bass as bass
from concourse import mybir

ALU = mybir.AluOpType
ACT = mybir.ActivationFunctionType
F32 = mybir.dt.float32
F32R = mybir.dt.float32r
AX_X = mybir.AxisListType.X

P = 128
D = 1024
SEQ = 1024
HALF = 512
KT = D // P
MEM = 256
SB_HEADS, SB_DIM = 8, 64
SB_PAIRS = SB_HEADS // 2
RET_HEADS, RET_QK, RET_V = 4, 128, 256
MEM_HEADS, MEM_DIM = 4, 256
FFN = 2816
FFN_TILES = FFN // P
FFN_PARTS = (8, 7, 7)
ALPHA = 2.0 ** 0.25
EPS = 1e-5
QT = SEQ // P
MASKED = -1e30

BLK_SB_Q, BLK_SB_K, BLK_SB_V = 0, 4, 8
BLK_RET_Q, BLK_RET_K, BLK_RET_V, BLK_RET_G = 12, 16, 20, 28
BLK_GATE_SB, BLK_GATE_RET = 36, 44

CH_RET, CH_GRET, CH_SB, CH_GSB, CH_MIX, CH_MEM, CH_MO, CH_FFN = 0, 24, 40, 56, 64, 72, 96, 104
U_RET, U_GRET, U_SB, U_GSB, U_MIX, U_MEM, U_MO, U_FFN = 0, 40, 56, 136, 148, 156, 180, 188
CH_OUT1 = CH_FFN + 3 * FFN_PARTS[0] + 2 * FFN_PARTS[1]
CH_IN2 = CH_OUT1 + KT
CH_OUT2 = CH_IN2 + 2 * FFN_PARTS[2]
U_OUT2 = U_FFN + 2 * FFN_TILES + 2 * KT
RU, SU, GU, XU = 10, 20, 6, 6


def f32(ap):
    return ap.bitcast(F32)


def half(hf):
    return slice(hf * HALF, (hf + 1) * HALF)


def layer_program(nc, xT, memT, stream8, stream7, params, rope, consts, outT):
    ctx = ExitStack()
    with ctx:
        def sem(name):
            return ctx.enter_context(nc.semaphore(name))

        def sb(stack, name, shape, dt=F32):
            return stack.enter_context(nc.sbuf_tensor(name, shape, dt))

        x_hi = sb(ctx, "x_hi", [P, KT, SEQ], F32R)
        x_lo = sb(ctx, "x_lo", [P, KT, SEQ], F32R)
        acc = sb(ctx, "acc", [P, KT, SEQ])
        w_raw = sb(ctx, "w_raw", [P, 2, D])
        w_hi = [sb(ctx, f"w_hi{s}", [P, D], F32R) for s in range(2)]
        w_lo = [sb(ctx, f"w_lo{s}", [P, D], F32R) for s in range(2)]
        par = sb(ctx, "par", [P, 64])
        one = sb(ctx, "one", [P, 1])
        root_table = sb(ctx, "root_table", [P, 3])
        ident = sb(ctx, "ident", [P, P])
        causal = sb(ctx, "causal", [P, P])
        ln_ones = sb(ctx, "ln_ones", [P, P], F32R)

        with ExitStack() as st:
            rq_hi, rq_lo = sb(st, "rq_hi", [P, SEQ], F32R), sb(st, "rq_lo", [P, SEQ], F32R)
            rk_hi, rk_lo = sb(st, "rk_hi", [P, SEQ], F32R), sb(st, "rk_lo", [P, SEQ], F32R)
            rv_hi, rv_lo = sb(st, "rv_hi", [P, QT, RET_V], F32R), sb(st, "rv_lo", [P, QT, RET_V], F32R)
            tmp_a, tmp_b = sb(st, "tmp_a", [P, SEQ]), sb(st, "tmp_b", [P, SEQ])
            rope_sb = sb(st, "rope_sb", [P, 2, SEQ])
            rp_hi, rp_lo = sb(st, "rp_hi", [P, 2, HALF], F32R), sb(st, "rp_lo", [P, 2, HALF], F32R)
            ret_out = sb(st, "ret_out", [P, 2, HALF])
            rt_sum, rt_sq = sb(st, "rt_sum", [P, HALF]), sb(st, "rt_sq", [P, HALF])
            rt_sum_hi, rt_sum_lo, rt_sq_hi, rt_sq_lo = (
                sb(st, n, [P, HALF], F32R) for n in ("rt_sum_hi", "rt_sum_lo", "rt_sq_hi", "rt_sq_lo"))
            r_mean2, r_rstd = sb(st, "r_mean2", [P, HALF]), sb(st, "r_rstd", [P, HALF])
            silu_g = sb(st, "silu_g", [P, 2, SEQ])
            diag = sb(st, "diag", [P, P])
            ret_ones = sb(st, "ret_ones", [P, P], F32R)
        with ExitStack() as st:
            ret_hi, ret_lo = sb(st, "ret_hi", [P, KT, SEQ], F32R), sb(st, "ret_lo", [P, KT, SEQ], F32R)
            gate_ret = sb(st, "gate_ret", [P, SEQ])
        with ExitStack() as st:
            sb_out = sb(st, "sb_out", [P, 4, SEQ])
            early_gate = sb(st, "early_gate", [P, 4, SEQ])
            with ExitStack() as s2:
                sq_hi, sq_lo = sb(s2, "sq_hi", [P, SEQ], F32R), sb(s2, "sq_lo", [P, SEQ], F32R)
                sk_hi, sk_lo = sb(s2, "sk_hi", [P, SEQ], F32R), sb(s2, "sk_lo", [P, SEQ], F32R)
                sv_hi, sv_lo = sb(s2, "sv_hi", [P, QT, P], F32R), sb(s2, "sv_lo", [P, QT, P], F32R)
                beta = sb(s2, "beta", [P, 2, SEQ])
                sv_T = beta[:, 1, :]
                stick = sb(s2, "stick", [P, SEQ + 1])
                wT_hi, wT_lo = sb(s2, "wT_hi", [P, 2, SEQ], F32R), sb(s2, "wT_lo", [P, 2, SEQ], F32R)
                ident_r = sb(s2, "ident_r", [P, P], F32R)
                neg_r = sb(s2, "neg_r", [P, P], F32R)
                neg = beta[:, 1, 0:P]
            with ExitStack() as s2:
                sbo_hi, sbo_lo = sb(s2, "sbo_hi", [P, 4, SEQ], F32R), sb(s2, "sbo_lo", [P, 4, SEQ], F32R)
                gate_sb = sb(s2, "gate_sb", [P, 2, SEQ])
        with ExitStack() as st:
            a_hi, a_lo = sb(st, "a_hi", [P, KT, SEQ], F32R), sb(st, "a_lo", [P, KT, SEQ], F32R)
            with ExitStack() as s2:
                square = sb(s2, "square", [P, SEQ])
                total, total_sq = sb(s2, "total", [P, SEQ]), sb(s2, "total_sq", [P, SEQ])
                total_hi, total_lo, total_sq_hi, total_sq_lo = (
                    sb(s2, n, [P, HALF], F32R) for n in ("total_hi", "total_lo", "total_sq_hi", "total_sq_lo"))
            with ExitStack() as s2:
                silu_h = sb(s2, "silu_h", [P, SEQ])
                hidden = sb(s2, "hidden", [P, SEQ])
        with ExitStack() as st:
            y_out = sb(st, "y_out", [P, KT, SEQ])
        with ExitStack() as st:
            mem_raw = sb(st, "mem_raw", [P, KT, MEM])
            mem_hi, mem_lo = sb(st, "mem_hi", [P, KT, MEM], F32R), sb(st, "mem_lo", [P, KT, MEM], F32R)
            mk_hi, mk_lo = sb(st, "mk_hi", [P, 2, MEM], F32R), sb(st, "mk_lo", [P, 2, MEM], F32R)
            mv_T = sb(st, "mv_T", [P, 2, MEM])
            mv_hi, mv_lo = sb(st, "mv_hi", [P, 2, MEM_DIM], F32R), sb(st, "mv_lo", [P, 2, MEM_DIM], F32R)
            with ExitStack() as s2:
                ln_mean2, ln_rstd = sb(s2, "ln_mean2", [P, SEQ]), sb(s2, "ln_rstd", [P, SEQ])
                ln_t = sb(s2, "ln_t", [P, 4, HALF])
                ln_x = sb(s2, "ln_x", [P, 4, HALF])
                inv_col = sb(s2, "inv_col", [P, 2, 4])
            with ExitStack() as s2:
                mq_hi, mq_lo = sb(s2, "mq_hi", [P, 2, SEQ], F32R), sb(s2, "mq_lo", [P, 2, SEQ], F32R)
                prob = [sb(s2, f"prob{hf}", [P, 4, MEM]) for hf in range(2)]
                pT_hi = [sb(s2, f"pT_hi{hf}", [P, 2, HALF], F32R) for hf in range(2)]
                pT_lo = [sb(s2, f"pT_lo{hf}", [P, 2, HALF], F32R) for hf in range(2)]
                neg_max, row_sum, inv_sum = ([sb(s2, f"{n}{hf}", [P, 4]) for hf in range(2)]
                                             for n in ("neg_max", "row_sum", "inv_sum"))

        unit = ctx.enter_context(nc.psum_tensor("unit", [P, 2, SEQ], F32))
        aux = ctx.enter_context(nc.psum_tensor("aux", [P, 4, HALF], F32))

        w_loaded = [sem(f"w_loaded{s}") for s in range(2)]
        w_hi_done, w_split, chunk_started = sem("w_hi_done"), sem("w_split"), sem("chunk_started")
        one_ready = sem("one_ready")
        consts_loaded, consts_ready = sem("consts_loaded"), sem("consts_ready")
        x_loaded = [sem(f"x_loaded{k}") for k in range(KT)]
        x_hi_done, x_split = sem("x_hi_done"), sem("x_split")
        unit_ready = sem("unit_ready")
        unit_drained = [sem(f"unit_drained{s}") for s in range(2)]

        rope_loaded, rope_products, rotated, rot_hi, rot_split = (
            sem(n) for n in ("rope_loaded", "rope_products", "rotated", "rot_hi", "rot_split"))
        rv_hi_done = sem("rv_hi_done")
        rz_ready, rp_hi_done, diag_masked, diag_hi, diag_lo, rp_split = (
            sem(n) for n in ("rz_ready", "rp_hi_done", "diag_masked", "diag_hi", "diag_lo", "rp_split"))
        ret_copied, rt_added, rt_hi, rt_split, norm_ready = (
            sem(n) for n in ("ret_copied", "rt_added", "rt_hi", "rt_split", "norm_ready"))
        r_mean_sq, r_var, r_std, r_rstd_ready, ret_centered, ret_normed, ret_gated = (
            sem(n) for n in ("r_mean_sq", "r_var", "r_std", "r_rstd_ready", "ret_centered", "ret_normed", "ret_gated"))
        ret_hi_done, ret_split = sem("ret_hi_done"), sem("ret_split")

        stick_consts, neg_loaded = sem("stick_consts"), sem("neg_loaded")
        gate_half_ready, gate_half_made = sem("gate_half_ready"), sem("gate_half_made")
        sqkv_hi, stick_scanned, w_ready, wt_ready, wt_hi, wt_split, sbo_ready, sbo_stored = (
            sem(n) for n in ("sqkv_hi", "stick_scanned", "w_ready", "wt_ready", "wt_hi", "wt_split",
                             "sbo_ready", "sbo_stored"))
        sbo_hi_done, sbo_split, branch_summed = sem("sbo_hi_done"), sem("sbo_split"), sem("branch_summed")

        mem_loaded, mem_hi_done, mem_split = sem("mem_loaded"), sem("mem_hi_done"), sem("mem_split")
        mkq_hi, s_ready, max_ready, neg_ready, exp_done, inv_ready, prob_ready = (
            sem(n) for n in ("mkq_hi", "s_ready", "max_ready", "neg_ready", "exp_done", "inv_ready", "prob_ready"))
        turn_ready, turn_hi, turn_split = sem("turn_ready"), sem("turn_hi"), sem("turn_split")

        hid_hi, hid_lo = sem("hid_hi"), sem("hid_lo")
        scaled_odd, y_ready, out_stored = sem("scaled_odd"), sem("y_ready"), sem("out_stored")

        class Norm:

            def __init__(self, tag):
                (self.a_hi, self.a_split, self.summed, self.first_half, self.added, self.last_summed, self.squared,
                 self.total_added, self.square_added, self.total_ready, self.total_hi, self.total_split,
                 self.sums_taken, self.mean_sq, self.var, self.std, self.turned, self.inverted, self.rstd,
                 self.rstd_copied, self.centered, self.scaled, self.affine, self.hi, self.done) = (
                    sem(f"{tag}_{n}") for n in (
                        "a_hi", "a_split", "summed", "first_half", "added", "last_summed", "squared", "total_added",
                        "square_added", "total_ready", "total_hi", "total_split", "sums_taken", "mean_sq", "var",
                        "std", "turned", "inverted", "rstd", "rstd_copied", "centered", "scaled", "affine", "hi",
                        "done"))

        n1, n2, n3 = Norm("n1"), Norm("n2"), Norm("n3")

        block = ctx.enter_context(nc.Block())

        @block.sync
        def _(sp):
            def stream(source, first, chunk, count, width):
                with sp.Fori(0, count // 2) as i:
                    for s in range(2):
                        sp.wait_ge(w_split, i * 2 + (chunk + s - 1))
                        sp.dma_start(w_raw[:, s, 0:width],
                                     source[bass.ds(i * 2 + (first + s), 1)].rearrange("a p w -> p (a w)")
                                     ).then_inc(w_loaded[s], 16)

            sp.dma_start(w_raw[:, 0, :], stream8[0]).then_inc(w_loaded[0], 16)
            sp.dma_start(w_raw[:, 1, :], stream8[1]).then_inc(w_loaded[1], 16)
            sp.dma_start(ident[:], consts[0]).then_inc(consts_loaded, 16)
            sp.dma_start(causal[:], consts[1]).then_inc(consts_loaded, 16)
            sp.dma_start(par[:], params).then_inc(consts_loaded, 16)
            stream(stream8, 2, 2, CH_OUT1 - 2, 8 * P)
            stream(stream7, 0, CH_OUT1, KT, 7 * P)
            stream(stream8, CH_OUT1, CH_IN2, CH_OUT2 - CH_IN2, 8 * P)
            stream(stream7, KT, CH_OUT2, KT, 7 * P)
            for q in range(2 * KT):
                hf, k = divmod(q, KT)
                sp.wait_ge(y_ready, q + 1)
                sp.dma_start(outT[k * P:(k + 1) * P, half(hf)], y_out[:, k, half(hf)]).then_inc(out_stored, 16)
            sp.wait_ge(out_stored, 16 * 2 * KT)

        @block.gpsimd
        def _(pool):
            def split(chunk, count, width):
                with pool.Fori(0, count // 2) as i:
                    for s in range(2):
                        c = i * 2 + (chunk + s)
                        pool.wait_ge(w_loaded[s], i * 16 + (chunk // 2 + 1) * 16)
                        pool.wait_ge(chunk_started, c)
                        pool.tensor_tensor(w_hi[s][:, 0:width], w_raw[:, s, 0:width], one[:].to_broadcast([P, width]),
                                           ALU.mult).then_inc(w_hi_done, 1)
                        pool.wait_ge(w_hi_done, c + 1)
                        pool.tensor_tensor(w_lo[s][:, 0:width], w_raw[:, s, 0:width], f32(w_hi[s][:, 0:width]),
                                           ALU.subtract).then_inc(w_split, 1)

            pool.memset(one[:], 1.0).then_inc(one_ready, 1)
            pool.wait_ge(one_ready, 1)
            for s in range(2):
                pool.wait_ge(w_loaded[s], 16)
                pool.tensor_tensor(w_hi[s][:], w_raw[:, s, :], one[:].to_broadcast([P, D]), ALU.mult
                                   ).then_inc(w_hi_done, 1)
                pool.wait_ge(w_hi_done, s + 1)
                pool.tensor_tensor(w_lo[s][:], w_raw[:, s, :], f32(w_hi[s][:]), ALU.subtract).then_inc(w_split, 1)

            def normed_lo(m, qs):
                for q in qs:
                    hf, k = divmod(q, KT)
                    pool.wait_ge(m.hi, q + 1)
                    pool.tensor_tensor(x_lo[:, k, half(hf)], ln_x[:, q % 4, :], f32(x_hi[:, k, half(hf)]), ALU.subtract
                                       ).then_inc(m.done, 1)

            def single(c, width=D):
                s = c % 2
                pool.wait_ge(w_loaded[s], (c // 2 + 1) * 16)
                pool.wait_ge(chunk_started, c)
                pool.tensor_tensor(w_hi[s][:, 0:width], w_raw[:, s, 0:width], one[:].to_broadcast([P, width]), ALU.mult
                                   ).then_inc(w_hi_done, 1)
                pool.wait_ge(w_hi_done, c + 1)
                pool.tensor_tensor(w_lo[s][:, 0:width], w_raw[:, s, 0:width], f32(w_hi[s][:, 0:width]), ALU.subtract
                                   ).then_inc(w_split, 1)

            def residual(m, first, chunk, by_drain, width, splits):
                def stands(n, j):
                    if by_drain:
                        pool.wait_ge(unit_drained[j], n // 2 + (first // 2 + 1))
                    else:
                        pool.wait_ge(m.summed, n + 1)
                    pool.wait_ge(m.squared, n + 1)

                single(chunk + 2, width)
                stands(0, 0)
                pool.tensor_tensor(total[:], acc[:, 0, :], one[:].to_broadcast([P, SEQ]), ALU.mult
                                   ).then_inc(m.total_added, 1)
                pool.tensor_tensor(total_sq[:], square[:], one[:].to_broadcast([P, SEQ]), ALU.mult
                                   ).then_inc(m.square_added, 1)
                with pool.Fori(0, 2) as i:
                    for s in range(2):
                        w, j = 1 - s, 1 - s
                        c = i * 2 + (chunk + s + 3)
                        pool.wait_ge(w_loaded[w], i * 16 + ((chunk + s + 3) // 2 + 1) * 16)
                        pool.wait_ge(chunk_started, c)
                        pool.tensor_tensor(w_hi[w][:, 0:width], w_raw[:, w, 0:width], one[:].to_broadcast([P, width]),
                                           ALU.mult).then_inc(w_hi_done, 1)
                        pool.wait_ge(w_hi_done, c + 1)
                        pool.tensor_tensor(w_lo[w][:, 0:width], w_raw[:, w, 0:width], f32(w_hi[w][:, 0:width]),
                                           ALU.subtract).then_inc(w_split, 1)
                        if by_drain:
                            pool.wait_ge(unit_drained[j], i + (first // 2 + 1 + s))
                        else:
                            pool.wait_ge(m.summed, i * 2 + (s + 2))
                        pool.wait_ge(m.total_added, i * 2 + (s + 1))
                        pool.tensor_tensor(total[:], total[:], acc[:, bass.ds(i * 2 + (s + 1), 1), :].rearrange(
                            "p a t -> p (a t)"), ALU.add).then_inc(m.total_added, 1)
                        pool.wait_ge(m.squared, i * 2 + (s + 2))
                        pool.wait_ge(m.square_added, i * 2 + (s + 1))
                        pool.tensor_tensor(total_sq[:], total_sq[:], square[:], ALU.add).then_inc(m.square_added, 1)
                single(chunk + 7, width)
                stands(5, 1)
                pool.wait_ge(m.total_added, 5)
                pool.tensor_tensor(total[:], total[:], acc[:, 5, :], ALU.add).then_inc(m.total_added, 1)
                pool.wait_ge(m.square_added, 5)
                pool.tensor_tensor(total_sq[:], total_sq[:], square[:], ALU.add).then_inc(m.square_added, 1)
                if splits:
                    single(chunk + 8, width)
                stands(6, 0)
                for hf in range(2):
                    pool.wait_ge(m.total_added, 6)
                    pool.tensor_tensor(total[:, half(hf)], total[:, half(hf)], acc[:, 6, half(hf)], ALU.add
                                       ).then_inc(m.total_added, 1)
                    pool.wait_ge(m.square_added, 6)
                    pool.tensor_tensor(total_sq[:, half(hf)], total_sq[:, half(hf)], square[:, half(hf)], ALU.add
                                       ).then_inc(m.square_added, 1)

            split(2, CH_MIX, 8 * P)
            residual(n1, U_MIX, CH_MIX, False, D, True)
            single(CH_MEM + 1)
            normed_lo(n1, range(2 * KT))
            split(CH_MEM + 4, CH_MO + 2 - CH_MEM - 4, 8 * P)
            residual(n2, U_MO, CH_MO, False, D, True)
            single(CH_FFN + 1)
            normed_lo(n2, range(2 * KT))
            split(CH_FFN + 2, CH_OUT1 - CH_FFN - 2, 8 * P)
            split(CH_OUT1, KT, 7 * P)
            split(CH_IN2, CH_OUT2 - CH_IN2, 8 * P)
            split(CH_OUT2, 2, 7 * P)
            residual(n3, U_OUT2, CH_OUT2, True, 7 * P, False)
            for q in range(1, 2 * KT, 2):
                hf = q // KT
                pool.wait_ge(n3.centered, q + 1)
                pool.wait_ge(n3.rstd_copied, hf + 1)
                pool.tensor_tensor(ln_t[:, q % 4, :], ln_t[:, q % 4, :], ln_rstd[:, half(hf)], ALU.mult
                                   ).then_inc(scaled_odd, 1)

        @block.tensor
        def _(pe):
            def triple(out, l_hi, l_lo, r_hi, r_lo, start, stop):
                pe.matmul(out, l_hi, r_lo, start=start, stop=False, skip_group_check=True)
                pe.matmul(out, l_hi, r_hi, start=False, stop=False, skip_group_check=True)
                return pe.matmul(out, l_lo, r_hi, start=False, stop=stop, skip_group_check=True)

            def free_unit(first, per, i, k):
                pe.wait_ge(unit_drained[k % 2], i * (per // 2) + (first // 2 + k // 2))
                return unit[:, k % 2, :]

            def project(chunk, s, outs, hi, lo, kts=KT, w0=0, arrived=None, before=0, mid=None, begins=True):
                pe.wait_ge(w_split, chunk + 1)
                last = None
                for k in range(kts):
                    if arrived:
                        pe.wait_ge(arrived, before + k + 1)
                    if mid and k == kts // 2:
                        mid()
                    wk = slice((w0 + k) * P, (w0 + k + 1) * P)
                    for j, (out, cols) in enumerate(outs):
                        first = k == 0
                        x = pe.matmul(out, w_hi[s][:, wk], lo[:, k, cols], start=first, stop=False,
                                      skip_group_check=True)
                        if k == 0 and j == 0 and w0 == 0 and begins:
                            x.then_inc(chunk_started, 1)
                        pe.matmul(out, w_hi[s][:, wk], hi[:, k, cols], start=False, stop=False,
                                  skip_group_check=True)
                        last = pe.matmul(out, w_lo[s][:, wk], hi[:, k, cols], start=False, stop=(k == kts - 1),
                                         skip_group_check=True)
                return last

            def halves(u):
                return [(u[:, h * HALF:(h + 1) * HALF], slice(h * HALF, (h + 1) * HALF)) for h in range(2)]

            with pe.Fori(0, RET_HEADS) as h:
                def proj(k, c, arrived=None):
                    u = free_unit(U_RET, RU, h, k)
                    project(h * 6 + c, c % 2, halves(u), x_hi, x_lo, arrived=arrived).then_inc(unit_ready, 1)

                def turn_v(k, source):
                    u = free_unit(U_RET, RU, h, k)
                    for b in range(QT):
                        t = pe.transpose(u[:, b * P:(b + 1) * P], source[:, b * P:(b + 1) * P], ident[:])
                    t.then_inc(unit_ready, 1)

                pe.wait_ge(consts_ready, 2)
                proj(0, 0, x_split)
                proj(1, 1)
                proj(2, 2)
                proj(3, 3)
                pe.wait_ge(unit_drained[0], h * 5 + 2)
                turn_v(4, tmp_a)
                pe.wait_ge(unit_drained[1], h * 5 + 2)
                turn_v(5, tmp_b)

                def score(t):
                    hf, kb, q0, n = ret_tile(t)
                    z = aux[:, t % 2, 0:n]
                    triple(z, rk_hi[:, kb * P:(kb + 1) * P], rk_lo[:, kb * P:(kb + 1) * P],
                           rq_hi[:, q0:q0 + n], rq_lo[:, q0:q0 + n], True, True).then_inc(rz_ready, 1)

                def values(t):
                    hf, kb, q0, n = ret_tile(t)
                    u = unit[:, (7 + hf) % 2, :]
                    if kb == 0:
                        free_unit(U_RET, RU, h, 7 + hf)
                    pe.wait_ge(rp_split, h * 12 + (t + 1))
                    last_kb = 3 if hf == 0 else 7
                    for e in range(2):
                        c0 = e * HALF + q0 - hf * HALF
                        x = triple(u[:, c0:c0 + n], rv_hi[:, kb, e * P:(e + 1) * P], rv_lo[:, kb, e * P:(e + 1) * P],
                                   rp_hi[:, t % 2, 0:n], rp_lo[:, t % 2, 0:n], kb == 0, kb == last_kb)
                    if kb == last_kb:
                        x.then_inc(unit_ready, 1)

                def norm_sums(hf):
                    pe.wait_ge(rt_split, h * 2 + (hf + 1))
                    pe.wait_ge(ret_centered, h * 2 + hf)
                    for b, (hi, lo) in enumerate(((rt_sum_hi, rt_sum_lo), (rt_sq_hi, rt_sq_lo))):
                        pe.matmul(aux[:, 2 + b, :], ret_ones[:], lo[:], start=True, stop=False, skip_group_check=True)
                        x = pe.matmul(aux[:, 2 + b, :], ret_ones[:], hi[:], start=False, stop=True,
                                      skip_group_check=True)
                    x.then_inc(norm_ready, 1)

                pe.wait_ge(rot_split, h * 2 + 2)
                score(0)
                for t in range(1, 12):
                    score(t)
                    if t == 1:
                        proj(6, 4)
                    values(t - 1)
                    if t == 10:
                        norm_sums(0)
                values(11)
                proj(9, 5)
                norm_sums(1)

            with pe.Fori(0, KT) as n:
                u = free_unit(U_GRET, 2, n, 0)
                project(n * 2 + CH_GRET, 0, halves(u), x_hi, x_lo).then_inc(unit_ready, 1)
                u = free_unit(U_GRET, 2, n, 1)
                project(n * 2 + (CH_GRET + 1), 1, halves(u), ret_hi, ret_lo, arrived=ret_split).then_inc(unit_ready, 1)

            with pe.Fori(0, SB_PAIRS // 2) as i:
                for pp in range(2):
                    def sbu(k):
                        return free_unit(U_SB + SU * pp, 2 * SU, i, k)

                    def drained(k):
                        pe.wait_ge(unit_drained[k % 2], i * SU + (U_SB + SU * pp) // 2 + (k // 2 + 1))

                    def count(per_pair, k):
                        return i * (2 * per_pair) + (per_pair * pp + k)

                    for k in range(3):
                        c = 4 * pp + k
                        u = sbu(k)
                        project(i * 8 + (CH_SB + c), c % 2, halves(u), x_hi, x_lo).then_inc(unit_ready, 1)
                    drained(0)
                    drained(1)
                    pe.wait_ge(stick_consts, 4)

                    def logits(s):
                        qt, hd, n = stick_step(s)
                        q, rows = slice(qt * P, (qt + 1) * P), slice(hd * SB_DIM, (hd + 1) * SB_DIM)
                        u = sbu(4 + s if s else 3)
                        for c0 in range(0, n, HALF):
                            c1 = min(n, c0 + HALF)
                            triple(u[:, c0:c1], sq_hi[rows, q], sq_lo[rows, q], sk_hi[rows, c0:c1], sk_lo[rows, c0:c1],
                                   True, False)
                        pe.matmul(u[:, n - P:n], ident_r[:], neg_r[:], start=False, stop=True,
                                  skip_group_check=True).then_inc(unit_ready, 1)

                    def turn_w(s):
                        qt, hd, n = stick_step(s)
                        pe.wait_ge(w_ready, count(16, s + 1))
                        pe.wait_ge(wt_split, count(16, s))
                        for b in range(qt + 1):
                            x = pe.transpose(aux[:, b // 4, b % 4 * P:(b % 4 + 1) * P],
                                             beta[:, s % 2, b * P:(b + 1) * P], ident[:])
                        x.then_inc(wt_ready, 1)

                    def values(s):
                        qt, hd, n = stick_step(s)
                        pe.wait_ge(wt_split, count(16, s + 1))
                        if qt == 0 and hd == 0:
                            drained(4)
                        if qt and qt % 2 == 0 and hd == 0:
                            pe.wait_ge(sbo_stored, count(8, qt))
                        c0 = hd * 2 * P + qt % 2 * P
                        out = aux[0:SB_DIM, 2, c0:c0 + P]
                        for b in range(qt + 1):
                            v = slice(hd * SB_DIM, (hd + 1) * SB_DIM)
                            x = triple(out, sv_hi[:, b, v], sv_lo[:, b, v], wT_hi[:, s % 2, b * P:(b + 1) * P],
                                       wT_lo[:, s % 2, b * P:(b + 1) * P], b == 0, b == qt)
                        if qt % 2 and hd:
                            x.then_inc(sbo_ready, 1)

                    def early_gate_piece(hf, k):
                        c, wk, cols = 4 * pp + 3, slice(k * P, (k + 1) * P), slice(hf * HALF, (hf + 1) * HALF)
                        if k == 0:
                            pe.wait_ge(gate_half_made, count(2, hf))
                            if hf == 0:
                                pe.wait_ge(w_split, i * 8 + (CH_SB + c + 1))
                        x = pe.matmul(aux[:, 3, :], w_hi[1][:, wk], x_lo[:, k, cols], start=(k == 0), stop=False,
                                      skip_group_check=True)
                        if k == 0 and hf == 0:
                            x.then_inc(chunk_started, 1)
                        pe.matmul(aux[:, 3, :], w_hi[1][:, wk], x_hi[:, k, cols], start=False, stop=False,
                                  skip_group_check=True)
                        x = pe.matmul(aux[:, 3, :], w_lo[1][:, wk], x_hi[:, k, cols], start=False, stop=(k == KT - 1),
                                      skip_group_check=True)
                        if k == KT - 1:
                            x.then_inc(gate_half_ready, 1)

                    for s in range(19):
                        if 2 <= s <= 17:
                            turn_w(s - 2)
                        if s < 16:
                            logits(s)
                        if s == 0:
                            drained(2)
                            u = sbu(4)
                            for b in range(QT):
                                t = pe.transpose(u[:, b * P:(b + 1) * P], sv_T[:, b * P:(b + 1) * P], ident[:])
                            t.then_inc(unit_ready, 1)
                        if s >= 3:
                            values(s - 3)
                        for hf, k in gate_pieces(s):
                            early_gate_piece(hf, k)

            with pe.Fori(0, 2) as i:
                for c in range(2):
                    u = free_unit(U_GSB, GU, i, c)
                    project(i * 4 + (CH_GSB + c), c, halves(u), x_hi, x_lo).then_inc(unit_ready, 1)
                for c in range(2):
                    for j in range(2):
                        u = free_unit(U_GSB, GU, i, 2 + 2 * c + j)
                        project(i * 4 + (CH_GSB + 2 + c), c, halves(u), sbo_hi, sbo_lo, kts=4, w0=4 * j,
                                arrived=sbo_split).then_inc(unit_ready, 1)

            def spread_rstd(m, hf, counts_chunk=False):
                pe.wait_ge(m.std, hf + 1)
                for b in range(4):
                    x = pe.transpose(aux[:, 2 + hf, b * P:(b + 1) * P],
                                     ln_mean2[:, hf * HALF + b * P:hf * HALF + (b + 1) * P], ident[:])
                    if b == 0 and counts_chunk:
                        x.then_inc(chunk_started, 1)
                x.then_inc(m.turned, 1)
                pe.wait_ge(m.inverted, hf + 1)
                for b in range(4):
                    x = pe.transpose(aux[:, 2 + hf, b * P:(b + 1) * P],
                                     inv_col[:, hf, b:b + 1].to_broadcast([P, P]), ident[:])
                x.then_inc(m.rstd, 1)

            def residual(m, chunk, first, kts, arrived, stats, next_chunk=False, before=0):

                def sums(hf, counts_chunk=False):
                    pe.wait_ge(m.total_split, hf + 1)
                    for b, (hi, lo) in enumerate(((total_hi, total_lo), (total_sq_hi, total_sq_lo))):
                        x = pe.matmul(aux[:, 2 * b + hf, :], ln_ones[:], lo[:], start=True, stop=False,
                                      skip_group_check=True)
                        if counts_chunk and b == 0:
                            x.then_inc(chunk_started, 1)
                        x = pe.matmul(aux[:, 2 * b + hf, :], ln_ones[:], hi[:], start=False, stop=True,
                                      skip_group_check=True)
                    x.then_inc(m.sums_taken, 1)

                def block(i, j):
                    u = free_unit(first, 2, i, j)
                    project(i * 2 + (chunk + j), j, halves(u), a_hi, a_lo, kts=kts, arrived=arrived, before=before
                            ).then_inc(unit_ready, 1)

                with pe.Fori(0, 3 if stats else 4) as i:
                    for j in range(2):
                        block(i, j)
                if not stats:
                    return
                block(3, 0)
                halves_u = halves(free_unit(first, 2, 3, 1))
                project(chunk + 7, 1, halves_u[0:1], a_hi, a_lo, kts=kts).then_inc(m.first_half, 1)
                project(chunk + 7, 1, halves_u[1:2], a_hi, a_lo, kts=kts, begins=False).then_inc(unit_ready, 1)
                sums(0, counts_chunk=next_chunk)
                spread_rstd(m, 0)
                sums(1)

            residual(n1, CH_MIX, U_MIX, KT, n1.a_split, True, next_chunk=True)

            def mem_chunk(h, c, u, j, begins=True):
                return project(h * 6 + (CH_MEM + c), c % 2, [(u[:, j * HALF:j * HALF + MEM], slice(0, MEM))],
                               mem_hi, mem_lo, begins=begins)

            def mem_queries(h, c, u):
                project(h * 6 + (CH_MEM + c), c % 2, halves(u), x_hi, x_lo).then_inc(unit_ready, 1)

            def as_normed(m, chunk, first, mid=None):
                slots = [(first + c) % 2 for c in range(2)]
                for c in range(2):
                    pe.wait_ge(unit_drained[slots[c]], (first + c) // 2)
                    pe.wait_ge(w_split, chunk + c + 1)
                for k in range(KT):
                    pe.wait_ge(m.done, k + 1)
                    wk = slice(k * P, (k + 1) * P)
                    for c in range(2):
                        out, start, stop = unit[:, slots[c], half(0)], k == 0, k == KT - 1
                        pe.matmul(out, w_hi[c][:, wk], x_lo[:, k, half(0)], start=start, stop=False,
                                  skip_group_check=True)
                        pe.matmul(out, w_hi[c][:, wk], x_hi[:, k, half(0)], start=False, stop=False,
                                  skip_group_check=True)
                        pe.matmul(out, w_lo[c][:, wk], x_hi[:, k, half(0)], start=False, stop=stop,
                                  skip_group_check=True)
                    if mid and k == 1:
                        mid()
                for c in range(2):
                    project(chunk + c, c, [(unit[:, slots[c], half(1)], half(1))], x_hi, x_lo,
                            arrived=m.done if c == 0 else None, before=KT, begins=c == 1).then_inc(unit_ready, 1)

            def turn_mem_v():
                for dt in range(2):
                    for mt in range(2):
                        t = pe.transpose(aux[:, mt, dt * P:(dt + 1) * P], mv_T[:, dt, mt * P:(mt + 1) * P], ident[:])
                t.then_inc(turn_ready, 1)

            def mem_head(h, more):
                base = U_MEM + 4

                def scores(hf):
                    for tt in range(4):
                        tok = slice((hf * 4 + tt) * P, (hf * 4 + tt + 1) * P)
                        out = aux[:, 2 * hf + tt // 2, tt % 2 * MEM:(tt % 2 + 1) * MEM]
                        for dt in range(2):
                            x = triple(out, mq_hi[:, dt, tok], mq_lo[:, dt, tok], mk_hi[:, dt, :], mk_lo[:, dt, :],
                                       dt == 0, dt == 1)
                    x.then_inc(s_ready, 1)

                def turn_p(hf):
                    pe.wait_ge(prob_ready, h * 2 + (hf + 1))
                    for tt in range(4):
                        for mt in range(2):
                            x = pe.transpose(aux[:, 2 * hf + mt, tt * P:(tt + 1) * P],
                                             prob[hf][:, tt, mt * P:(mt + 1) * P], ident[:])
                    x.then_inc(turn_ready, 1)

                def values(hf, k):
                    u = free_unit(base, XU, h, k)
                    pe.wait_ge(turn_split, h * 3 + (hf + 2))
                    for dt in range(2):
                        for mt in range(2):
                            x = triple(u[:, dt * HALF:(dt + 1) * HALF], mv_hi[:, mt, dt * P:(dt + 1) * P],
                                       mv_lo[:, mt, dt * P:(dt + 1) * P], pT_hi[hf][:, mt, :], pT_lo[hf][:, mt, :],
                                       mt == 0, mt == 1)
                    x.then_inc(unit_ready, 1)

                if more:
                    u = free_unit(base, XU, h, 0)
                    mem_chunk(h + 1, 0, u, 0)
                pe.wait_ge(unit_drained[0], h * 3 + (U_MEM // 2 + 2))
                pe.wait_ge(unit_drained[1], h * 3 + (U_MEM // 2 + 2))
                pe.wait_ge(turn_split, h * 3 + 1)
                scores(0)
                scores(1)
                if more:
                    mem_chunk(h + 1, 1, u, 1).then_inc(unit_ready, 1)
                turn_p(0)
                if more:
                    u = free_unit(base, XU, h, 2)
                    mem_chunk(h + 1, 2, u, 0)
                turn_p(1)
                values(0, 1 if more else 0)
                if more:
                    mem_chunk(h + 1, 3, u, 1).then_inc(unit_ready, 1)
                values(1, 3 if more else 1)
                if more:
                    mem_queries(h + 1, 4, free_unit(base, XU, h, 4))
                    turn_mem_v()
                    mem_queries(h + 1, 5, free_unit(base, XU, h, 5))

            pe.wait_ge(mem_split, KT)
            u = free_unit(U_MEM, XU, 0, 0)
            mem_chunk(0, 0, u, 0, begins=False)
            mem_chunk(0, 1, u, 1).then_inc(unit_ready, 1)
            spread_rstd(n1, 1, counts_chunk=True)
            as_normed(n1, CH_MEM + 2, U_MEM + 1)
            u = free_unit(U_MEM, XU, 0, 3)
            mem_chunk(0, 4, u, 0)
            mem_chunk(0, 5, u, 1).then_inc(unit_ready, 1)
            pe.wait_ge(unit_drained[1], U_MEM // 2 + 2)
            turn_mem_v()
            with pe.Fori(0, MEM_HEADS - 1) as h:
                mem_head(h, True)
            mem_head(MEM_HEADS - 1, False)

            residual(n2, CH_MO, U_MO, KT, n2.a_split, True, next_chunk=True)

            chunk, first, tiles = CH_FFN, U_FFN, 0
            for part, kts in enumerate(FFN_PARTS):
                if part == 0:
                    as_normed(n2, chunk, first, mid=lambda: spread_rstd(n2, 1))
                with pe.Fori(0 if part else 1, kts) as j:
                    for g in range(2):
                        u = free_unit(first, 2, j, g)
                        project(j * 2 + (chunk + g), g, halves(u), x_hi, x_lo).then_inc(unit_ready, 1)
                chunk, first, tiles = chunk + 2 * kts, first + 2 * kts, tiles + kts
                residual(n3, chunk, first, kts, hid_lo, part == 2, before=tiles - kts)
                chunk, first = chunk + 8, first + 8
            spread_rstd(n3, 1)

        @block.scalar
        def _(act):
            for k in range(KT):
                act.dma_start(acc[:, k, :], xT[k * P:(k + 1) * P, :]).then_inc(x_loaded[k], 16)
            for k in range(KT):
                act.wait_ge(x_loaded[k], 16)
                act.activation(x_hi[:, k, :], acc[:, k, :], ACT.Copy).then_inc(x_hi_done, 1)

            with act.Fori(0, RET_HEADS) as h:
                def ready(k):
                    act.wait_ge(unit_ready, h * RU + (U_RET + k + 1))

                for w in range(2):
                    act.wait_ge(rotated, h * 2 + w)
                    act.dma_start(rope_sb[:].rearrange("p a t -> p (a t)"),
                                  rope[bass.ds(h * 2 + w, 1)].rearrange("a p t -> p (a t)")).then_inc(rope_loaded, 16)
                    act.wait_ge(rotated, h * 2 + (w + 1))
                    act.activation((rq_hi, rk_hi)[w][:], tmp_a[:], ACT.Copy).then_inc(rot_hi, 1)
                ready(2)
                act.wait_ge(rot_split, h * 2 + 2)
                act.activation(tmp_a[:], unit[:, 0, :], ACT.Copy).then_inc(unit_drained[0], 1)
                ready(3)
                act.activation(tmp_b[:], unit[:, 1, :], ACT.Copy).then_inc(unit_drained[1], 1)
                ready(4)
                act.activation(rv_hi[:, :, 0:P], unit[:, 0, :].rearrange("p (b d) -> p b d", d=P), ACT.Copy
                               ).then_inc(rv_hi_done, 1)
                ready(5)
                act.activation(rv_hi[:, :, P:2 * P], unit[:, 1, :].rearrange("p (b d) -> p b d", d=P), ACT.Copy
                               ).then_inc(rv_hi_done, 1)

                def copy_output(hf):
                    ready(7 + hf)
                    act.wait_ge(ret_centered, h * 2 + hf)
                    act.activation(ret_out[:].rearrange("p e t -> p (e t)"), unit[:, (7 + hf) % 2, :], ACT.Copy
                                   ).then_inc(ret_copied, 1)

                def square_output(hf):
                    act.activation(tmp_b[:], unit[:, (7 + hf) % 2, :], ACT.Square
                                   ).then_inc(unit_drained[(7 + hf) % 2], 1)

                def mean_square(hf):
                    act.wait_ge(norm_ready, h * 2 + (hf + 1))
                    act.wait_ge(r_rstd_ready, h * 2 + hf)
                    act.activation(r_mean2[:], aux[:, 2, :], ACT.Square).then_inc(r_mean_sq, 1)

                def root(hf):
                    act.wait_ge(r_var, h * 2 + (hf + 1))
                    act.activation(r_mean2[:], r_rstd[:], ACT.Sqrt).then_inc(r_std, 1)

                diags = 0
                for t in range(12):
                    if t == 2:
                        ready(6)
                        act.wait_ge(ret_gated, h * 2)
                        act.activation(silu_g[:, 0, :], unit[:, 0, :], ACT.Silu).then_inc(unit_drained[0], 1)
                    hf, kb, q0, n = ret_tile(t)
                    a = P if q0 == kb * P else 0
                    if a:
                        diags += 1
                        if n > a:
                            act.wait_ge(diag_masked, h * 8 + diags)
                    if n > a:
                        act.wait_ge(rz_ready, h * 12 + (t + 1))
                        act.activation(rp_hi[:, t % 2, a:n], aux[:, t % 2, a:n], ACT.Copy).then_inc(rp_hi_done, 1)
                    if t == 4:
                        copy_output(0)
                    if t == 5:
                        square_output(0)
                mean_square(0)
                copy_output(1)
                square_output(1)
                root(0)
                ready(9)
                act.activation(silu_g[:, 1, :], unit[:, 1, :], ACT.Silu).then_inc(unit_drained[1], 1)
                mean_square(1)
                root(1)

            for k in range(KT):
                act.wait_ge(ret_gated, max(k + 1, 2 * RET_HEADS - 2))
                act.activation(ret_hi[:, k, :], acc[:, k, :], ACT.Copy).then_inc(ret_hi_done, 1)
            with act.Fori(0, KT) as n:
                act.wait_ge(unit_ready, n * 2 + (U_GRET + 1))
                act.wait_ge(unit_drained[1], n + U_GRET // 2)
                act.activation(gate_ret[:], unit[:, 0, :], ACT.Sigmoid, bias=par[:, bass.ds(n + 56, 1)]
                               ).then_inc(unit_drained[0], 1)

            act.wait_ge(unit_drained[1], U_SB // 2)
            act.dma_start(neg[:], consts[2]).then_inc(neg_loaded, 16)
            with act.Fori(0, SB_PAIRS // 2) as i:
                for pp in range(2):
                    def ready(k):
                        act.wait_ge(unit_ready, i * (2 * SU) + (U_SB + SU * pp + k + 1))

                    def count(per_pair, k):
                        return i * (2 * per_pair) + (per_pair * pp + k)

                    ready(0)
                    act.activation(sq_hi[:], unit[:, 0, :], ACT.Copy, scale=SB_DIM ** -0.5).then_inc(sqkv_hi, 1)
                    ready(1)
                    act.activation(sk_hi[:], unit[:, 1, :], ACT.Copy).then_inc(sqkv_hi, 1)
                    ready(2)
                    if pp == 0:
                        act.wait_ge(stick_consts, 4)
                    act.activation(sv_T, unit[:, 0, :], ACT.Copy).then_inc(unit_drained[0], 1)

                    def split_w(s):
                        qt, hd, n = stick_step(s)
                        act.wait_ge(wt_ready, count(16, s + 1))
                        act.activation(wT_hi[:, s % 2, 0:n], aux[:, 0:2, :].rearrange("p b t -> p (b t)")[:, 0:n],
                                       ACT.Copy).then_inc(wt_hi, 1)

                    def store(s):
                        qt, hd, n = stick_step(s)
                        two = qt // 2
                        act.wait_ge(sbo_ready, count(4, two + 1))
                        for hd in range(2):
                            act.activation(sb_out[hd * SB_DIM:(hd + 1) * SB_DIM, bass.ds(i * 2 + pp, 1),
                                                  two * 2 * P:(two + 1) * 2 * P].rearrange("p a t -> p (a t)"),
                                           aux[0:SB_DIM, 2, hd * 2 * P:(hd + 1) * 2 * P], ACT.Copy
                                           ).then_inc(sbo_stored, 1)

                    for s in range(19):
                        if 2 <= s <= 17:
                            split_w(s - 2)
                        if s < 16:
                            qt, hd, n = stick_step(s)
                            slot = s % 2 if s else 1
                            ready(4 + s if s else 3)
                            act.activation(beta[:, s % 2, 0:n], unit[:, slot, 0:n], ACT.Sigmoid)
                            act.wait_ge(w_ready, count(16, s))
                            act.activation(stick[:, SEQ - n:SEQ], unit[:, slot, 0:n], ACT.Sigmoid, scale=-1.0
                                           ).then_inc(unit_drained[slot], 1)
                        if s == 0:
                            ready(4)
                            act.activation(sv_hi[:].rearrange("p b d -> p (b d)"), unit[:, 0, :], ACT.Copy
                                           ).then_inc(sqkv_hi, 1)
                        if s >= 3 and (s - 3) % 4 == 3:
                            store(s - 3)
                        for hf, k in gate_pieces(s - 1):
                            if k == KT - 1:
                                act.wait_ge(gate_half_ready, count(2, hf + 1))
                                act.activation(early_gate[:, bass.ds(i * 2 + pp, 1), hf * HALF:(hf + 1) * HALF
                                                          ].rearrange("p a t -> p (a t)"), aux[:, 3, :], ACT.Sigmoid,
                                               bias=par[:, bass.ds(i * 4 + (50 + pp), 1)]).then_inc(gate_half_made, 1)

            for k in range(4):
                act.wait_ge(sbo_stored, 8 * SB_PAIRS)
                act.activation(sbo_hi[:, k, :], sb_out[:, k, :], ACT.Copy).then_inc(sbo_hi_done, 1)
            with act.Fori(0, 2) as i:
                for j in range(2):
                    act.wait_ge(unit_ready, i * GU + (U_GSB + j + 1))
                    act.wait_ge(branch_summed, i * 4)
                    act.activation(gate_sb[:, j, :], unit[:, j, :], ACT.Sigmoid,
                                   bias=par[:, bass.ds(i * 4 + (48 + j), 1)]).then_inc(unit_drained[j], 1)

            def split_a(m, before, value, ks=range(KT)):
                for k in ks:
                    act.wait_ge(before, value(k))
                    act.activation(a_hi[:, k, :], acc[:, k, :], ACT.Copy).then_inc(m.a_hi, 1)

            def root(m, hf):
                act.wait_ge(m.var, hf + 1)
                act.activation(ln_mean2[:, half(hf)], ln_rstd[:, half(hf)], ACT.Sqrt).then_inc(m.std, 1)

            def statistics(m, which, first, by_drain, between=None):
                def block(i, j):
                    if by_drain:
                        act.wait_ge(unit_drained[j], i + (first // 2 + 1))
                    else:
                        act.wait_ge(m.summed, i * 2 + (j + 1))
                    act.wait_ge(m.square_added, i * 2 + j)
                    r = acc[:, bass.ds(i * 2 + j, 1), :].rearrange("p a t -> p (a t)") if not isinstance(i, int) else \
                        acc[:, 2 * i + j, :]
                    act.activation(square[:], r, ACT.Square).then_inc(m.squared, 1)

                def last_square(hf):
                    act.wait_ge(m.square_added, 7 + hf)
                    act.activation(square[:, half(hf)], acc[:, 7, half(hf)], ACT.Square).then_inc(m.squared, 1)

                def total_hi_parts(hf):
                    act.wait_ge(m.sums_taken, hf)
                    for n, (hi, t) in enumerate(((total_hi, total), (total_sq_hi, total_sq))):
                        act.wait_ge(m.total_ready, 2 * hf + n + 1)
                        act.activation(hi[:], t[:, half(hf)], ACT.Copy).then_inc(m.total_hi, 1)

                def mean_square(hf):
                    act.wait_ge(m.sums_taken, hf + 1)
                    act.activation(ln_mean2[:, half(hf)], aux[:, hf, :], ACT.Square).then_inc(m.mean_sq, 1)

                with act.Fori(0, KT // 2 - 1) as i:
                    for j in range(2):
                        block(i, j)
                act.activation(root_table[:, which:which + 1], one[:], ACT.Sqrt)
                block(3, 0)
                act.wait_ge(m.last_summed, 1)
                last_square(0)
                total_hi_parts(0)
                if between:
                    between[0]()
                if by_drain:
                    act.wait_ge(unit_drained[1], first // 2 + 4)
                else:
                    act.wait_ge(m.last_summed, 2)
                last_square(1)
                mean_square(0)
                total_hi_parts(1)
                root(m, 0)
                if between:
                    between[1]()
                mean_square(1)

            def layer_norm(m, which, between=None):
                for q in range(2 * KT):
                    hf, k = divmod(q, KT)
                    if between and q in between:
                        between[q]()
                    if q == 2:
                        root(m, 1)
                    g, b = par[:, 16 * which + k:16 * which + k + 1], par[:, 16 * which + 8 + k:16 * which + 9 + k]
                    if which == 2:
                        if q % 2:
                            act.wait_ge(scaled_odd, q // 2 + 1)
                        else:
                            act.wait_ge(m.scaled, q // 2 + 1)
                        act.activation(y_out[:, k, half(hf)], ln_t[:, q % 4, :], ACT.Identity, scale=g, bias=b
                                       ).then_inc(y_ready, 1)
                        continue
                    act.wait_ge(m.scaled, q + 1)
                    if q >= 4:
                        act.wait_ge(m.done, q - 3)
                    act.activation(ln_x[:, q % 4, :], ln_t[:, q % 4, :], ACT.Identity, scale=g, bias=b
                                   ).then_inc(m.affine, 1)
                    act.wait_ge(m.affine, q + 1)
                    act.activation(x_hi[:, k, half(hf)], ln_x[:, q % 4, :], ACT.Copy).then_inc(m.hi, 1)

            split_a(n1, branch_summed, lambda k: k + 1)
            def load_memory():
                act.wait_ge(unit_ready, U_MIX + KT)
                act.dma_start(mem_raw[:], memT.rearrange("(a p) t -> p a t", p=P)).then_inc(mem_loaded, 16)

            def split_memory():
                act.wait_ge(mem_loaded, 16)
                for k in range(0, KT, 4):
                    act.activation(mem_hi[:, k:k + 4, :], mem_raw[:, k:k + 4, :], ACT.Copy).then_inc(mem_hi_done, 4)

            statistics(n1, 0, U_MIX, False, (load_memory, split_memory))
            def mem_unit(s):
                return unit[:, s, :].rearrange("p (a t) -> p a t", a=2)[:, :, 0:MEM]

            def keys(h, k):
                act.wait_ge(unit_ready, h * XU + k)
                act.activation(mk_hi[:], mem_unit(0), ACT.Copy, scale=MEM_DIM ** -0.5).then_inc(mkq_hi, 1)

            def mem_values(h, k, s):
                act.wait_ge(unit_ready, h * XU + k)
                act.activation(mv_T[:], mem_unit(s), ACT.Copy).then_inc(unit_drained[s], 1)

            def queries_and_v(h, k):
                act.wait_ge(unit_ready, h * XU + k)
                act.activation(mq_hi[:, 0, :], unit[:, 0, :], ACT.Copy).then_inc(mkq_hi, 1)
                act.wait_ge(turn_ready, h * 3 + 4)
                act.activation(mv_hi[:], aux[:, 0:2, 0:MEM_DIM], ACT.Copy).then_inc(turn_hi, 1)
                act.wait_ge(unit_ready, h * XU + (k + 1))
                act.activation(mq_hi[:, 1, :], unit[:, 1, :], ACT.Copy).then_inc(mkq_hi, 1)

            def mem_head(h, more):
                base = U_MEM + 5

                def exponent(hf):
                    act.wait_ge(neg_ready, h * 2 + (hf + 1))
                    for tt in range(4):
                        z = aux[:, 2 * hf + tt // 2, tt % 2 * MEM:(tt % 2 + 1) * MEM]
                        x = act.activation(prob[hf][:, tt, :], z, ACT.Exp, bias=neg_max[hf][:, tt:tt + 1],
                                           accum_out=row_sum[hf][:, tt:tt + 1])
                    x.then_inc(exp_done, 1)

                def split_p(hf):
                    act.wait_ge(turn_ready, h * 3 + (hf + 2))
                    act.activation(pT_hi[hf][:], aux[:, 2 * hf:2 * hf + 2, :], ACT.Copy).then_inc(turn_hi, 1)

                def store(hf, k):
                    act.wait_ge(unit_ready, h * XU + (base + k))
                    r = acc[:, bass.ds(h * 2, 2), hf * HALF:(hf + 1) * HALF] if more else \
                        acc[:, 2 * h:2 * h + 2, hf * HALF:(hf + 1) * HALF]
                    act.activation(r, unit[:, k % 2, :].rearrange("p (a t) -> p a t", a=2), ACT.Copy
                                   ).then_inc(unit_drained[k % 2], 1)

                def early_split(ks):
                    split_a(n2, unit_drained[1], lambda k: U_MEM // 2 + 10, ks)

                exponent(0)
                exponent(1)
                if more:
                    keys(h, base)
                split_p(0)
                split_p(1)
                if not more:
                    early_split(range(3))
                store(0, 1 if more else 0)
                if not more:
                    early_split(range(3, 6))
                if more:
                    mem_values(h, base + 2, 0)
                store(1, 3 if more else 1)
                if more:
                    queries_and_v(h, base + 4)

            layer_norm(n1, 0, {4: lambda: keys(0, U_MEM + 1)})
            for k in range(2):
                act.wait_ge(unit_ready, U_MEM + k + 2)
                act.activation(mq_hi[:, k, :], unit[:, 1 - k, :], ACT.Copy).then_inc(mkq_hi, 1)
            mem_values(0, U_MEM + 4, 1)
            act.wait_ge(turn_ready, 1)
            act.activation(mv_hi[:], aux[:, 0:2, 0:MEM_DIM], ACT.Copy).then_inc(turn_hi, 1)
            with act.Fori(0, MEM_HEADS - 1) as h:
                mem_head(h, True)
            mem_head(MEM_HEADS - 1, False)

            split_a(n2, unit_drained[1], lambda k: U_MO // 2, range(6, KT))
            statistics(n2, 1, U_MO, False)
            layer_norm(n2, 1)

            first, tiles = U_FFN, 0
            for part, kts in enumerate(FFN_PARTS):
                with act.Fori(0, kts) as j:
                    act.wait_ge(unit_ready, j * 2 + (first + 1))
                    act.activation(silu_h[:], unit[:, 0, :], ACT.Silu).then_inc(unit_drained[0], 1)
                    act.wait_ge(unit_drained[1], j + (first // 2 + 1))
                    act.activation(a_hi[:, bass.ds(j, 1), :].rearrange("p a t -> p (a t)"), hidden[:], ACT.Copy
                                   ).then_inc(hid_hi, 1)
                first, tiles = first + 2 * kts + 8, tiles + kts
            statistics(n3, 2, first - 8, True)
            layer_norm(n3, 2)

        @block.vector
        def _(dve):
            dve.memset(f32(ret_ones[:]), 1.0 / RET_V).then_inc(consts_ready, 1)
            dve.memset(f32(ln_ones[:]), 1.0 / D)
            for k in range(KT):
                dve.wait_ge(x_hi_done, k + 1)
                dve.tensor_tensor(x_lo[:, k, :], acc[:, k, :], f32(x_hi[:, k, :]), ALU.subtract).then_inc(x_split, 1)
                if k == 0:
                    dve.memset(diag[:], 0.0).then_inc(consts_ready, 1)
            dve.wait_ge(consts_loaded, 48)

            with dve.Fori(0, RET_HEADS) as h:
                def ready(k):
                    dve.wait_ge(unit_ready, h * RU + (U_RET + k + 1))

                for w in range(2):
                    u = unit[:, w, :]
                    ready(w)
                    dve.wait_ge(rope_loaded, h * 32 + 16 * (w + 1))
                    if w:
                        dve.wait_ge(rot_split, h * 2 + 1)
                    dve.tensor_tensor(tmp_a[:], u, rope_sb[:, 0, :], ALU.mult).then_inc(rope_products, 1)
                    dve.tensor_tensor(tmp_b[0:64, :], u[64:128, :], rope_sb[64:128, 1, :], ALU.mult
                                      ).then_inc(rope_products, 1)
                    dve.tensor_tensor(tmp_b[64:128, :], u[0:64, :], rope_sb[0:64, 1, :], ALU.mult
                                      ).then_inc(unit_drained[w], 1)
                    dve.wait_ge(rope_products, h * 4 + 2 * (w + 1))
                    dve.wait_ge(unit_drained[w], h * 5 + 1)
                    dve.tensor_tensor(tmp_a[:], tmp_a[:], tmp_b[:], ALU.add).then_inc(rotated, 1)
                    dve.wait_ge(rot_hi, h * 2 + (w + 1))
                    dve.tensor_tensor((rq_lo, rk_lo)[w][:], tmp_a[:], f32((rq_hi, rk_hi)[w][:]), ALU.subtract
                                      ).then_inc(rot_split, 1)
                for e in range(2):
                    dve.wait_ge(rv_hi_done, h * 2 + (e + 1))
                    dve.tensor_tensor(rv_lo[:, :, e * P:(e + 1) * P], unit[:, e, :].rearrange("p (b d) -> p b d", d=P),
                                      f32(rv_hi[:, :, e * P:(e + 1) * P]), ALU.subtract).then_inc(unit_drained[e], 1)

                def add_blocks(hf):
                    dve.wait_ge(ret_copied, h * 2 + (hf + 1))
                    dve.wait_ge(rt_split, h * 2 + hf)
                    dve.tensor_tensor(rt_sum[:], ret_out[:, 0, :], ret_out[:, 1, :], ALU.add).then_inc(rt_added, 1)
                    dve.wait_ge(unit_drained[(7 + hf) % 2], h * 5 + (4 + hf))
                    dve.tensor_tensor(rt_sq[:], tmp_b[:, 0:HALF], tmp_b[:, HALF:SEQ], ALU.add).then_inc(rt_added, 1)

                def sums_hi(hf):
                    dve.wait_ge(norm_ready, h * 2 + hf)
                    for n, (hi, t) in enumerate(((rt_sum_hi, rt_sum), (rt_sq_hi, rt_sq))):
                        dve.wait_ge(rt_added, h * 4 + (2 * hf + n + 1))
                        dve.tensor_copy(hi[:], t[:]).then_inc(rt_hi, 1)

                def sums_lo(hf):
                    dve.wait_ge(rt_hi, h * 4 + (2 * hf + 1))
                    dve.tensor_tensor(rt_sum_lo[:], rt_sum[:], f32(rt_sum_hi[:]), ALU.subtract)
                    dve.wait_ge(rt_hi, h * 4 + (2 * hf + 2))
                    dve.tensor_tensor(rt_sq_lo[:], rt_sq[:], f32(rt_sq_hi[:]), ALU.subtract).then_inc(rt_split, 1)

                wide = tmp_a[:].rearrange("p (e t) -> p e t", e=2)

                def center(hf):
                    m = h * 2 + (hf + 1)
                    dve.wait_ge(ret_normed, h * 2 + hf)
                    dve.wait_ge(r_mean_sq, m)
                    dve.scalar_tensor_tensor(out=r_rstd[:], in0=aux[:, 3, :], scalar=EPS, in1=r_mean2[:],
                                             op0=ALU.add, op1=ALU.subtract).then_inc(r_var, 1)
                    dve.tensor_tensor(wide, ret_out[:], aux[:, 2:3, :].to_broadcast([P, 2, HALF]), ALU.subtract
                                      ).then_inc(ret_centered, 1)

                def scale(hf):
                    m = h * 2 + (hf + 1)
                    dve.wait_ge(r_std, m)
                    dve.reciprocal(r_rstd[:], r_mean2[:]).then_inc(r_rstd_ready, 1)
                    dve.wait_ge(r_rstd_ready, m)
                    dve.wait_ge(ret_centered, m)
                    dve.tensor_tensor(acc[:, bass.ds(h * 2, 2), hf * HALF:(hf + 1) * HALF], wide,
                                      r_rstd[:, None, :].to_broadcast([P, 2, HALF]), ALU.mult).then_inc(ret_normed, 1)

                tiles_hi = diags = 0
                for t in range(12):
                    hf, kb, q0, n = ret_tile(t)
                    a = P if q0 == kb * P else 0
                    if a:
                        dve.wait_ge(rp_split, h * 12 + t)
                        dve.wait_ge(rz_ready, h * 12 + (t + 1))
                        dve.tensor_tensor(diag[:], aux[:, t % 2, 0:P], causal[:], ALU.mult).then_inc(diag_masked, 1)
                        dve.wait_ge(diag_masked, h * 8 + (diags + 1))
                        dve.tensor_copy(rp_hi[:, t % 2, 0:P], diag[:]).then_inc(diag_hi, 1)
                        dve.wait_ge(diag_hi, h * 8 + (diags + 1))
                        dve.tensor_tensor(rp_lo[:, t % 2, 0:P], diag[:], f32(rp_hi[:, t % 2, 0:P]), ALU.subtract
                                          ).then_inc(diag_lo if n > a else rp_split, 1)
                        diags += 1
                    if n > a:
                        tiles_hi += 1
                        dve.wait_ge(rp_hi_done, h * 10 + tiles_hi)
                        dve.tensor_tensor(rp_lo[:, t % 2, a:n], aux[:, t % 2, a:n], f32(rp_hi[:, t % 2, a:n]),
                                          ALU.subtract).then_inc(rp_split, 1)
                    if t == 6:
                        add_blocks(0)
                    if t == 7:
                        sums_hi(0)
                    if t == 8:
                        sums_lo(0)
                center(0)
                add_blocks(1)
                sums_hi(1)
                sums_lo(1)
                scale(0)
                center(1)
                scale(1)
                dve.wait_ge(ret_normed, h * 2 + 2)
                dve.wait_ge(unit_drained[1], h * 5 + 5)
                for e in range(2):
                    r = acc[:, bass.ds(h * 2 + e, 1), :].rearrange("p a t -> p (a t)")
                    dve.tensor_tensor(r, r, silu_g[:, e, :], ALU.mult).then_inc(ret_gated, 1)

            for k in range(KT):
                dve.wait_ge(ret_hi_done, k + 1)
                dve.tensor_tensor(ret_lo[:, k, :], acc[:, k, :], f32(ret_hi[:, k, :]), ALU.subtract).then_inc(ret_split, 1)
            with dve.Fori(0, KT) as n:
                dve.wait_ge(unit_ready, n * 2 + (U_GRET + 2))
                dve.wait_ge(unit_drained[0], n + (U_GRET // 2 + 1))
                dve.tensor_tensor(acc[:, bass.ds(n, 1), :].rearrange("p a t -> p (a t)"), unit[:, 1, :], gate_ret[:],
                                  ALU.mult).then_inc(unit_drained[1], 1)

            dve.memset(stick[:, SEQ:SEQ + 1], 1.0).then_inc(stick_consts, 1)
            dve.tensor_copy(ident_r[:], ident[:]).then_inc(stick_consts, 1)
            dve.wait_ge(neg_loaded, 16)
            dve.tensor_copy(neg_r[:], neg[:]).then_inc(stick_consts, 2)
            with dve.Fori(0, SB_PAIRS // 2) as i:
                for pp in range(2):
                    def count(per_pair, k):
                        return i * (2 * per_pair) + (per_pair * pp + k)

                    dve.wait_ge(sqkv_hi, count(3, 1))
                    dve.scalar_tensor_tensor(out=sq_lo[:], in0=unit[:, 0, :], scalar=SB_DIM ** -0.5, in1=f32(sq_hi[:]),
                                             op0=ALU.mult, op1=ALU.subtract).then_inc(unit_drained[0], 1)
                    dve.wait_ge(sqkv_hi, count(3, 2))
                    dve.tensor_tensor(sk_lo[:], unit[:, 1, :], f32(sk_hi[:]), ALU.subtract).then_inc(unit_drained[1], 1)
                    for s in range(18):
                        if s >= 2:
                            r = s - 2
                            qt, hd, n = stick_step(r)
                            dve.wait_ge(wt_hi, count(16, r + 1))
                            dve.tensor_tensor(wT_lo[:, r % 2, 0:n], aux[:, 0:2, :].rearrange("p b t -> p (b t)")[:, 0:n],
                                              f32(wT_hi[:, r % 2, 0:n]), ALU.subtract).then_inc(wt_split, 1)
                        if s < 16:
                            qt, hd, n = stick_step(s)
                            slot = s % 2 if s else 1
                            dve.wait_ge(unit_drained[slot], i * SU + ((U_SB + SU * pp + (4 + s if s else 3)) // 2 + 1))
                            left = stick[:, SEQ - n:SEQ]
                            dve.tensor_tensor_scan(left[:, ::-1], left[:, ::-1], left[:, ::-1], 1.0,
                                                   ALU.mult, ALU.bypass).then_inc(stick_scanned, 1)
                            dve.wait_ge(stick_scanned, count(16, s + 1))
                            dve.tensor_tensor(beta[:, s % 2, 0:n], beta[:, s % 2, 0:n], stick[:, SEQ - n + 1:SEQ + 1],
                                              ALU.mult).then_inc(w_ready, 1)
                        if s == 0:
                            dve.wait_ge(sqkv_hi, count(3, 3))
                            dve.tensor_tensor(sv_lo[:].rearrange("p b d -> p (b d)"), unit[:, 0, :],
                                              f32(sv_hi[:].rearrange("p b d -> p (b d)")), ALU.subtract
                                              ).then_inc(unit_drained[0], 1)

            for k in range(4):
                dve.wait_ge(sbo_hi_done, k + 1)
                dve.tensor_tensor(sbo_lo[:, k, :], sb_out[:, k, :], f32(sbo_hi[:, k, :]), ALU.subtract
                                  ).then_inc(sbo_split, 1)
            def add_branch(i, g, j):
                k = 2 * g + j
                dve.wait_ge(unit_ready, i * GU + (U_GSB + k + 3))
                if g == 0:
                    dve.wait_ge(unit_drained[j], i * (GU // 2) + (U_GSB // 2 + 1))
                    gate = gate_sb[:, j, :]
                else:
                    gate = early_gate[:, 2 * i + j, :]
                dve.tensor_tensor(gate, gate, unit[:, j, :], ALU.mult).then_inc(unit_drained[j], 1)
                dve.wait_ge(unit_drained[j], i * (GU // 2) + (U_GSB // 2 + g + 2))
                r = acc[:, 4 * i + k, :]
                dve.tensor_tensor(r, r, gate, ALU.add).then_inc(branch_summed, 1)

            def split_a(m, ks):
                for k in ks:
                    dve.wait_ge(m.a_hi, k + 1)
                    dve.tensor_tensor(a_lo[:, k, :], acc[:, k, :], f32(a_hi[:, k, :]), ALU.subtract
                                      ).then_inc(m.a_split, 1)

            for i, g, j in ((0, 0, 0), (0, 0, 1), (0, 1, 0), (0, 1, 1), (1, 0, 0), (1, 0, 1), (1, 1, 0)):
                add_branch(i, g, j)
            dve.wait_ge(unit_ready, U_MIX)
            split_a(n1, range(4))
            add_branch(1, 1, 1)
            split_a(n1, range(4, KT))

            def residual(m, first, add_x, stats):
                def last_totals(hf):
                    dve.wait_ge(m.last_summed if add_x or not hf else unit_drained[1],
                                hf + 1 if add_x or not hf else first // 2 + 4)
                    dve.wait_ge(m.total_added, 7 + hf)
                    dve.tensor_tensor(total[:, half(hf)], total[:, half(hf)], acc[:, 7, half(hf)], ALU.add
                                      ).then_inc(m.total_ready, 1)
                    dve.wait_ge(m.square_added, 7 + hf)
                    dve.wait_ge(m.squared, 8 + hf)
                    dve.tensor_tensor(total_sq[:, half(hf)], total_sq[:, half(hf)], square[:, half(hf)], ALU.add
                                      ).then_inc(m.total_ready, 1)

                def total_lo_parts(hf):
                    dve.wait_ge(m.total_hi, 2 * hf + 1)
                    dve.tensor_tensor(total_lo[:], total[:, half(hf)], f32(total_hi[:]), ALU.subtract)
                    dve.wait_ge(m.total_hi, 2 * hf + 2)
                    dve.tensor_tensor(total_sq_lo[:], total_sq[:, half(hf)], f32(total_sq_hi[:]), ALU.subtract
                                      ).then_inc(m.total_split, 1)

                def block(i, j):
                    r, xh, xl = (t[:, bass.ds(i * 2 + j, 1), :].rearrange("p a t -> p (a t)") if not isinstance(i, int)
                                 else t[:, 2 * i + j, :] for t in (acc, x_hi, x_lo))
                    dve.wait_ge(unit_ready, i * 2 + (first + j + 1))
                    if add_x:
                        dve.scalar_tensor_tensor(out=r, in0=f32(xh), scalar=ALPHA, in1=unit[:, j, :], op0=ALU.mult,
                                                 op1=ALU.add).then_inc(unit_drained[j], 1)
                        dve.wait_ge(unit_drained[j], i + (first // 2 + 1))
                        dve.scalar_tensor_tensor(out=r, in0=f32(xl), scalar=ALPHA, in1=r, op0=ALU.mult, op1=ALU.add
                                                 ).then_inc(m.summed, 1)
                    else:
                        dve.tensor_tensor(r, r, unit[:, j, :], ALU.add).then_inc(unit_drained[j], 1)

                if not stats:
                    with dve.Fori(0, 4) as i:
                        for j in range(2):
                            block(i, j)
                    return
                with dve.Fori(0, 3) as i:
                    for j in range(2):
                        block(i, j)
                block(3, 0)
                for hf in range(2):
                    r, u = acc[:, 7, half(hf)], unit[:, 1, half(hf)]
                    if hf:
                        dve.wait_ge(unit_ready, first + KT)
                    else:
                        dve.wait_ge(m.first_half, 1)
                    if add_x:
                        x = dve.scalar_tensor_tensor(out=r, in0=f32(x_hi[:, 7, half(hf)]), scalar=ALPHA, in1=u,
                                                     op0=ALU.mult, op1=ALU.add)
                        if hf:
                            x.then_inc(unit_drained[1], 1)
                            dve.wait_ge(unit_drained[1], first // 2 + 4)
                        else:
                            x.then_inc(m.added, 1)
                            dve.wait_ge(m.added, 1)
                        dve.scalar_tensor_tensor(out=r, in0=f32(x_lo[:, 7, half(hf)]), scalar=ALPHA, in1=r,
                                                 op0=ALU.mult, op1=ALU.add).then_inc(m.last_summed, 1)
                    else:
                        dve.tensor_tensor(r, r, u, ALU.add).then_inc(unit_drained[1] if hf else m.last_summed, 1)
                    last_totals(hf)
                    if hf:
                        variance(m, 0)
                    total_lo_parts(hf)

            def variance(m, hf):
                dve.wait_ge(m.mean_sq, hf + 1)
                dve.scalar_tensor_tensor(out=ln_rstd[:, half(hf)], in0=aux[:, 2 + hf, :], scalar=EPS,
                                         in1=ln_mean2[:, half(hf)], op0=ALU.add, op1=ALU.subtract).then_inc(m.var, 1)

            def invert(m, hf):
                dve.wait_ge(m.turned, hf + 1)
                dve.reciprocal(inv_col[:, hf, :], aux[:, 2 + hf, :].rearrange("p (b t) -> p b t", t=P)[:, :, 0]
                               ).then_inc(m.inverted, 1)

            def center(m, q):
                hf, k = divmod(q, KT)
                dve.tensor_tensor(ln_t[:, q % 4, :], acc[:, k, half(hf)], aux[:, hf, :], ALU.subtract
                                  ).then_inc(m.centered, 1)

            def layer_norm(m, last, between=None, inverted_at=7):
                center(m, 0)
                center(m, 1)
                invert(m, 0)
                center(m, 2)
                center(m, 3)
                for q in range(2 * KT):
                    hf, k = divmod(q, KT)
                    if between and q in between:
                        between[q]()
                    if q == 1:
                        variance(m, 1)
                    if q >= 4:
                        dve.wait_ge(y_ready if last else m.affine, q - 3)
                        center(m, q)
                    if q == inverted_at:
                        invert(m, 1)
                    rstd = aux[:, 2 + hf, :]
                    dve.wait_ge(m.rstd, hf + 1)
                    if last:
                        rstd = ln_rstd[:, half(hf)]
                        if q % KT == 0:
                            dve.tensor_copy(rstd, aux[:, 2 + hf, :]).then_inc(m.rstd_copied, 1)
                        if q % 2:
                            continue
                        dve.wait_ge(m.rstd_copied, hf + 1)
                    dve.wait_ge(m.centered, q + 1)
                    dve.tensor_tensor(ln_t[:, q % 4, :], ln_t[:, q % 4, :], rstd, ALU.mult).then_inc(m.scaled, 1)

            residual(n1, U_MIX, True, True)
            def memory_lo():
                for k in range(0, KT, 4):
                    dve.wait_ge(mem_hi_done, k + 4)
                    dve.tensor_tensor(mem_lo[:, k:k + 4, :], mem_raw[:, k:k + 4, :], f32(mem_hi[:, k:k + 4, :]),
                                      ALU.subtract).then_inc(mem_split, 4)

            def split_chunk(c):
                s = c % 2
                dve.wait_ge(w_loaded[s], (c // 2 + 1) * 16)
                dve.wait_ge(chunk_started, c)
                dve.tensor_copy(w_hi[s][:], w_raw[:, s, :]).then_inc(w_hi_done, 1)
                dve.wait_ge(w_hi_done, c + 1)
                dve.tensor_tensor(w_lo[s][:], w_raw[:, s, :], f32(w_hi[s][:]), ALU.subtract).then_inc(w_split, 1)

            def keys(h):
                dve.wait_ge(mkq_hi, h * 3 + 1)
                dve.scalar_tensor_tensor(out=mk_lo[:], in0=unit[:, 0, :].rearrange("p (a t) -> p a t", a=2)[:, :, 0:MEM],
                                         scalar=MEM_DIM ** -0.5, in1=f32(mk_hi[:]), op0=ALU.mult, op1=ALU.subtract
                                         ).then_inc(unit_drained[0], 1)

            def queries_and_v(h):
                dve.wait_ge(mkq_hi, h * 3 + 2)
                dve.tensor_tensor(mq_lo[:, 0, :], unit[:, 0, :], f32(mq_hi[:, 0, :]), ALU.subtract
                                  ).then_inc(unit_drained[0], 1)
                dve.wait_ge(turn_hi, h * 3 + 1)
                dve.tensor_tensor(mv_lo[:], aux[:, 0:2, 0:MEM_DIM], f32(mv_hi[:]), ALU.subtract).then_inc(turn_split, 1)
                dve.wait_ge(mkq_hi, h * 3 + 3)
                dve.tensor_tensor(mq_lo[:, 1, :], unit[:, 1, :], f32(mq_hi[:, 1, :]), ALU.subtract
                                  ).then_inc(unit_drained[1], 1)

            def mem_head(h, more):
                def maxima(hf):
                    m = h * 2 + (hf + 1)
                    dve.wait_ge(s_ready, m)
                    dve.tensor_reduce(neg_max[hf][:], aux[:, 2 * hf:2 * hf + 2, :].rearrange("p b (t m) -> p (b t) m", m=MEM),
                                      AX_X, ALU.max).then_inc(max_ready, 1)
                    dve.wait_ge(max_ready, m)
                    dve.tensor_scalar(neg_max[hf][:], neg_max[hf][:], -1.0, None, ALU.mult).then_inc(neg_ready, 1)

                def probabilities(hf):
                    m = h * 2 + (hf + 1)
                    dve.wait_ge(exp_done, m)
                    dve.reciprocal(inv_sum[hf][:], row_sum[hf][:]).then_inc(inv_ready, 1)
                    dve.wait_ge(inv_ready, m)
                    for tt in range(4):
                        x = dve.tensor_scalar(prob[hf][:, tt, :], prob[hf][:, tt, :], inv_sum[hf][:, tt:tt + 1], None,
                                              ALU.mult)
                    x.then_inc(prob_ready, 1)

                def split_p(hf):
                    dve.wait_ge(turn_hi, h * 3 + (hf + 2))
                    dve.tensor_tensor(pT_lo[hf][:], aux[:, 2 * hf:2 * hf + 2, :], f32(pT_hi[hf][:]), ALU.subtract
                                      ).then_inc(turn_split, 1)

                maxima(0)
                maxima(1)
                probabilities(0)
                if more:
                    keys(h + 1)
                probabilities(1)
                split_p(0)
                split_p(1)
                if more:
                    queries_and_v(h + 1)

            layer_norm(n1, False, {0: memory_lo, 2: lambda: split_chunk(CH_MEM + 2), 5: lambda: keys(0),
                                   4: lambda: split_chunk(CH_MEM + 3)}, inverted_at=3)
            for k in range(2):
                dve.wait_ge(mkq_hi, k + 2)
                dve.tensor_tensor(mq_lo[:, k, :], unit[:, 1 - k, :], f32(mq_hi[:, k, :]), ALU.subtract
                                  ).then_inc(unit_drained[1 - k], 1)
            dve.wait_ge(turn_hi, 1)
            dve.tensor_tensor(mv_lo[:], aux[:, 0:2, 0:MEM_DIM], f32(mv_hi[:]), ALU.subtract).then_inc(turn_split, 1)
            with dve.Fori(0, MEM_HEADS - 1) as h:
                mem_head(h, True)
            mem_head(MEM_HEADS - 1, False)

            dve.wait_ge(unit_ready, U_MO)
            split_a(n2, range(KT))
            residual(n2, U_MO, True, True)
            layer_norm(n2, False, inverted_at=6)

            first, tiles = U_FFN, 0
            for part, kts in enumerate(FFN_PARTS):
                with dve.Fori(0, kts) as j:
                    dve.wait_ge(unit_ready, j * 2 + (first + 2))
                    dve.wait_ge(unit_drained[0], j + (first // 2 + 1))
                    dve.wait_ge(hid_lo, j + tiles)
                    dve.tensor_tensor(hidden[:], unit[:, 1, :], silu_h[:], ALU.mult).then_inc(unit_drained[1], 1)
                    dve.wait_ge(hid_hi, j + (tiles + 1))
                    dve.tensor_tensor(a_lo[:, bass.ds(j, 1), :].rearrange("p a t -> p (a t)"), hidden[:],
                                      f32(a_hi[:, bass.ds(j, 1), :].rearrange("p a t -> p (a t)")), ALU.subtract
                                      ).then_inc(hid_lo, 1)
                first, tiles = first + 2 * kts, tiles + kts
                residual(n3, first, part == 0, part == 2)
                first += 8
            layer_norm(n3, True)


def ret_tile(t):
    hf, kb = (0, t) if t < 4 else (1, t - 4)
    q0 = max(hf * HALF, kb * P)
    return hf, kb, q0, (hf + 1) * HALF - q0


def stick_step(s):
    return s // 2, s % 2, (s // 2 + 1) * P


def gate_pieces(s):
    if 0 <= s <= 6:
        return [(0, k) for k in ((0, 1) if s == 0 else (s + 1,))]
    return [(1, k) for k in {8: (0,), 9: (1,), 10: (2,), 11: (3,), 16: (4, 5), 17: (6, 7)}.get(s, ())]


def blocks_of(w):
    k, n = w.shape
    return np.ascontiguousarray(w.reshape(k // P, P, n // P, P).transpose(2, 1, 0, 3))


def weight_streams(w_in, w_sb_o, w_ret_o, w_mix_o, w_mem_q, w_mem_kv, w_mem_o, w_ffn_in, w_ffn_out):
    win, kv, q = blocks_of(w_in), blocks_of(w_mem_kv), blocks_of(w_mem_q)
    ret_o, sb_o, ffn_in, ffn_out = blocks_of(w_ret_o), blocks_of(w_sb_o), blocks_of(w_ffn_in), blocks_of(w_ffn_out)
    eight, seven = [], []
    for h in range(RET_HEADS):
        v, g = BLK_RET_V + 2 * h, BLK_RET_G + 2 * h
        eight += [win[BLK_RET_Q + h], win[BLK_RET_K + h], win[v], win[v + 1], win[g], win[g + 1]]
    for n in range(KT):
        eight += [win[BLK_GATE_RET + n], ret_o[n]]
    for p in range(SB_PAIRS):
        gate = BLK_GATE_SB + p // 2 * 4 + 2 + p % 2
        eight += [win[BLK_SB_Q + p], win[BLK_SB_K + p], win[BLK_SB_V + p], win[gate]]
    for n in range(0, KT, 4):
        eight += [win[BLK_GATE_SB + n], win[BLK_GATE_SB + n + 1],
                  np.concatenate([sb_o[n], sb_o[n + 1]], 1), np.concatenate([sb_o[n + 2], sb_o[n + 3]], 1)]
    eight += list(blocks_of(w_mix_o))
    for h in range(MEM_HEADS):
        k_h, v_h, q_h = kv[2 * h:2 * h + 2], kv[KT + 2 * h:KT + 2 * h + 2], q[2 * h:2 * h + 2]
        for w in (k_h, v_h, q_h) if h else (k_h, q_h, v_h):
            eight += list(w)
    eight += list(blocks_of(w_mem_o))
    j0 = 0
    for kts in FFN_PARTS:
        for j in range(j0, j0 + kts):
            eight += [ffn_in[j], ffn_in[FFN_TILES + j]]
        (eight if kts == 8 else seven).extend(ffn_out[n][:, j0:j0 + kts] for n in range(KT))
        j0 += kts
    return (np.ascontiguousarray(np.stack(eight).reshape(len(eight), P, 8 * P)),
            np.ascontiguousarray(np.stack(seven).reshape(len(seven), P, 7 * P)))


def rope_tables():
    half = RET_QK // 2
    inv = (1.0 / (np.float32(10000.0) ** (np.arange(half, dtype=np.float32) / np.float32(half)))).astype(np.float32)
    pos = np.arange(SEQ, dtype=np.float32)
    ang = (pos[None, :] * inv[:, None]).astype(np.float64)
    cos = np.concatenate([np.cos(ang), np.cos(ang)], 0)
    sin = np.concatenate([np.sin(ang), -np.sin(ang)], 0)
    out = np.empty((RET_HEADS, 2, P, 2, SEQ), np.float64)
    for h in range(RET_HEADS):
        log_gamma = float(np.float32(np.log1p(-(2.0 ** (-5.0 - h)))))
        rel = log_gamma * (np.arange(SEQ) - SEQ // 2)
        for w, f in enumerate((np.exp(rel) * RET_QK ** -0.5, np.exp(-rel))):
            out[h, w, :, 0], out[h, w, :, 1] = cos * f, sin * f
    return out.astype(np.float32).reshape(2 * RET_HEADS, P, 2 * SEQ)


def kernel(x, mem, w_in, b_gate, w_sb_o, w_ret_o, w_mix_o, ln1_g, ln1_b, w_mem_q, w_mem_kv, w_mem_o, ln2_g, ln2_b,
           w_ffn_in, w_ffn_out, ln3_g, ln3_b):
    import concourse.bacc as _bacc
    from concourse.bass_utils import run_bass_kernel_spmd as _run

    x, mem = np.asarray(x), np.asarray(mem)
    eight, seven = weight_streams(*(np.asarray(w)[0] for w in (
        w_in, w_sb_o, w_ret_o, w_mix_o, w_mem_q, w_mem_kv, w_mem_o, w_ffn_in, w_ffn_out)))
    vectors = [np.asarray(v)[0].reshape(-1, P).T for v in (ln1_g, ln1_b, ln2_g, ln2_b, ln3_g, ln3_b, b_gate)]
    row, col = np.arange(P)[:, None], np.arange(P)[None, :]
    arrays = {
        "xT": np.ascontiguousarray(x[0].T),
        "memT": np.ascontiguousarray(mem[0].T),
        "stream8": eight,
        "stream7": seven,
        "params": np.ascontiguousarray(np.concatenate(vectors, 1)),
        "rope": rope_tables(),
        "consts": np.stack([row == col, col >= row, MASKED * (col >= row)]).astype(np.float32),
    }
    nc = _bacc.Bacc("TRN2", target_bir_lowering=False, num_devices=1)
    args = [nc.dram_tensor(n, a.shape, mybir.dt.from_np(a.dtype), kind="ExternalInput").ap() for n, a in arrays.items()]
    args.append(nc.dram_tensor("outT", (D, SEQ), F32, kind="ExternalOutput").ap())
    layer_program(nc, *args)
    r = _run(nc, [arrays], core_ids=[0])
    return np.ascontiguousarray(r.results[0]["outT"].T)[None]
```
